# Optimizing a Trainium2 kernel written in Bass

```python
import math
import numpy as np
import jax
import jax.numpy as jnp
from jax import lax
import jax, jax.numpy as jnp

D_MODEL = 1024
BATCH = 1
SEQ = 256
DEPTH = 2

CTX_LEN = 256
GRID_W = 64
N_EVEN = (DEPTH + 1) // 2
N_ODD = DEPTH // 2
N_MOD = 9
D_FF = 2816
EPS = 1e-6

DA_HEADS = 4
DA_HD = 64
DA_VD = 2 * DA_HD
ML_HEADS = 4
ML_QK = 64
ML_V = 128
ML_CONV = 3
GLA_HEADS = 4
GLA_K = 128
GLA_V = 256
GLA_RANK = 16
GLA_TAU = 16.0

CHUNK = 64
Q_BLOCK = 128
ROPE_BASE = 10000.0
ROPE_AXIS = DA_HD // 2

EVEN_SPLITS = (DA_HEADS * 2 * DA_HD, DA_HEADS * 2 * DA_HD, DA_HEADS * DA_VD,
               2 * ML_HEADS * ML_QK, ML_HEADS * ML_V, ML_HEADS * ML_V, 4 * ML_HEADS)
EVEN_IN = sum(EVEN_SPLITS)
ODD_SPLITS = (GLA_HEADS * GLA_K, GLA_HEADS * GLA_K, GLA_HEADS * GLA_V, GLA_HEADS * GLA_V, 2 * GLA_RANK)
ODD_IN = sum(ODD_SPLITS)


def _split(p, sizes):
    idx = np.cumsum(sizes)[:-1].tolist()
    return jnp.split(p, idx, axis=-1)

def rms_norm(x, g):
    xf = x.astype(jnp.float32)
    y = xf * lax.rsqrt(jnp.mean(xf * xf, axis=-1, keepdims=True) + EPS)
    return y.astype(x.dtype) * g

def ada_norm(x, g, shift, scale):
    return rms_norm(x, g) * (1.0 + scale) + shift

def swiglu(h, w_in, w_out):
    a, b = jnp.split(h @ w_in, 2, axis=-1)
    return (jax.nn.silu(a) * b) @ w_out

def axial_rope_tables(rows, dtype):
    row = jnp.repeat(jnp.arange(rows), GRID_W).astype(jnp.float32)
    col = (jnp.arange(rows * GRID_W) % GRID_W).astype(jnp.float32)
    inv = ROPE_BASE ** (-jnp.arange(ROPE_AXIS // 2, dtype=jnp.float32) * 2.0 / ROPE_AXIS)
    ar = row[:, None] * inv
    ac = col[:, None] * inv
    return (jnp.cos(ar).astype(dtype), jnp.sin(ar).astype(dtype),
            jnp.cos(ac).astype(dtype), jnp.sin(ac).astype(dtype))

def _rope_1d(x, cos, sin):
    cos = cos[None, :, None, None, :]
    sin = sin[None, :, None, None, :]
    x1, x2 = jnp.split(x, 2, axis=-1)
    return jnp.concatenate([x1 * cos - x2 * sin, x2 * cos + x1 * sin], axis=-1)

def rope_2d(x, rope):
    cr, sr, cc, sc = rope
    xr, xc = jnp.split(x, 2, axis=-1)
    return jnp.concatenate([_rope_1d(xr, cr, sr), _rope_1d(xc, cc, sc)], axis=-1)

def diff_softmax_core(q, k, v, lam):
    s = jnp.einsum('bqhcd,bkhcd->bhcqk', q.astype(jnp.float32), k.astype(jnp.float32)) * (DA_HD ** -0.5)
    p = jax.nn.softmax(s, axis=-1)
    w = p[:, :, 0] - lam * p[:, :, 1]
    return jnp.einsum('bhqk,bkhe->bqhe', w, v.astype(jnp.float32))

def diff_attn_latent(q, k, v, lam):
    b, t, h, _, d = q.shape
    nb = t // Q_BLOCK
    qb = jnp.moveaxis(q.reshape(b, nb, Q_BLOCK, h, 2, d), 1, 0)
    out = lax.map(lambda qq: diff_softmax_core(qq, k, v, lam), qb)
    return jnp.moveaxis(out, 0, 1).reshape(b, t, h, -1)

def dw_conv(x, w, bias):
    ch = x.shape[-1]
    pad = ML_CONV // 2
    y = lax.conv_general_dilated(x, w[:, None, :].astype(x.dtype), window_strides=(1,),
                                 padding=((pad, pad),), dimension_numbers=('NWC', 'WIO', 'NWC'),
                                 feature_group_count=ch)
    return y + bias

def to_chunks(a):
    b, s, h = a.shape[:3]
    rest = a.shape[3:]
    a = a.reshape((b, s // CHUNK, CHUNK, h) + rest)
    return a.transpose((1, 0, 3, 2) + tuple(range(4, a.ndim)))

def from_chunks(y):
    nc, b, h, l = y.shape[:4]
    rest = y.shape[4:]
    y = y.transpose((1, 0, 3, 2) + tuple(range(4, y.ndim)))
    return y.reshape((b, nc * l, h) + rest)

def mlstm_scan(q, k, v, ig, lf, state):
    xs = tuple(to_chunks(a.astype(jnp.float32)) for a in (q, k, v, ig, lf))
    tril = jnp.tril(jnp.ones((CHUNK, CHUNK), dtype=bool))

    def step(carry, inp):
        cmat, nvec, m = carry
        qc, kc, vc, ic, fc = inp
        bcum = jnp.cumsum(fc, axis=-1)
        dmat = jnp.where(tril, bcum[..., :, None] - bcum[..., None, :] + ic[..., None, :], -jnp.inf)
        m_inter = bcum + m[..., None]
        m_t = jnp.maximum(m_inter, jnp.max(dmat, axis=-1))
        w_inter = jnp.exp(m_inter - m_t)
        s = jnp.einsum('bhtd,bhsd->bhts', qc, kc) * jnp.exp(dmat - m_t[..., None])
        num = jnp.einsum('bhts,bhse->bhte', s, vc) + w_inter[..., None] * jnp.einsum('bhtd,bhed->bhte', qc, cmat)
        den = jnp.sum(s, axis=-1) + w_inter * jnp.einsum('bhtd,bhd->bht', qc, nvec)
        h = num / jnp.maximum(jnp.abs(den), jnp.exp(-m_t))[..., None]
        bl = bcum[..., -1]
        g = bl[..., None] - bcum + ic
        m_new = jnp.maximum(bl + m, jnp.max(g, axis=-1))
        decay = jnp.exp(bl + m - m_new)
        wk = jnp.exp(g - m_new[..., None])
        cmat = decay[..., None, None] * cmat + jnp.einsum('bhs,bhse,bhsd->bhed', wk, vc, kc)
        nvec = decay[..., None] * nvec + jnp.einsum('bhs,bhsd->bhd', wk, kc)
        return (cmat, nvec, m_new), h

    state, hs = lax.scan(step, state, xs)
    return from_chunks(hs), state

def gla_scan(q, k, v, la, state):
    xs = tuple(to_chunks(a.astype(jnp.float32)) for a in (q, k, v, la))
    tril = jnp.tril(jnp.ones((CHUNK, CHUNK), dtype=bool))

    def step(smat, inp):
        qc, kc, vc, ac = inp
        bcum = jnp.cumsum(ac, axis=2)
        qe = qc * jnp.exp(bcum)
        ke = kc * jnp.exp(-bcum)
        a = jnp.where(tril, jnp.einsum('bhtd,bhsd->bhts', qe, ke), 0.0)
        o = jnp.einsum('bhts,bhse->bhte', a, vc) + jnp.einsum('bhtd,bhde->bhte', qe, smat)
        bl = bcum[:, :, -1]
        kd = kc * jnp.exp(bl[:, :, None] - bcum)
        smat = jnp.exp(bl)[..., None] * smat + jnp.einsum('bhsd,bhse->bhde', kd, vc)
        return smat, o

    state, os_ = lax.scan(step, state, xs)
    return from_chunks(os_), state

def bidir_scan(scan, qkv_c, qkv_x, gc_f, gc_b, gx_f, gx_b, st0, need_ctx):
    def rev(arrs):
        return tuple(jnp.flip(a, axis=1) for a in arrs)
    yc_f, s_f = scan(*qkv_c, *gc_f, st0)
    yc_b, s_b = scan(*rev(qkv_c), *rev(gc_b), st0)
    yx_f, _ = scan(*qkv_x, *gx_f, s_f)
    yx_b, _ = scan(*rev(qkv_x), *rev(gx_b), s_b)
    yx = yx_f + jnp.flip(yx_b, axis=1)
    yc = yc_f + jnp.flip(yc_b, axis=1) if need_ctx else None
    return yx, yc

def even_mixer(hx, hc, w_in, w_out, diff_lambda, diff_norm_g, conv_w, conv_b, gate_b, ml_norm_g,
               lam_init, rope, need_ctx):
    dt = hx.dtype
    px = _split(hx @ w_in, EVEN_SPLITS)
    pc = _split(hc @ w_in, EVEN_SPLITS)
    lp = diff_lambda.astype(jnp.float32)
    lam = jnp.exp(jnp.sum(lp[0] * lp[1])) - jnp.exp(jnp.sum(lp[2] * lp[3])) + lam_init

    def da_heads(p):
        b, t = p[0].shape[:2]
        return (p[0].reshape(b, t, DA_HEADS, 2, DA_HD), p[1].reshape(b, t, DA_HEADS, 2, DA_HD),
                p[2].reshape(b, t, DA_HEADS, DA_VD))

    def ml_heads(p):
        b, t = p[0].shape[:2]
        qk = jax.nn.silu(dw_conv(p[3], conv_w, conv_b))
        q, k = jnp.split(qk, 2, axis=-1)
        q = q.reshape(b, t, ML_HEADS, ML_QK) * (ML_QK ** -0.5)
        k = k.reshape(b, t, ML_HEADS, ML_QK)
        v = p[4].reshape(b, t, ML_HEADS, ML_V)
        g = (p[6] + gate_b.reshape(-1)).astype(jnp.float32).reshape(b, t, 4, ML_HEADS)
        fwd = (g[:, :, 0], jax.nn.log_sigmoid(g[:, :, 2]))
        bwd = (g[:, :, 1], jax.nn.log_sigmoid(g[:, :, 3]))
        return (q, k, v), fwd, bwd

    def merge(attn, mem, o_pre):
        b, t = attn.shape[:2]
        a = (rms_norm(attn, diff_norm_g) * (1.0 - lam_init)).reshape(b, t, -1)
        m = rms_norm(mem, ml_norm_g).reshape(b, t, -1) * jax.nn.sigmoid(o_pre)
        return jnp.concatenate([a, m], axis=-1).astype(dt) @ w_out

    qx, kx, vx = da_heads(px)
    qc, kc, vc = da_heads(pc)
    qx = rope_2d(qx, rope)
    kx = rope_2d(kx, rope)
    ax = diff_attn_latent(qx, jnp.concatenate([kc, kx], axis=1), jnp.concatenate([vc, vx], axis=1), lam)

    qkv_x, gx_f, gx_b = ml_heads(px)
    qkv_c, gc_f, gc_b = ml_heads(pc)
    bsz = hx.shape[0]
    st0 = (jnp.zeros((bsz, ML_HEADS, ML_V, ML_QK), jnp.float32),
           jnp.zeros((bsz, ML_HEADS, ML_QK), jnp.float32),
           jnp.zeros((bsz, ML_HEADS), jnp.float32))
    mx, mc = bidir_scan(mlstm_scan, qkv_c, qkv_x, gc_f, gc_b, gx_f, gx_b, st0, need_ctx)

    out_x = merge(ax, mx, px[5])
    out_c = merge(diff_softmax_core(qc, kc, vc, lam), mc, pc[5]) if need_ctx else None
    return out_x, out_c

def odd_mixer(hx, hc, w_in, w_out, w_gate, b_gate, norm_g, need_ctx):
    dt = hx.dtype
    px = _split(hx @ w_in, ODD_SPLITS)
    pc = _split(hc @ w_in, ODD_SPLITS)

    def heads(p):
        b, t = p[0].shape[:2]
        q = p[0].reshape(b, t, GLA_HEADS, GLA_K) * (GLA_K ** -0.5)
        k = p[1].reshape(b, t, GLA_HEADS, GLA_K)
        v = p[2].reshape(b, t, GLA_HEADS, GLA_V)
        lr_f, lr_b = jnp.split(p[4], 2, axis=-1)

        def decay(lr, d):
            z = (lr @ w_gate[d] + b_gate[d]).astype(jnp.float32)
            return (jax.nn.log_sigmoid(z) / GLA_TAU).reshape(b, t, GLA_HEADS, GLA_K)
        return (q, k, v), (decay(lr_f, 0),), (decay(lr_b, 1),)

    def merge(o, r):
        b, t = o.shape[:2]
        y = rms_norm(o, norm_g).reshape(b, t, -1) * jax.nn.silu(r)
        return y.astype(dt) @ w_out

    qkv_x, gx_f, gx_b = heads(px)
    qkv_c, gc_f, gc_b = heads(pc)
    st0 = jnp.zeros((hx.shape[0], GLA_HEADS, GLA_K, GLA_V), jnp.float32)
    ox, oc = bidir_scan(gla_scan, qkv_c, qkv_x, gc_f, gc_b, gx_f, gx_b, st0, need_ctx)
    out_x = merge(ox, px[3])
    out_c = merge(oc, pc[3]) if need_ctx else None
    return out_x, out_c

def first_inputs(seed: int = 0) -> dict:
    key = jax.random.key(seed)
    ks = iter(jax.random.split(key, 32))

    def nrm(shape, scale):
        return jax.random.normal(next(ks), shape, jnp.float32) * scale

    d = D_MODEL
    inv = d ** -0.5
    x = nrm((BATCH, SEQ, d), 1.0)
    c = nrm((BATCH, d), 1.0)
    ctx = nrm((BATCH, CTX_LEN, d), 1.0)
    c_ctx = nrm((d,), 1.0)
    ada_w = nrm((DEPTH, d, N_MOD * d), 0.3 * inv)
    ada_b = nrm((DEPTH, N_MOD * d), 0.02)
    norm_g = 1.0 + nrm((DEPTH, 3, d), 0.02)
    ffn_w_in = nrm((DEPTH, 2, d, 2 * D_FF), inv)
    ffn_w_out = nrm((DEPTH, 2, D_FF, d), D_FF ** -0.5)
    even_w_in = nrm((N_EVEN, d, EVEN_IN), inv)
    even_w_out = nrm((N_EVEN, d, d), inv)
    diff_lambda = nrm((N_EVEN, 4, DA_HD), 0.1)
    diff_norm_g = 1.0 + nrm((N_EVEN, DA_VD), 0.02)
    mlstm_conv_w = nrm((N_EVEN, ML_CONV, 2 * ML_HEADS * ML_QK), ML_CONV ** -0.5)
    mlstm_conv_b = nrm((N_EVEN, 2 * ML_HEADS * ML_QK), 0.02)
    fbias = jnp.concatenate([jnp.zeros((2, ML_HEADS), jnp.float32),
                             jnp.tile(jnp.linspace(3.0, 6.0, ML_HEADS, dtype=jnp.float32)[None], (2, 1))], axis=0)
    mlstm_gate_b = fbias[None] + nrm((N_EVEN, 4, ML_HEADS), 0.1)
    mlstm_norm_g = 1.0 + nrm((N_EVEN, ML_HEADS, ML_V), 0.02)
    odd_w_in = nrm((N_ODD, d, ODD_IN), inv)
    odd_w_out = nrm((N_ODD, d, d), inv)
    gla_w_gate = nrm((N_ODD, 2, GLA_RANK, GLA_HEADS * GLA_K), GLA_RANK ** -0.5)
    gla_b_gate = nrm((N_ODD, 2, GLA_HEADS * GLA_K), 0.1)
    gla_norm_g = 1.0 + nrm((N_ODD, GLA_V), 0.02)
    final_g = 1.0 + nrm((d,), 0.02)
    return {"x": x, "c": c, "ctx": ctx, "c_ctx": c_ctx, "ada_w": ada_w, "ada_b": ada_b,
            "norm_g": norm_g, "ffn_w_in": ffn_w_in, "ffn_w_out": ffn_w_out,
            "even_w_in": even_w_in, "even_w_out": even_w_out, "diff_lambda": diff_lambda,
            "diff_norm_g": diff_norm_g, "mlstm_conv_w": mlstm_conv_w, "mlstm_conv_b": mlstm_conv_b,
            "mlstm_gate_b": mlstm_gate_b, "mlstm_norm_g": mlstm_norm_g, "odd_w_in": odd_w_in,
            "odd_w_out": odd_w_out, "gla_w_gate": gla_w_gate, "gla_b_gate": gla_b_gate,
            "gla_norm_g": gla_norm_g, "final_g": final_g}

def first_block(x, c, ctx, c_ctx, ada_w, ada_b, norm_g, ffn_w_in, ffn_w_out, even_w_in, even_w_out,
              diff_lambda, diff_norm_g, mlstm_conv_w, mlstm_conv_b, mlstm_gate_b, mlstm_norm_g,
              odd_w_in, odd_w_out, gla_w_gate, gla_b_gate, gla_norm_g, final_g):
    bsz, n_tok, d = x.shape
    rows = n_tok // GRID_W
    rope = axial_rope_tables(rows, x.dtype)
    s_lat = jax.nn.silu(c)
    s_ctx = jax.nn.silu(c_ctx)
    hctx = ctx
    for l in range(DEPTH):
        last = l == DEPTH - 1
        mx = (s_lat @ ada_w[l] + ada_b[l]).reshape(bsz, N_MOD, 1, d)
        mc = (s_ctx @ ada_w[l] + ada_b[l]).reshape(N_MOD, d)
        x = x + 0.5 * mx[:, 2] * swiglu(ada_norm(x, norm_g[l, 0], mx[:, 0], mx[:, 1]), ffn_w_in[l, 0], ffn_w_out[l, 0])
        hctx = hctx + 0.5 * mc[2] * swiglu(ada_norm(hctx, norm_g[l, 0], mc[0], mc[1]), ffn_w_in[l, 0], ffn_w_out[l, 0])
        hx = ada_norm(x, norm_g[l, 1], mx[:, 3], mx[:, 4])
        hc = ada_norm(hctx, norm_g[l, 1], mc[3], mc[4])
        if l % 2 == 0:
            e = l // 2
            lam_init = 0.8 - 0.6 * math.exp(-0.3 * l)
            yx, yc = even_mixer(hx, hc, even_w_in[e], even_w_out[e], diff_lambda[e], diff_norm_g[e],
                                mlstm_conv_w[e], mlstm_conv_b[e], mlstm_gate_b[e], mlstm_norm_g[e],
                                lam_init, rope, not last)
        else:
            o = l // 2
            yx, yc = odd_mixer(hx, hc, odd_w_in[o], odd_w_out[o], gla_w_gate[o], gla_b_gate[o],
                               gla_norm_g[o], not last)
        x = x + mx[:, 5] * yx
        x = x + 0.5 * mx[:, 8] * swiglu(ada_norm(x, norm_g[l, 2], mx[:, 6], mx[:, 7]), ffn_w_in[l, 1], ffn_w_out[l, 1])
        if not last:
            hctx = hctx + mc[5] * yc
            hctx = hctx + 0.5 * mc[8] * swiglu(ada_norm(hctx, norm_g[l, 2], mc[6], mc[7]), ffn_w_in[l, 1], ffn_w_out[l, 1])
    return rms_norm(x, final_g)


_first_inputs = first_inputs


def first_inputs(seed=0):
    import zlib

    import numpy as np

    out = dict(_first_inputs(seed))
    spreads = {}
    factors = {}
    for name, (base, spread) in spreads.items():
        noise = np.random.default_rng([zlib.crc32(name.encode()), seed]).standard_normal(out[name].shape)
        drawn = base * np.exp(spread * noise) if base else spread * noise
        out[name] = jnp.asarray(drawn.astype(out[name].dtype))
    for name, factor in factors.items():
        out[name] = (out[name] * factor).astype(out[name].dtype)
    return out


_narrow_inputs = first_inputs


def first_inputs(seed=0):
    out = dict(_narrow_inputs(seed))
    wider = {'norm_g': 9.14,
     'diff_lambda': 6.13,
     'diff_norm_g': 12.0,
     'mlstm_conv_b': 12.0,
     'mlstm_norm_g': 12.0,
     'gla_w_gate': 4.28,
     'gla_b_gate': 12.0,
     'gla_norm_g': 12.0,
     'final_g': 3.18}
    for name, times in wider.items():
        mean = out[name].mean()
        out[name] = (mean + times * (out[name] - mean)).astype(out[name].dtype)
    return out


N_MIXERS = 3
ROPE_THETA = 10000.0
LN_EPS = 1e-5
RMS_EPS = 1e-6
D_FF_2 = 4 * D_MODEL

MLA_HEADS = 8
MLA_Q_RANK = 512
MLA_KV_RANK = 256
MLA_NOPE = 128
MLA_ROPE = 64
MLA_V = 128

NA_HEADS = 16
NA_HEAD_DIM = D_MODEL // NA_HEADS
NA_WIN_ROWS = 8
NA_WIN_COLS = 16

GQA_HEAD_DIM = 128
GQA_Q_HEADS = D_MODEL // GQA_HEAD_DIM
GQA_KV_HEADS = GQA_Q_HEADS // 4
GQA_GROUP = GQA_Q_HEADS // GQA_KV_HEADS


def _layer_norm(x, g, b):
    xf = x.astype(jnp.float32)
    mu = jnp.mean(xf, -1, keepdims=True)
    var = jnp.mean(jnp.square(xf - mu), -1, keepdims=True)
    return ((xf - mu) * lax.rsqrt(var + LN_EPS) * g + b).astype(x.dtype)

def _rms_norm(x, g):
    xf = x.astype(jnp.float32)
    return (xf * lax.rsqrt(jnp.mean(xf * xf, -1, keepdims=True) + RMS_EPS) * g).astype(x.dtype)

def _rope_1d_2(x, pos):
    half = x.shape[-1] // 2
    freqs = ROPE_THETA ** (-jnp.arange(half, dtype=jnp.float32) / half)
    ang = pos.astype(jnp.float32)[:, None, None] * freqs
    cos, sin = jnp.cos(ang), jnp.sin(ang)
    xf = x.astype(jnp.float32)
    x1, x2 = xf[..., :half], xf[..., half:]
    return jnp.concatenate([x1 * cos - x2 * sin, x1 * sin + x2 * cos], -1).astype(x.dtype)

def _rope_2d(x, rows, cols):
    h = x.shape[-1] // 2
    return jnp.concatenate([_rope_1d_2(x[..., :h], rows), _rope_1d_2(x[..., h:], cols)], -1)

def _grid_positions(s):
    t = jnp.arange(s, dtype=jnp.int32)
    return t // GRID_W, t % GRID_W

def _block_attention(q, k, v, scale):
    b, sq, hk, g, dk = q.shape
    nb = sq // Q_BLOCK
    qb = q.reshape(b, nb, Q_BLOCK, hk, g, dk).transpose(1, 0, 2, 3, 4, 5)

    def step(qi):
        s = jnp.einsum('bqhgd,bkhd->bhgqk', qi, k).astype(jnp.float32) * scale
        p = jax.nn.softmax(s, axis=-1).astype(v.dtype)
        return jnp.einsum('bhgqk,bkhd->bqhgd', p, v)

    o = lax.map(step, qb)
    return o.transpose(1, 0, 2, 3, 4, 5).reshape(b, sq, hk * g * v.shape[-1])

def _mla_q(h, w_dq, q_norm, w_uq, rows, cols):
    b, s, _ = h.shape
    q = (_rms_norm(h @ w_dq, q_norm) @ w_uq).reshape(b, s, MLA_HEADS, MLA_NOPE + MLA_ROPE)
    q_nope, q_pe = q[..., :MLA_NOPE], q[..., MLA_NOPE:]
    if rows is not None:
        q_pe = _rope_2d(q_pe, rows, cols)
    return jnp.concatenate([q_nope, q_pe], -1)

def _mla_kv(h, w_dkv, kv_norm, w_ukv, rows, cols):
    b, s, _ = h.shape
    ckv = h @ w_dkv
    c_kv, k_pe = ckv[..., :MLA_KV_RANK], ckv[..., MLA_KV_RANK:]
    kv = (_rms_norm(c_kv, kv_norm) @ w_ukv).reshape(b, s, MLA_HEADS, MLA_NOPE + MLA_V)
    k_nope, v = kv[..., :MLA_NOPE], kv[..., MLA_NOPE:]
    k_pe = k_pe[:, :, None, :]
    if rows is not None:
        k_pe = _rope_2d(k_pe, rows, cols)
    k = jnp.concatenate([k_nope, jnp.broadcast_to(k_pe, (b, s, MLA_HEADS, MLA_ROPE))], -1)
    return k, v

def _mla_mixer(h, hc, w_dq, q_norm, w_uq, w_dkv, kv_norm, w_ukv, w_o, need_ctx):
    rows, cols = _grid_positions(h.shape[1])
    scale = (MLA_NOPE + MLA_ROPE) ** -0.5
    q = _mla_q(h, w_dq, q_norm, w_uq, rows, cols)
    k, v = _mla_kv(h, w_dkv, kv_norm, w_ukv, rows, cols)
    kc, vc = _mla_kv(hc, w_dkv, kv_norm, w_ukv, None, None)
    k_all = jnp.concatenate([kc, k], 1)
    v_all = jnp.concatenate([vc, v], 1)
    out = _block_attention(q[:, :, :, None], k_all, v_all, scale) @ w_o
    out_c = None
    if need_ctx:
        qc = _mla_q(hc, w_dq, q_norm, w_uq, None, None)
        out_c = _block_attention(qc[:, :, :, None], kc, vc, scale) @ w_o
    return out, out_c

def _na_mixer(h, hc, w_qkv, b_qkv, rpb, w_o, need_ctx):
    b, s, _ = h.shape
    n_rows = s // GRID_W
    kr = min(NA_WIN_ROWS, n_rows)
    scale = NA_HEAD_DIM ** -0.5

    def proj(t):
        qkv = (t @ w_qkv + b_qkv).reshape(t.shape[0], t.shape[1], 3, NA_HEADS, NA_HEAD_DIM)
        return qkv[:, :, 0], qkv[:, :, 1], qkv[:, :, 2]

    q, k, v = proj(h)
    qc, kc, vc = proj(hc)
    grid = (b, n_rows, GRID_W, NA_HEADS, NA_HEAD_DIM)
    q_grid, k_grid, v_grid = q.reshape(grid), k.reshape(grid), v.reshape(grid)

    r_idx = jnp.arange(n_rows, dtype=jnp.int32)
    row_start = jnp.clip(r_idx - kr // 2, 0, n_rows - kr)
    c_idx = jnp.arange(GRID_W, dtype=jnp.int32)
    col_start = jnp.clip(c_idx - NA_WIN_COLS // 2, 0, GRID_W - NA_WIN_COLS)
    col_valid = (c_idx[None, :] >= col_start[:, None]) & (c_idx[None, :] < col_start[:, None] + NA_WIN_COLS)
    mask = jnp.tile(col_valid, (1, kr))
    dc = jnp.clip(c_idx[None, :] - c_idx[:, None] + NA_WIN_COLS - 1, 0, 2 * NA_WIN_COLS - 2)
    rpb_cols = rpb[:, :, dc]

    def row_step(args):
        r, rs = args
        q_row = lax.dynamic_index_in_dim(q_grid, r, axis=1, keepdims=False)
        k_strip = lax.dynamic_slice_in_dim(k_grid, rs, kr, axis=1).reshape(b, kr * GRID_W, NA_HEADS, NA_HEAD_DIM)
        v_strip = lax.dynamic_slice_in_dim(v_grid, rs, kr, axis=1).reshape(b, kr * GRID_W, NA_HEADS, NA_HEAD_DIM)
        dr = rs + jnp.arange(kr, dtype=jnp.int32) - r + NA_WIN_ROWS - 1
        bias = jnp.take(rpb_cols, dr, axis=1).transpose(0, 2, 1, 3).reshape(NA_HEADS, GRID_W, kr * GRID_W)
        s_lat = jnp.einsum('bqhd,bkhd->bhqk', q_row, k_strip).astype(jnp.float32) * scale + bias
        s_lat = jnp.where(mask, s_lat, -jnp.inf)
        s_ctx = jnp.einsum('bqhd,bkhd->bhqk', q_row, kc).astype(jnp.float32) * scale
        p = jax.nn.softmax(jnp.concatenate([s_ctx, s_lat], -1), axis=-1).astype(v.dtype)
        return jnp.einsum('bhqk,bkhd->bqhd', p, jnp.concatenate([vc, v_strip], 1))

    o = lax.map(row_step, (r_idx, row_start))
    out = o.transpose(1, 0, 2, 3, 4).reshape(b, s, NA_HEADS * NA_HEAD_DIM) @ w_o
    out_c = None
    if need_ctx:
        out_c = _block_attention(qc[:, :, :, None], kc, vc, scale) @ w_o
    return out, out_c

def _gqa_proj(t, w_qkv, q_norm, k_norm, rows, cols):
    bb, ss, _ = t.shape
    nq = GQA_Q_HEADS * GQA_HEAD_DIM
    nk = GQA_KV_HEADS * GQA_HEAD_DIM
    qkv = t @ w_qkv
    q = _rms_norm(qkv[..., :nq].reshape(bb, ss, GQA_Q_HEADS, GQA_HEAD_DIM), q_norm)
    k = _rms_norm(qkv[..., nq:nq + nk].reshape(bb, ss, GQA_KV_HEADS, GQA_HEAD_DIM), k_norm)
    v = qkv[..., nq + nk:].reshape(bb, ss, GQA_KV_HEADS, GQA_HEAD_DIM)
    if rows is not None:
        q = _rope_2d(q, rows, cols)
        k = _rope_2d(k, rows, cols)
    return q.reshape(bb, ss, GQA_KV_HEADS, GQA_GROUP, GQA_HEAD_DIM), k, v

def _gqa_mixer(h, hc, w_qkv, q_norm, k_norm, w_o, need_ctx):
    rows, cols = _grid_positions(h.shape[1])
    scale = GQA_HEAD_DIM ** -0.5
    q, k, v = _gqa_proj(h, w_qkv, q_norm, k_norm, rows, cols)
    qc, kc, vc = _gqa_proj(hc, w_qkv, q_norm, k_norm, None, None)
    out = _block_attention(q, jnp.concatenate([kc, k], 1), jnp.concatenate([vc, v], 1), scale) @ w_o
    out_c = None
    if need_ctx:
        out_c = _block_attention(qc, kc, vc, scale) @ w_o
    return out, out_c

def _mlp(h, w1, w2):
    return jnp.square(jax.nn.relu(h @ w1)) @ w2

def second_inputs(seed: int = 0) -> dict:
    key = jax.random.key(seed)
    ks = iter(jax.random.split(key, 32))
    beta = (8.0 * DEPTH) ** -0.25
    n_a = len(range(0, DEPTH, N_MIXERS))
    n_b = len(range(1, DEPTH, N_MIXERS))
    n_c = len(range(2, DEPTH, N_MIXERS))
    D = D_MODEL

    def nrm(shape, s=1.0):
        return jax.random.normal(next(ks), shape, jnp.float32) * s

    def w(shape, fan_in, g=1.0):
        return nrm(shape, g * fan_in ** -0.5)

    def gain(shape):
        return 1.0 + nrm(shape, 0.05)

    return {
        "x": nrm((BATCH, SEQ, D)),
        "c": nrm((BATCH, D)),
        "ctx": nrm((BATCH, CTX_LEN, D)),
        "c_ctx": nrm((D,)),
        "ada_w": w((DEPTH, D, 6 * D), D),
        "ada_b": nrm((DEPTH, 6 * D), 0.02),
        "ln1_g": gain((DEPTH, D)),
        "ln1_b": nrm((DEPTH, D), 0.02),
        "ln2_g": gain((DEPTH, D)),
        "ln2_b": nrm((DEPTH, D), 0.02),
        "mlp_w1": w((DEPTH, D, D_FF_2), D),
        "mlp_w2": w((DEPTH, D_FF_2, D), D_FF_2, beta),
        "mla_w_dq": w((n_a, D, MLA_Q_RANK), D),
        "mla_q_norm": gain((n_a, MLA_Q_RANK)),
        "mla_w_uq": w((n_a, MLA_Q_RANK, MLA_HEADS * (MLA_NOPE + MLA_ROPE)), MLA_Q_RANK),
        "mla_w_dkv": w((n_a, D, MLA_KV_RANK + MLA_ROPE), D),
        "mla_kv_norm": gain((n_a, MLA_KV_RANK)),
        "mla_w_ukv": w((n_a, MLA_KV_RANK, MLA_HEADS * (MLA_NOPE + MLA_V)), MLA_KV_RANK),
        "mla_w_o": w((n_a, MLA_HEADS * MLA_V, D), MLA_HEADS * MLA_V, beta),
        "na_w_qkv": w((n_b, D, 3 * NA_HEADS * NA_HEAD_DIM), D),
        "na_b_qkv": nrm((n_b, 3 * NA_HEADS * NA_HEAD_DIM), 0.02),
        "na_rpb": nrm((n_b, NA_HEADS, 2 * NA_WIN_ROWS - 1, 2 * NA_WIN_COLS - 1), 0.1),
        "na_w_o": w((n_b, NA_HEADS * NA_HEAD_DIM, D), NA_HEADS * NA_HEAD_DIM, beta),
        "gqa_w_qkv": w((n_c, D, (GQA_Q_HEADS + 2 * GQA_KV_HEADS) * GQA_HEAD_DIM), D),
        "gqa_q_norm": gain((n_c, GQA_HEAD_DIM)),
        "gqa_k_norm": gain((n_c, GQA_HEAD_DIM)),
        "gqa_w_o": w((n_c, GQA_Q_HEADS * GQA_HEAD_DIM, D), GQA_Q_HEADS * GQA_HEAD_DIM, beta),
    }

def second_block(x, c, ctx, c_ctx, ada_w, ada_b, ln1_g, ln1_b, ln2_g, ln2_b, mlp_w1, mlp_w2,
              mla_w_dq, mla_q_norm, mla_w_uq, mla_w_dkv, mla_kv_norm, mla_w_ukv, mla_w_o,
              na_w_qkv, na_b_qkv, na_rpb, na_w_o,
              gqa_w_qkv, gqa_q_norm, gqa_k_norm, gqa_w_o):
    alpha = (2.0 * DEPTH) ** 0.25
    for i in range(DEPTH):
        kind, j = i % N_MIXERS, i // N_MIXERS
        need_ctx = i < DEPTH - 1
        mod = (jax.nn.silu(c) @ ada_w[i] + ada_b[i])[:, None, :]
        mod_c = jax.nn.silu(c_ctx) @ ada_w[i] + ada_b[i]
        sh1, sc1, g1, sh2, sc2, g2 = jnp.split(mod, 6, axis=-1)
        csh1, csc1, cg1, csh2, csc2, cg2 = jnp.split(mod_c, 6, axis=-1)

        h = x * (1 + sc1) + sh1
        hc = ctx * (1 + csc1) + csh1
        if kind == 0:
            y, yc = _mla_mixer(h, hc, mla_w_dq[j], mla_q_norm[j], mla_w_uq[j], mla_w_dkv[j],
                               mla_kv_norm[j], mla_w_ukv[j], mla_w_o[j], need_ctx)
        elif kind == 1:
            y, yc = _na_mixer(h, hc, na_w_qkv[j], na_b_qkv[j], na_rpb[j], na_w_o[j], need_ctx)
        else:
            y, yc = _gqa_mixer(h, hc, gqa_w_qkv[j], gqa_q_norm[j], gqa_k_norm[j], gqa_w_o[j], need_ctx)
        x = _layer_norm(alpha * x + g1 * y, ln1_g[i], ln1_b[i])
        if need_ctx:
            ctx = _layer_norm(alpha * ctx + cg1 * yc, ln1_g[i], ln1_b[i])

        x = _layer_norm(alpha * x + g2 * _mlp(x * (1 + sc2) + sh2, mlp_w1[i], mlp_w2[i]), ln2_g[i], ln2_b[i])
        if need_ctx:
            ctx = _layer_norm(alpha * ctx + cg2 * _mlp(ctx * (1 + csc2) + csh2, mlp_w1[i], mlp_w2[i]),
                              ln2_g[i], ln2_b[i])
    return x


def setup_inputs(seed=0):
    out = dict(first_inputs(seed))
    for name, value in second_inputs(seed + 1).items():
        if name != "x":
            out[name + "_2"] = value
    return out


def reference(
    x, c, ctx, c_ctx, ada_w, ada_b, norm_g, ffn_w_in, ffn_w_out, even_w_in, even_w_out,
    diff_lambda, diff_norm_g, mlstm_conv_w, mlstm_conv_b, mlstm_gate_b, mlstm_norm_g, odd_w_in,
    odd_w_out, gla_w_gate, gla_b_gate, gla_norm_g, final_g, c_2, ctx_2, c_ctx_2, ada_w_2,
    ada_b_2, ln1_g_2, ln1_b_2, ln2_g_2, ln2_b_2, mlp_w1_2, mlp_w2_2, mla_w_dq_2, mla_q_norm_2,
    mla_w_uq_2, mla_w_dkv_2, mla_kv_norm_2, mla_w_ukv_2, mla_w_o_2, na_w_qkv_2, na_b_qkv_2,
    na_rpb_2, na_w_o_2, gqa_w_qkv_2, gqa_q_norm_2, gqa_k_norm_2, gqa_w_o_2,
):
    x = first_block(
        x, c, ctx, c_ctx, ada_w, ada_b, norm_g, ffn_w_in, ffn_w_out, even_w_in, even_w_out,
        diff_lambda, diff_norm_g, mlstm_conv_w, mlstm_conv_b, mlstm_gate_b, mlstm_norm_g,
        odd_w_in, odd_w_out, gla_w_gate, gla_b_gate, gla_norm_g, final_g,
    )
    return second_block(
        x, c_2, ctx_2, c_ctx_2, ada_w_2, ada_b_2, ln1_g_2, ln1_b_2, ln2_g_2, ln2_b_2, mlp_w1_2,
        mlp_w2_2, mla_w_dq_2, mla_q_norm_2, mla_w_uq_2, mla_w_dkv_2, mla_kv_norm_2, mla_w_ukv_2,
        mla_w_o_2, na_w_qkv_2, na_b_qkv_2, na_rpb_2, na_w_o_2, gqa_w_qkv_2, gqa_q_norm_2,
        gqa_k_norm_2, gqa_w_o_2,
    )


_drawn_inputs = setup_inputs


def setup_inputs(seed=0):
    import zlib

    import numpy as np

    out = dict(_drawn_inputs(seed))
    spreads = {}
    factors = {'mlstm_conv_b': 3.464,
     'mlstm_norm_g': 3.177,
     'mla_q_norm_2': 8.0,
     'mla_kv_norm_2': 8.0,
     'na_b_qkv_2': 8.0,
     'na_rpb_2': 8.0}
    for name, (base, spread) in spreads.items():
        noise = np.random.default_rng([zlib.crc32(name.encode()), seed]).standard_normal(out[name].shape)
        drawn = base * np.exp(spread * noise) if base else spread * noise
        out[name] = jnp.asarray(drawn.astype(out[name].dtype))
    for name, factor in factors.items():
        out[name] = (out[name] * factor).astype(out[name].dtype)
    return out
```

```python
import math
from contextlib import ExitStack, contextmanager

import numpy as np
import concourse.bass as bass
from concourse import mybir
from concourse.alu_op_type import AluOpType as ALU

F32 = mybir.dt.float32
ACT = mybir.ActivationFunctionType
AX = mybir.AxisListType

P = 128
D = 1024
DT = D // P
NC_TOK = 256
NX_TOK = 256
T = NC_TOK + NX_TOK
TT = T // P
GRID_W = 64
FF = 2816
FT = FF // P
FF2 = 4096
FT2 = FF2 // P
N_MOD1, N_MOD2 = 9, 6
SLAB = 2048
W_SLOTS = 4
HD = 64
RMS_EPS, LN_EPS = 1e-6, 1e-5
LAM_INIT = 0.8 - 0.6 * math.exp(0.0)
ALPHA = (2.0 * 2) ** 0.25
NEG = -1.0e30
CTX, LAT = slice(0, NC_TOK), slice(NC_TOK, T)
STREAMS = ((0, CTX), (1, LAT))
GLA_CHUNK = 64


class Loop:

    def __init__(self, n, at):
        self.n, self.at, self.step = n, at, {}


class Event:

    def __init__(self, sem, value, loop):
        self.sem, self.value, self.loop = sem, value, loop


class LastTurn:

    def __init__(self, slot, loop):
        self.slot, self.loop = slot, loop


class Sem:
    def __init__(self, handle, start):
        self.handle, self.count = handle, start


class Slot:

    def __init__(self, ap):
        self.ap, self.last_use, self.in_loop, self.busy = ap, [], {}, False

    def free(self, loop):
        assert not self.busy
        self.busy = True
        waits = list(self.last_use)
        if loop is not None and not any(t.loop is loop for t in self.last_use):
            waits.append(LastTurn(self, loop))
        return waits

    def free_after(self, *events):
        self.last_use, self.busy = list(events), False
        for t in events:
            if t.loop is not None:
                self.in_loop[t.loop] = list(events)


ENGINES = ("tensor", "scalar", "vector", "gpsimd", "sync")
PRIME = 512


def op(build, *args, **kwargs):
    return lambda i: build(*args, **kwargs)


class Queues:
    def __init__(self, nc, stack):
        self.nc, self.stack = nc, stack
        self.queue = {e: [] for e in ENGINES}
        self.sems = []
        self.done = {e: self.sem(f"done_{e}", PRIME) for e in ENGINES if e != "sync"}
        self.loop_now = None

    def sem(self, name, start=0):
        s = Sem(self.stack.enter_context(self.nc.semaphore(name)), start)
        self.sems.append(s)
        return s

    @contextmanager
    def loop(self, n):
        lp = Loop(n, {s: s.count for s in self.sems})
        outer, self.queue = self.queue, {e: [] for e in ENGINES}
        self.loop_now = lp
        yield
        self.loop_now = None
        inner, self.queue = self.queue, outer
        for s in self.sems:
            lp.step[s] = s.count - lp.at.get(s, s.count)
            s.count += (n - 1) * lp.step[s]
        for e in ENGINES:
            if inner[e]:
                self.queue[e].append((lp, inner[e]))

    def add(self, engine, fn, waits, sem, inc):
        flat = []
        for w in waits:
            flat += w if isinstance(w, (list, tuple)) else [w]
        self.queue[engine].append((fn, [w for w in flat if w is not None], sem, inc))
        if sem is None:
            return None
        sem.count += inc
        return Event(sem, sem.count, self.loop_now)

    def pe(self, fn, *waits, signal=True):
        return self.add("tensor", fn, waits, self.done["tensor"] if signal else None, 1)

    def act(self, fn, *waits):
        return self.add("scalar", fn, waits, self.done["scalar"], 1)

    def dve(self, fn, *waits):
        return self.add("vector", fn, waits, self.done["vector"], 1)

    def pool(self, fn, *waits):
        return self.add("gpsimd", fn, waits, self.done["gpsimd"], 1)

    def dma(self, fn, sem, *waits, engine="sync"):
        return self.add(engine, fn, waits, sem, 16)

    def emit(self):
        with self.nc.Block() as block:
            for name in ENGINES:
                self._register(block, name)

    def _register(self, block, name):
        def program(eng):
            if name in self.done:
                eng.sem_inc(self.done[name].handle, PRIME)
            self._run(eng, self.queue[name], None, 0, {})

        {"tensor": block.tensor, "scalar": block.scalar, "vector": block.vector,
         "gpsimd": block.gpsimd, "sync": block.sync}[name](program)

    def _run(self, eng, items, loop, i, seen):
        for item in items:
            if isinstance(item[0], Loop):
                with eng.Fori(0, item[0].n) as j:
                    self._run(eng, item[1], item[0], j, dict(seen))
                continue
            fn, waits, sem, inc = item
            for w in waits:
                for handle, key, base, slope in self._values(w, loop):
                    if seen.get((key, slope), -1) >= base:
                        continue
                    seen[(key, slope)] = base
                    eng.wait_ge(handle, base if slope == 0 else i * slope + base)
            ins = fn(i)
            if sem is not None:
                ins.then_inc(sem.handle, inc)

    def _values(self, w, loop):
        if isinstance(w, LastTurn):
            out = []
            for t in w.slot.in_loop.get(w.loop, []):
                d = w.loop.step[t.sem]
                if t.value - d < 1:
                    raise ValueError("a loop's wait below one: raise PRIME")
                out.append((t.sem.handle, t.sem, t.value - d, d))
            return out
        if w.loop is None:
            return [(w.sem.handle, w.sem, w.value, 0)]
        d = w.loop.step[w.sem]
        if w.loop is loop:
            return [(w.sem.handle, w.sem, w.value, d)]
        return [(w.sem.handle, w.sem, w.value + (w.loop.n - 1) * d, 0)]


def constant_table():
    parts, at, n = [], {}, 0

    def put(name, a):
        nonlocal n
        full = np.zeros((P, a.shape[1]), np.float32)
        full[: a.shape[0]] = a
        parts.append(full)
        at[name] = (n, n + a.shape[1])
        n += a.shape[1]

    p = np.arange(P)
    put("ident", np.eye(P))
    put("ones", np.ones((P, P)))
    partner = np.where(p % 32 < 16, p + 16, p - 16)
    put("swap", (p[:, None] == partner[None, :]).astype(np.float32))
    pos = np.arange(NX_TOK)
    inv = (10000.0 ** (-np.arange(16, dtype=np.float32) * 2.0 / 32)).astype(np.float32)
    place = np.where((p % HD < 32)[:, None], pos[None, :] // GRID_W, pos[None, :] % GRID_W).astype(np.float32)
    ang = (place * inv[p % 16][:, None]).astype(np.float32)
    put("cos", np.cos(ang))
    put("sin", np.sin(ang) * np.where(p % 32 < 16, -1.0, 1.0)[:, None])
    t = np.arange(T)[:, None]
    s = np.arange(T)[None, :]
    same = (t >= NC_TOK) == (s >= NC_TOK)
    before = (t >= NC_TOK) & (s < NC_TOK)
    for d, see in enumerate((before | (same & (s <= t)), before | (same & (s >= t)))):
        m = np.where(see, 0.0, NEG).reshape(TT, P, T).transpose(1, 0, 2).reshape(P, TT * T)
        put(f"ml_mask{d}", m)
    sel = np.zeros((8, 8, P))
    for r in range(8):
        sel[r, r] = 1.0
    put("sel8", sel.reshape(8, 8 * P))
    put("is_fwd", (np.arange(8) < 4)[:, None].astype(np.float32))
    put("is_bwd", (np.arange(8) >= 4)[:, None].astype(np.float32))
    carry = np.ones(T)
    carry[0] = 0.0
    carry[NC_TOK::GLA_CHUNK] = 0.0
    put("gla_carry", np.tile(carry, (P, 1)))
    blk = p[:, None] // GLA_CHUNK == p[None, :] // GLA_CHUNK
    put("gla_mask0", (blk & (p[:, None] <= p[None, :])).astype(np.float32))
    put("gla_mask1", (blk & (p[:, None] >= p[None, :])).astype(np.float32))
    c = np.arange(GRID_W)
    start = np.clip(c - 8, 0, GRID_W - 16)
    ok = (c[None, :] >= start[:, None]) & (c[None, :] < start[:, None] + 16)
    put("na_mask", np.where(ok, 0.0, NEG)[p % GRID_W][:, np.arange(NX_TOK) % GRID_W])
    return np.ascontiguousarray(np.concatenate(parts, 1).astype(np.float32)), at


def columns(v):
    return np.asarray(v).reshape(-1, P).T


SMALL = [("c_ctx", 8), ("c", 8), ("ada_b", 2 * 72), ("norm_g", 48), ("final_g", 8), ("diff_norm_g", 1),
         ("ml_norm_g", 4), ("conv_w", 12), ("conv_b", 4), ("gla_b", 8), ("gla_norm_g", 2),
         ("c_ctx_2", 8), ("c_2", 8), ("ada_b_2", 2 * 48), ("ln", 64), ("q_norm", 4), ("kv_norm", 2),
         ("na_b", 24), ("lambda", 4 * HD), ("gate_b", 2), ("na_bv", D)]


def small_at():
    at, n = {}, 0
    for name, w in SMALL:
        at[name] = (n, n + w)
        n += w
    return at, n


def small_table(a):
    def flat(x):
        return columns(np.asarray(x).reshape(-1))

    gate = np.zeros((P, 2), np.float32)
    gate[:8] = np.asarray(a["mlstm_gate_b"]).reshape(2, 8).T
    qb = np.asarray(a["na_b_qkv_2"]).reshape(3, D)
    ln = np.stack([np.asarray(a[k]) for k in ("ln1_g_2", "ln1_b_2", "ln2_g_2", "ln2_b_2")], 1)
    parts = dict(
        c_ctx=flat(a["c_ctx"]), c=flat(a["c"]), ada_b=flat(a["ada_b"]), norm_g=flat(a["norm_g"]),
        final_g=flat(a["final_g"]), diff_norm_g=flat(a["diff_norm_g"]), ml_norm_g=flat(a["mlstm_norm_g"]),
        conv_w=flat(a["mlstm_conv_w"]), conv_b=flat(a["mlstm_conv_b"]), gla_b=flat(a["gla_b_gate"]),
        gla_norm_g=flat(a["gla_norm_g"]), c_ctx_2=flat(a["c_ctx_2"]), c_2=flat(a["c_2"]),
        ada_b_2=flat(a["ada_b_2"]), ln=flat(ln), q_norm=flat(a["mla_q_norm_2"]), kv_norm=flat(a["mla_kv_norm_2"]),
        na_b=flat(qb), gate_b=gate,
        na_bv=np.broadcast_to(qb[2], (P, D)),
    )
    parts["lambda"] = np.broadcast_to(np.asarray(a["diff_lambda"]).reshape(-1), (P, 4 * HD))
    return np.ascontiguousarray(np.concatenate([parts[n] for n, _ in SMALL], 1))


def slabs(w, k_tiles, cols):
    K, N = w.shape
    r = w.reshape(K // (P * k_tiles), k_tiles, P, N // cols, cols)
    return np.ascontiguousarray(r.transpose(3, 0, 2, 1, 4).reshape(-1, P, k_tiles * cols))


def slab_arrays(a):
    out = {}
    for l in range(2):
        out[f"ada{l}"] = slabs(np.asarray(a["ada_w"])[l], 8, 256)
        out[f"ada2{l}"] = slabs(np.asarray(a["ada_w_2"])[l], 8, 256)
        for h in range(2):
            w = np.asarray(a["ffn_w_in"])[l, h]
            ab = w.reshape(D, 2, FT, P).transpose(0, 2, 1, 3).reshape(D, 2 * FF)
            out[f"ffn_in{l}{h}"] = slabs(ab, 8, 256)
            out[f"ffn_out{l}{h}"] = slabs(np.asarray(a["ffn_w_out"])[l, h], 11, P)
        out[f"mlp1{l}"] = slabs(np.asarray(a["mlp_w1_2"])[l], 8, 256)
        out[f"mlp2{l}"] = slabs(np.asarray(a["mlp_w2_2"])[l], 16, P)
    e = np.asarray(a["even_w_in"])[0]
    q, k, v, mqk, mv, mo, g = np.split(e, np.cumsum([512] * 6), axis=1)
    out["even_fm"] = slabs(np.concatenate([q, k, mqk, mo], 1), 8, 256)
    out["even_tm"] = slabs(np.concatenate([v, mv], 1), 8, 256)
    out["even_gates"] = slabs(g, 8, 16)
    out["even_out"] = slabs(np.asarray(a["even_w_out"])[0], 8, 256)
    o = np.asarray(a["odd_w_in"])[0]
    q, k, v, r, lr = np.split(o, np.cumsum([512, 512, 1024, 1024]), axis=1)
    out["odd_fm"] = slabs(np.concatenate([q, k, r], 1), 8, 256)
    out["odd_tm"] = slabs(v, 8, 256)
    out["odd_rank"] = slabs(lr, 8, 32)
    out["odd_gate"] = np.ascontiguousarray(np.asarray(a["gla_w_gate"])[0].transpose(1, 0, 2).reshape(1, 16, 1024))
    out["odd_out"] = slabs(np.asarray(a["odd_w_out"])[0], 8, 256)
    out["mla_dq"] = slabs(np.asarray(a["mla_w_dq_2"])[0], 8, 256)
    uq = np.asarray(a["mla_w_uq_2"])[0].reshape(512, 4, 2, 192)
    uq = np.concatenate([uq[..., :P].reshape(512, 4, 2 * P), uq[..., P:].reshape(512, 4, P)], 2).reshape(512, -1)
    out["mla_uq"] = slabs(uq, 4, 384)
    dkv = np.asarray(a["mla_w_dkv_2"])[0]
    out["mla_dkv"] = slabs(dkv[:, :256], 8, 256)
    out["mla_kpe"] = slabs(np.concatenate([dkv[:, 256:]] * 2, 1), 8, P)
    ukv = np.asarray(a["mla_w_ukv_2"])[0].reshape(256, 8, 2, P).transpose(0, 2, 1, 3).reshape(256, -1)
    out["mla_ukv"] = slabs(ukv, 2, 1024)
    out["mla_out"] = slabs(np.asarray(a["mla_w_o_2"])[0], 8, 256)
    qkv = np.asarray(a["na_w_qkv_2"])[0]
    out["na_fm"] = slabs(qkv[:, : 2 * D], 8, 256)
    out["na_tm"] = slabs(qkv[:, 2 * D:], 8, 256)
    out["na_out"] = slabs(np.asarray(a["na_w_o_2"])[0], 8, 256)
    out["na_rpb"] = np.ascontiguousarray(np.asarray(a["na_rpb_2"])[0][:, ::-1, ::-1])
    return out


def feature_major(x):
    return np.asarray(x).reshape(-1, DT, P).transpose(2, 1, 0)


def lay_out(a):
    x = np.concatenate([feature_major(np.asarray(a["ctx"])[0]), feature_major(np.asarray(a["x"])[0])], 2)
    out = slab_arrays(a)
    out["tokens"] = np.ascontiguousarray(x)
    out["ctx_2"] = np.ascontiguousarray(feature_major(np.asarray(a["ctx_2"])[0]))
    out["small"] = small_table(a)
    out["constants"] = constant_table()[0]
    return out


class Model:

    def __init__(self, nc, stack, w, out):
        self.nc, self.w, self.out = nc, w, out
        self.q = Queues(nc, stack)
        self.c_at = constant_table()[1]
        self.s_at, n_small = small_at()

        def sb(name, shape):
            return stack.enter_context(nc.sbuf_tensor(f"sb_{name}", list(shape), F32))

        n_const = max(b for _, b in self.c_at.values())
        self.const = sb("const", (P, n_const))
        self.small = sb("small", (P, n_small))
        self.x = sb("x_res", (P, DT, T))
        self.h = sb("h", (P, DT, T))
        self.big = sb("big", (P, FT2, T))
        self.s_cols = sb("s_cols", (P, 2, DT, 2))
        self.mods = sb("mods", (P, 72, 2))
        self.scales = sb("scales", (P, DT, 2))
        self.gates = sb("gates", (P, DT, 2))
        self.colmath = sb("colmath", (P, 64))
        self.stat = sb("stat", (P, T))
        self.rstd = sb("rstd", (P, T))
        self.slab = [Slot(sb(f"slab{i}", (P, SLAB))) for i in range(W_SLOTS)]
        self.slab_sem = [self.q.sem(f"slab{i}_loaded") for i in range(W_SLOTS)]
        self.slab_at = 0
        self.temp = [Slot(sb(f"temp{i}", (P, T))) for i in range(4)]
        self.temp_at = 0
        self.bank = [Slot(stack.enter_context(nc.psum_tensor(f"bank{i}", [P, 512], F32))) for i in range(8)]
        self.bank_at = 0
        self.ring = range(8)
        self.rows = sb("rows", (16, 4, T))
        self.fcol = sb("fcol", (P, TT * 8))
        self.neg_lam = sb("neg_lam", (P, 4))
        self.cols = [Slot(sb(f"cols{i}", (P, 8))) for i in range(6)]
        self.cols_at = 0
        self.gla_kt = [Slot(sb(f"gla_kt{i}", (P, T))) for i in range(2)]
        self.na_bias = [Slot(sb(f"na_bias{i}", (P, 6 * GRID_W))) for i in range(2)]
        self.gla_s = [Slot(sb(f"gla_s{i}", (P, 256))) for i in range(2)]
        self.gla_at = [Slot(sb(f"gla_at{i}", (P, 256))) for i in range(2)]
        self.load_sem = self.q.sem("inputs_loaded")
        self.store_sem = self.q.sem("output_stored")
        self.side_sem = self.q.sem("side_loaded")
        self.bias_sem = [self.q.sem(f"bias{i}_loaded") for i in range(2)]
        self.ready = []
        self.mods_free = self.scales_free = self.gates_free = self.rstd_free = []
        self.h_free = self.big_free = self.x_free = []

    def C(self, name, rows=P):
        a, b = self.c_at[name]
        return self.const[0:rows, a:b]

    def S(self, name, j=0, n=None):
        a, b = self.s_at[name]
        return self.small[:, a + j:(a + j + n if n else b)]

    def next_bank(self):
        b = self.bank[self.ring[self.bank_at % len(self.ring)]]
        self.bank_at += 1
        return b

    def next_temp(self):
        b = self.temp[self.temp_at % 4]
        self.temp_at += 1
        return b

    def next_cols(self):
        b = self.cols[self.cols_at % len(self.cols)]
        self.cols_at += 1
        return b

    def load_slab(self, name, index, cols):
        k = self.slab_at % W_SLOTS
        self.slab_at += 1
        buf, src = self.slab[k], self.w[name]

        def load(i):
            n = index(i)
            part = src[n, :, :] if isinstance(n, int) else src[bass.ds(n, 1), :, :].rearrange("a p n -> p (a n)")
            return self.nc.sync.dma_start(buf.ap[:, 0:cols], part)

        t = self.q.dma(load, self.slab_sem[k], buf.free(self.q.loop_now))
        return buf, t

    def matmuls(self, out, pairs, *waits):
        nc, n = self.nc, len(pairs)
        for j, (a, b) in enumerate(pairs):
            t = self.q.pe(op(nc.tensor.matmul, out, a, b, start=(j == 0), stop=(j == n - 1)),
                          *(waits if j == 0 else ()), signal=(j == n - 1))
        return t

    def load_inputs(self):
        q, nc = self.q, self.nc
        q.dma(op(nc.sync.dma_start, self.small[:, :], self.w["small"]), self.load_sem)
        q.dma(op(nc.sync.dma_start, self.const[:, :], self.w["constants"]), self.load_sem)
        t = q.dma(op(nc.sync.dma_start, self.x[:, :, :], self.w["tokens"]), self.load_sem)
        self.ready = [t]
        self.x_ready = [t]
        for b, (nctx, nlat) in enumerate((("c_ctx", "c"), ("c_ctx_2", "c_2"))):
            for s, name in enumerate((nctx, nlat)):
                t = q.act(op(nc.scalar.activation, self.s_cols[:, b, :, s], self.S(name), ACT.Silu), self.ready)
        self.s_ready = t

    def modulation(self, name, block, n_slabs, bias, bias_at):
        q, nc, unroll = self.q, self.nc, W_SLOTS
        ps = Slot(self.bank[7].ap)
        ps.last_use = self.bank[7].last_use
        free = self.mods_free
        with q.loop(n_slabs // unroll):
            waits = ps.free(self.q.loop_now)
            for j in range(unroll):
                buf, loaded = self.load_slab(name, lambda i, j=j: i * unroll + j, SLAB)
                for t in range(2):
                    done = self.matmuls(
                        ps.ap[:, 4 * j + 2 * t:4 * j + 2 * t + 2],
                        [(buf.ap[:, k * 256 + t * P:k * 256 + (t + 1) * P], self.s_cols[:, block, k, :]) for k in range(DT)],
                        loaded, self.s_ready, waits)
                buf.free_after(done)
            bias_cols = self.S(bias)

            def evacuate(i):
                tile0 = i * (2 * unroll)
                b = bias_cols[:, bass.ds(tile0 + bias_at, 2 * unroll)]
                return nc.vector.tensor_tensor(
                    self.mods[:, bass.ds(tile0, 2 * unroll), :],
                    ps.ap[:, 0:4 * unroll].rearrange("p (t s) -> p t s", s=2),
                    b.rearrange("p (t o) -> p t o", o=1).broadcast_to([P, 2 * unroll, 2]), ALU.add)

            got = q.dve(evacuate, done, free, self.ready)
            ps.free_after(got)
        self.bank[7].free_after(got)
        self.mods_ready = got

    def scale_and_gate(self, shift, scale, gate, g, half):
        q, nc = self.q, self.nc
        sc = self.mods[:, scale * DT:(scale + 1) * DT, :]
        if g is None:
            t = q.dve(op(nc.vector.tensor_scalar, self.scales[:, :, :], sc, 1.0, None, ALU.add),
                      self.mods_ready, self.scales_free)
        else:
            gb = g.rearrange("p (t o) -> p t o", o=1).broadcast_to([P, DT, 2])
            t = q.dve(op(nc.vector.scalar_tensor_tensor, self.scales[:, :, :], sc, 1.0, gb, ALU.add, ALU.mult),
                      self.mods_ready, self.scales_free)
        t2 = q.dve(op(nc.vector.tensor_scalar, self.gates[:, :, :], self.mods[:, gate * DT:(gate + 1) * DT, :], 0.5 if half else 1.0, None, ALU.mult),
            self.mods_ready, self.gates_free)
        self.scales_ready, self.gates_ready = t, t2
        self.mods_free = [t2]
        self.shift = lambda k, s: self.mods[:, shift * DT + k, s:s + 1]

    def inverse_rms(self, tiles, dim, eps, cols, *waits, scale=1.0):
        q, nc = self.q, self.nc
        n = cols.stop - cols.start
        bank = self.next_bank()
        free = bank.free(self.q.loop_now)
        for k, src in enumerate(tiles):
            tmp = self.next_temp()
            sq = q.act(op(nc.scalar.activation, tmp.ap[:, 0:n], src, ACT.Square),
                       tmp.free(self.q.loop_now), *waits)
            done = q.pe(op(nc.tensor.matmul, bank.ap[:, 0:n], self.C("ones"), tmp.ap[:, 0:n], start=(k == 0), stop=(k == len(tiles) - 1)),
                sq, free, self.ready)
            tmp.free_after(done)
        a = q.dve(op(nc.vector.tensor_scalar, self.stat[:, 0:n], bank.ap[:, 0:n], 1.0 / dim, eps, ALU.mult, ALU.add), done)
        bank.free_after(a)
        b = q.act(op(nc.scalar.activation, self.stat[:, 0:n], self.stat[:, 0:n], ACT.Sqrt), a)
        c = q.dve(op(nc.vector.reciprocal, self.rstd[:, 0:n], self.stat[:, 0:n]), b, self.rstd_free)
        self.rstd_free = []
        return c

    def ada_norm(self, streams):
        q, nc = self.q, self.nc
        lo = streams[0][1].start
        cols = slice(lo, T)
        r = self.inverse_rms([self.x[:, k, cols] for k in range(DT)], D, RMS_EPS, cols, self.x_ready)
        out, shift = [], self.shift
        for k in range(DT):
            for s, c in streams:
                a = q.dve(op(nc.vector.scalar_tensor_tensor, self.h[:, k, c], self.x[:, k, c], self.scales[:, k, s:s + 1],
                    self.rstd[:, c.start - lo:c.stop - lo], ALU.mult, ALU.mult),
                    r, self.scales_ready, self.h_free)
                out.append(q.act(op(nc.scalar.activation, self.h[:, k, c], self.h[:, k, c], ACT.Identity, bias=shift(k, s)), a))
        self.rstd_free = [a]
        self.scales_free = [a]
        self.mods_free = self.mods_free + [out[-1]]
        self.h_ready = [out[-1]]

    def add_branch(self, name, n_slabs, tiles_of, src, src_ready, streams, alpha=None):
        q, nc = self.q, self.nc
        lo = streams[0][1].start
        n = T - lo
        banks = [Slot(self.bank[b].ap) for b in range(2)]
        for b in range(2):
            banks[b].last_use = self.bank[b].last_use
        temps = [Slot(self.temp[b].ap) for b in range(2)]
        for b in range(2):
            temps[b].last_use = self.temp[b].last_use

        def finish(tile, bank, temp, done):
            free = temp.free(self.q.loop_now)
            for s, c in streams:
                g = q.act(lambda i, s=s, c=c: nc.scalar.activation(
                    temp.ap[:, c.start - lo:c.stop - lo], bank.ap[:, c.start - lo:c.stop - lo], ACT.Identity,
                    scale=self.gate_col(tile(i), s)), done, free, self.gates_ready)
            bank.free_after(g)
            xk = lambda i: self.x_tile(tile(i), lo)
            if alpha is None:
                a = q.dve(lambda i: nc.vector.tensor_tensor(xk(i), xk(i), temp.ap[:, 0:n], ALU.add), g, self.x_free)
            else:
                a = q.dve(lambda i: nc.vector.scalar_tensor_tensor(
                    xk(i), xk(i), alpha, temp.ap[:, 0:n], ALU.mult, ALU.add), g, self.x_free)
            temp.free_after(a)
            return a, g

        tile_no = 0
        per = 2 * W_SLOTS if tiles_of == "cols" else W_SLOTS // 2
        with q.loop(n_slabs // W_SLOTS):
            for j in range(W_SLOTS):
                if tiles_of == "cols":
                    buf, loaded = self.load_slab(name, lambda i, j=j: i * W_SLOTS + j, SLAB)
                    for t in range(2):
                        bank, temp = banks[tile_no % 2], temps[tile_no % 2]
                        done = self.matmuls(bank.ap[:, 0:n], [
                            (buf.ap[:, k * 256 + t * P:k * 256 + (t + 1) * P], src(k, lo)) for k in range(DT)],
                            loaded, src_ready, bank.free(self.q.loop_now))
                        if t == 1:
                            buf.free_after(done)
                        a, g = finish(lambda i, tn=tile_no: i * per + tn, bank, temp, done)
                        tile_no += 1
                else:
                    half, nk = j % 2, tiles_of
                    buf, loaded = self.load_slab(name, lambda i, j=j: i * W_SLOTS + j, nk * P)
                    bank, temp = banks[tile_no % 2], temps[tile_no % 2]
                    waits = bank.free(self.q.loop_now) if half == 0 else []
                    for k in range(nk):
                        done = q.pe(op(nc.tensor.matmul, bank.ap[:, 0:n], buf.ap[:, k * P:(k + 1) * P], src(half * nk + k, lo),
                            start=(half == 0 and k == 0), stop=(half == 1 and k == nk - 1)),
                            *((loaded, src_ready, waits) if k == 0 else ()), signal=(k == nk - 1))
                    buf.free_after(done)
                    if half == 1:
                        a, g = finish(lambda i, tn=tile_no: i * per + tn, bank, temp, done)
                        tile_no += 1
        for b in range(2):
            self.bank[b].free_after(g)
            self.temp[b].free_after(a)
        self.x_ready = [a]
        self.x_free = []
        self.gates_free = [g]
        return done

    def gate_col(self, k, s):
        if isinstance(k, int):
            return self.gates[:, k, s:s + 1]
        return self.gates[:, bass.ds(k, 1), s]

    def x_tile(self, k, lo):
        if isinstance(k, int):
            return self.x[:, k, lo:T]
        return self.x[:, bass.ds(k, 1), lo:T].rearrange("p a n -> p (a n)")

    def big_tile(self, k, lo=0, hi=T):
        if isinstance(k, int):
            return self.big[:, k, lo:hi]
        return self.big[:, bass.ds(k, 1), lo:hi].rearrange("p a n -> p (a n)")

    def swiglu(self, l, half, streams):
        lo = streams[0][1].start
        n = T - lo
        q, nc = self.q, self.nc
        name = f"ffn_in{l}{half}"
        banks = [Slot(self.bank[b].ap) for b in range(4)]
        temps = [Slot(self.temp[b].ap) for b in range(2)]
        for b in range(4):
            banks[b].last_use = self.bank[b].last_use
        for b in range(2):
            temps[b].last_use = self.temp[b].last_use

        def hidden_tile(j, index):
            buf, loaded = self.load_slab(name, index, SLAB)
            pair = banks[2 * (j % 2)], banks[2 * (j % 2) + 1]
            temp = temps[j % 2]
            done = []
            for t in range(2):
                done.append(self.matmuls(pair[t].ap[:, 0:n], [
                    (buf.ap[:, k * 256 + t * P:k * 256 + (t + 1) * P], self.h[:, k, lo:T]) for k in range(DT)],
                    loaded, self.h_ready, pair[t].free(self.q.loop_now)))
            buf.free_after(done[1])
            a = q.act(op(nc.scalar.activation, temp.ap[:, 0:n], pair[0].ap[:, 0:n], ACT.Silu),
                      done[0], temp.free(self.q.loop_now))
            pair[0].free_after(a)
            b = q.dve(lambda i: nc.vector.tensor_tensor(
                self.big_tile(index(i), lo), temp.ap[:, 0:n], pair[1].ap[:, 0:n], ALU.mult),
                a, done[1], self.big_free)
            pair[1].free_after(b)
            temp.free_after(b)
            return b, done[1]

        with q.loop(FT // W_SLOTS):
            for j in range(W_SLOTS):
                b, d = hidden_tile(j, lambda i, j=j: i * W_SLOTS + j)
        for j in range(FT // W_SLOTS * W_SLOTS, FT):
            b, d = hidden_tile(j, lambda i, j=j: j)
        for k in range(4):
            self.bank[k].free_after(b)
        for k in range(2):
            self.temp[k].free_after(b)
        self.h_free = [d]
        d = self.add_branch(f"ffn_out{l}{half}", 2 * DT, FT // 2, lambda k, lo: self.big[:, k, lo:T], b, streams)
        self.big_free = [d]

    def relu_mlp(self, l, streams):
        lo = streams[0][1].start
        n = T - lo
        q, nc = self.q, self.nc
        banks = [Slot(self.bank[b].ap) for b in range(4)]
        temps = [Slot(self.temp[b].ap) for b in range(2)]
        for b in range(4):
            banks[b].last_use = self.bank[b].last_use
        for b in range(2):
            temps[b].last_use = self.temp[b].last_use
        with q.loop(FT2 // 2 // W_SLOTS):
            for j in range(W_SLOTS):
                buf, loaded = self.load_slab(f"mlp1{l}", lambda i, j=j: i * W_SLOTS + j, SLAB)
                for t in range(2):
                    tile = lambda i, j=j, t=t: i * (2 * W_SLOTS) + (2 * j + t)
                    bank, temp = banks[(2 * j + t) % 4], temps[t]
                    done = self.matmuls(bank.ap[:, 0:n], [
                        (buf.ap[:, k * 256 + t * P:k * 256 + (t + 1) * P], self.h[:, k, lo:T]) for k in range(DT)],
                        loaded, self.h_ready, bank.free(self.q.loop_now))
                    if t == 1:
                        buf.free_after(done)
                    a = q.act(op(nc.scalar.activation, temp.ap[:, 0:n], bank.ap[:, 0:n], ACT.Relu), done, temp.free(self.q.loop_now))
                    bank.free_after(a)
                    b = q.dve(lambda i, temp=temp, tile=tile: nc.vector.tensor_tensor(
                        self.big_tile(tile(i), lo), temp.ap[:, 0:n], temp.ap[:, 0:n], ALU.mult), a, self.big_free)
                    temp.free_after(b)
        for k in range(4):
            self.bank[k].free_after(b)
        for k in range(2):
            self.temp[k].free_after(b)
        self.h_free = [done]
        d = self.add_branch(f"mlp2{l}", 2 * DT, FT2 // 2, lambda k, lo: self.big[:, k, lo:T], b, streams, alpha=ALPHA)
        self.big_free = [d]

    def project_fm(self, name, n_slabs, first, src, ready, kt=DT, bias=None, lo=0, slab0=0):
        q, nc = self.q, self.nc
        n = T - lo
        banks = [Slot(self.bank[b].ap) for b in range(4)]
        for b in range(4):
            banks[b].last_use = self.bank[b].last_use
        out = None

        def slab(j, index, out_tile):
            buf, loaded = self.load_slab(name, index, kt * 256)
            for t in range(2):
                bank = banks[(2 * j + t) % 4]
                done = self.matmuls(bank.ap[:, 0:n], [
                    (buf.ap[:, k * 256 + t * P:k * 256 + (t + 1) * P], src(k, lo)) for k in range(kt)],
                    loaded, ready, bank.free(self.q.loop_now))
                if t == 1:
                    buf.free_after(done)
                tile = lambda i, t=t: out_tile(i) + t

                def copy(i, bank=bank, tile=tile, eng=t):
                    if bias is None:
                        if eng == 0:
                            return nc.scalar.activation(self.big_tile(tile(i) + first, lo), bank.ap[:, 0:n], ACT.Identity)
                        return nc.vector.tensor_copy(self.big_tile(tile(i) + first, lo), bank.ap[:, 0:n])
                    k = tile(i)
                    col = bias[:, k:k + 1] if isinstance(k, int) else bias[:, bass.ds(k, 1)]
                    if eng == 0:
                        return nc.scalar.activation(self.big_tile(k + first, lo), bank.ap[:, 0:n], ACT.Identity, bias=col)
                    return nc.vector.tensor_scalar(self.big_tile(k + first, lo), bank.ap[:, 0:n], col, None, ALU.add)

                c = (q.act if t == 0 else q.dve)(copy, done, self.big_free)
                bank.free_after(c)
                last[t] = c
            return done

        last = [None, None]
        if n_slabs >= 2 * W_SLOTS:
            with q.loop(n_slabs // W_SLOTS):
                for j in range(W_SLOTS):
                    done = slab(j, lambda i, j=j: i * W_SLOTS + j, lambda i, j=j: i * (2 * W_SLOTS) + 2 * j)
            rest = range(n_slabs // W_SLOTS * W_SLOTS, n_slabs)
        else:
            rest = range(n_slabs)
        for j in rest:
            done = slab(j, lambda i, j=j: slab0 + j, lambda i, j=j: 2 * j)
        for k in range(4):
            self.bank[k].free_after(*last)
        return list(last), done

    def project_tm(self, name, n_slabs, first, src, ready, bias=None):
        q, nc = self.q, self.nc
        last = {}
        view = self.big[:, first:first + 2 * n_slabs, :].rearrange("p a n -> p (a n)").rearrange(
            "p (t n) -> p t n", t=TT)
        for j in range(n_slabs):
            buf, loaded = self.load_slab(name, lambda i, j=j: j, SLAB)
            for tt in range(TT):
                bank = self.next_bank()
                done = self.matmuls(bank.ap[:, 0:256], [
                    (src(k)[:, tt * P:(tt + 1) * P], buf.ap[:, k * 256:(k + 1) * 256]) for k in range(DT)],
                    loaded, ready, bank.free(self.q.loop_now))
                dst = view[:, tt, j * 256:(j + 1) * 256]
                if bias is not None:
                    c = q.dve(op(nc.vector.tensor_tensor, dst, bank.ap[:, 0:256], bias[:, j * 256:(j + 1) * 256], ALU.add), done, self.big_free)
                    last[0] = c
                elif tt % 2:
                    c = q.act(op(nc.scalar.activation, dst, bank.ap[:, 0:256], ACT.Identity),
                              done, self.big_free)
                    last[0] = c
                else:
                    c = q.dve(op(nc.vector.tensor_copy, dst, bank.ap[:, 0:256]),
                              done, self.big_free)
                    last[1] = c
                bank.free_after(c)
            buf.free_after(done)
        return view, list(last.values()), done

    def store_output(self, src, ready):
        q, nc = self.q, self.nc
        t = q.dma(op(nc.sync.dma_start, self.out, src), self.store_sem, ready)
        q.add("sync", op(nc.sync.nop, ), [t], None, 0)

    def transpose_weights(self, w, qt, n_keys, w_t, w_ready, wt_free):
        q, nc = self.q, self.nc
        bank = self.next_bank()
        free = bank.free(self.q.loop_now)
        nk = n_keys // P
        for kt in range(nk):
            done = q.pe(op(nc.tensor.transpose, bank.ap[:, kt * P:(kt + 1) * P], w[:, kt * P:(kt + 1) * P], self.C("ident")),
                w_ready, free, signal=(kt == nk - 1))
        copy = q.act(op(nc.scalar.activation, w_t[:, 0:nk, qt * P:(qt + 1) * P], bank.ap[:, 0:nk * P].rearrange("p (k n) -> p k n", k=nk), ACT.Identity),
            done, wt_free)
        bank.free_after(copy)
        return done, copy

    def weigh_values(self, value, w_t, ready, lo=0):
        q, nc = self.q, self.nc
        bank = self.next_bank()
        free = bank.free(self.q.loop_now)
        for kt in range(TT):
            c = slice(lo if kt < NC_TOK // P else NC_TOK, T)
            done = q.pe(op(nc.tensor.matmul, bank.ap[:, c], value(kt), w_t[:, kt, c], start=(kt == 0), stop=(kt == TT - 1)),
                ready, free, signal=(kt == TT - 1))
        return bank, done

    def in_order(self, units, start, finish):
        held = None
        for u in units:
            got = start(u)
            if held is not None:
                finish(*held)
            held = (u, got)
        finish(*held)

    def mix_pair(self, pair, n, coef, ready):
        q, nc = self.q, self.nc
        a = q.pool(op(nc.gpsimd.tensor_scalar, pair[0].ap[:, 0:n], pair[0].ap[:, 0:n], coef[:, 0:1], None, ALU.mult), ready)
        return q.dve(op(nc.vector.scalar_tensor_tensor, pair[0].ap[:, 0:n], pair[1].ap[:, 0:n], coef[:, 1:2], pair[0].ap[:, 0:n], ALU.mult, ALU.add), a)

    def rope(self, tile, ready):
        q, nc = self.q, self.nc
        x = self.big[:, tile, LAT]
        bank, tmp = self.next_bank(), self.next_temp()
        sw = self.matmuls(bank.ap[:, 0:NX_TOK], [(self.C("swap"), x)], ready, bank.free(self.q.loop_now))
        a = q.dve(op(nc.vector.tensor_tensor, tmp.ap[:, 0:NX_TOK], bank.ap[:, 0:NX_TOK], self.C("sin"), ALU.mult),
                  sw, tmp.free(self.q.loop_now))
        bank.free_after(a)
        b = q.pool(op(nc.gpsimd.tensor_tensor, x, x, self.C("cos"), ALU.mult), sw)
        c = q.pool(op(nc.gpsimd.tensor_tensor, x, x, tmp.ap[:, 0:NX_TOK], ALU.add), a, b)
        tmp.free_after(c)
        return c

    def even_mixer(self):
        q, nc = self.q, self.nc
        src = lambda k, lo=0: self.h[:, k, lo:T]
        Q0, K0, MQK0, OP0, V0, WT = 0, 4, 8, 12, 16, (24, 28)
        fm, _ = self.project_fm("even_fm", 8, 0, src, self.h_ready)
        vals, tm, _ = self.project_tm("even_tm", 4, V0, src, self.h_ready)
        buf, loaded = self.load_slab("even_gates", lambda i: 0, 8 * 16)
        for r in range(2):
            bank = self.next_bank()
            done = self.matmuls(bank.ap[0:8, :], [
                (buf.ap[:, k * 16 + 8 * r:k * 16 + 8 * r + 8], src(k)) for k in range(DT)],
                loaded, self.h_ready, bank.free(self.q.loop_now))
            t = q.act(op(nc.scalar.activation, self.rows[0:8, r, :], bank.ap[0:8, :], ACT.Identity, bias=self.S("gate_b", r, 1)[0:8, :]), done)
            bank.free_after(t)
        buf.free_after(done)
        h_free = done
        rows = lambda r: self.rows[0:8, r, :]
        g_ready, f_ready = self.forget_sums(rows, t)
        lam = self.diff_lambda()

        for j in range(4):
            t = q.pool(op(nc.gpsimd.tensor_scalar, self.big[:, Q0 + j, :], self.big[:, Q0 + j, :], HD ** -0.5, None, ALU.mult), fm)
        roped = [self.rope(Q0 + j, [t, *fm]) for j in range(8)]
        conv = self.conv_silu(MQK0, WT[0], fm)
        for j in range(4):
            og = q.act(op(nc.scalar.activation, self.big[:, OP0 + j, :], self.big[:, OP0 + j, :], ACT.Sigmoid), fm)

        wt_free = [conv, conv]
        h_ready = []
        n_keys = lambda qt: NC_TOK if qt < NC_TOK // P else T

        for hd in range(4):
            w_t = self.big[:, WT[hd % 2]:WT[hd % 2] + TT, :]
            copies = []

            def scores(qt, hd=hd):
                n = n_keys(qt)
                pair = self.temp[2 * (qt % 2):2 * (qt % 2) + 2]
                col = self.next_cols()
                free = col.free(self.q.loop_now)
                for c in range(2):
                    bank = self.next_bank()
                    s = self.matmuls(bank.ap[:, 0:n], [(
                        self.big[HD * c:HD * c + HD, Q0 + hd, qt * P:(qt + 1) * P],
                        self.big[HD * c:HD * c + HD, K0 + hd, 0:n])], roped, bank.free(self.q.loop_now))
                    m = q.dve(op(nc.vector.tensor_reduce, col.ap[:, c:c + 1], bank.ap[:, 0:n], AX.X, ALU.max, negate=True), s, free)
                    e = q.act(op(nc.scalar.activation, pair[c].ap[:, 0:n], bank.ap[:, 0:n], ACT.Exp, bias=col.ap[:, c:c + 1],
                        accum_out=col.ap[:, 2 + c:3 + c]), m, pair[c].free(self.q.loop_now))
                    bank.free_after(e)
                r = q.dve(op(nc.vector.reciprocal, col.ap[:, 4:6], col.ap[:, 2:4]), e)
                r2 = q.dve(op(nc.vector.tensor_tensor, col.ap[:, 5:6], col.ap[:, 5:6], self.neg_lam[:, 0:1], ALU.mult), r, lam)
                w = self.mix_pair(pair, n, col.ap[:, 4:6], [r, r2, e])
                col.free_after(w)
                pair[1].free_after(w)
                return pair[0], w

            def turn(qt, got, hd=hd):
                w, ready = got
                done, copy = self.transpose_weights(w.ap, qt, n_keys(qt), w_t, ready, wt_free[hd % 2])
                w.free_after(done)
                copies.append(copy)

            self.in_order(range(TT), scores, turn)
            bank, done = self.weigh_values(lambda kt, hd=hd: vals[:, kt, hd * P:(hd + 1) * P], w_t, copies + tm)
            wt_free[hd % 2] = done
            o = q.act(op(nc.scalar.activation, self.h[:, hd, :], bank.ap[:, :], ACT.Identity), done, h_free)
            bank.free_after(o)
            r = self.inverse_rms([self.h[:, hd, :]], P, RMS_EPS, slice(0, T), o)
            y = q.dve(op(nc.vector.scalar_tensor_tensor, self.h[:, hd, :], self.h[:, hd, :], self.neg_lam[:, 1:2], self.rstd[:, 0:T], ALU.mult, ALU.mult), r, lam)
            self.rstd_free = [y]

        self.ring = range(6)
        self.bank_at = 0
        for hd in range(4):
            w_t = self.big[:, WT[hd % 2]:WT[hd % 2] + TT, :]
            copies = []
            for d in range(2):
                row = 4 * d + hd
                g_bank = self.bank[6 + d]
                g_all = self.matmuls(g_bank.ap[:, :], [(self.C("sel8", 8)[:, row * P:(row + 1) * P], rows(0))],
                                     g_ready, g_bank.free(self.q.loop_now))
            base = HD * (hd % 2)

            def weights(qt, hd=hd, g_all=g_all, base=base):
                n = n_keys(qt)
                pair = self.temp[2 * (qt % 2):2 * (qt % 2) + 2]
                col = self.next_cols()
                free = col.free(self.q.loop_now)
                bank = self.next_bank()
                s = self.matmuls(bank.ap[:, 0:n], [(
                    self.big[base:base + HD, MQK0 + hd // 2, qt * P:(qt + 1) * P],
                    self.big[base:base + HD, MQK0 + 2 + hd // 2, 0:n])], conv, bank.free(self.q.loop_now))
                exps = []
                for d in range(2):
                    mask = self.C(f"ml_mask{d}")[:, qt * T:qt * T + n]
                    a = q.dve(op(nc.vector.tensor_tensor, pair[d].ap[:, 0:n], self.bank[6 + d].ap[:, 0:n], mask, ALU.add), g_all, pair[d].free(self.q.loop_now))
                    m = q.dve(op(nc.vector.tensor_reduce, col.ap[:, d:d + 1], pair[d].ap[:, 0:n], AX.X, ALU.max, negate=True), a, free)
                    exps.append(q.act(op(nc.scalar.activation, pair[d].ap[:, 0:n], pair[d].ap[:, 0:n], ACT.Exp, bias=col.ap[:, d:d + 1]), m))
                f = self.fcol[:, qt * 8:(qt + 1) * 8].rearrange("p (d h) -> p h d", d=2)[:, hd, :]
                b = q.dve(op(nc.vector.tensor_tensor, col.ap[:, 2:4], col.ap[:, 0:2], f, ALU.subtract), m, f_ready)
                b = q.dve(op(nc.vector.tensor_scalar, col.ap[:, 2:4], col.ap[:, 2:4], 80.0, None, ALU.min), b)
                b = q.act(op(nc.scalar.activation, col.ap[:, 2:4], col.ap[:, 2:4], ACT.Exp), b)
                for d in range(2):
                    w = q.dve(op(nc.vector.scalar_tensor_tensor, pair[d].ap[:, 0:n], bank.ap[:, 0:n], HD ** -0.5, pair[d].ap[:, 0:n], ALU.mult, ALU.mult,
                        accum_out=col.ap[:, 4 + d:5 + d]), s, exps[d])
                bank.free_after(w)
                c = q.dve(op(nc.vector.scalar_tensor_tensor, col.ap[:, 6:8], col.ap[:, 4:6], -1.0, col.ap[:, 4:6], ALU.mult, ALU.max), w)
                c = q.dve(op(nc.vector.tensor_tensor, col.ap[:, 6:8], col.ap[:, 6:8], col.ap[:, 2:4], ALU.max), c, b)
                c = q.dve(op(nc.vector.reciprocal, col.ap[:, 6:8], col.ap[:, 6:8]), c)
                out = self.mix_pair(pair, n, col.ap[:, 6:8], [c])
                col.free_after(out)
                pair[1].free_after(out)
                last_dve[0] = a
                return pair[0], out

            last_dve = [None]

            def turn(qt, got, hd=hd):
                w, ready = got
                done, copy = self.transpose_weights(w.ap, qt, n_keys(qt), w_t, ready, wt_free[hd % 2])
                w.free_after(done)
                copies.append(copy)

            self.in_order(range(TT), weights, turn)
            for d in range(2):
                self.bank[6 + d].free_after(last_dve[0])
            bank, done = self.weigh_values(lambda kt, hd=hd: vals[:, kt, 512 + hd * P:512 + (hd + 1) * P], w_t, copies + tm)
            wt_free[hd % 2] = done
            o = q.act(op(nc.scalar.activation, self.h[:, 4 + hd, :], bank.ap[:, :], ACT.Identity), done, h_free)
            bank.free_after(o)
            r = self.inverse_rms([self.h[:, 4 + hd, :]], P, RMS_EPS, slice(0, T), o)
            y = q.dve(op(nc.vector.scalar_tensor_tensor, self.h[:, 4 + hd, :], self.h[:, 4 + hd, :], self.S("ml_norm_g", hd, 1), self.rstd[:, 0:T], ALU.mult, ALU.mult), r)
            self.rstd_free = [y]
            y = q.dve(op(nc.vector.tensor_tensor, self.h[:, 4 + hd, :], self.h[:, 4 + hd, :], self.big[:, OP0 + hd, :], ALU.mult), y, og)
        self.ring = range(8)
        self.big_free = [done, y, *wt_free]
        self.h_ready = [y]

    def forget_sums(self, rows, ready):
        q, nc = self.q, self.nc
        a = q.act(op(nc.scalar.activation, rows(2), rows(1), ACT.Abs), ready)
        a = q.act(op(nc.scalar.activation, rows(2), rows(2), ACT.Exp, scale=-1.0), a)
        a = q.act(op(nc.scalar.activation, rows(2), rows(2), ACT.Ln, bias=1.0), a)
        lf = q.dve(op(nc.vector.scalar_tensor_tensor, rows(1), rows(1), 0.0, rows(2), ALU.min, ALU.subtract), a)
        one = self.C("ones")[0:8, 0:1].broadcast_to([8, T])
        s = q.dve(op(nc.vector.tensor_tensor_scan, rows(3), one, rows(1), 0.0, ALU.mult, ALU.add), lf)
        tot = self.neg_lam[0:8, 2:3]
        t = q.dve(op(nc.vector.tensor_tensor, tot, rows(3)[:, NC_TOK - 1:NC_TOK], rows(3)[:, T - 1:T], ALU.add), s)
        b = q.dve(op(nc.vector.tensor_tensor, rows(1), rows(1), rows(3), ALU.subtract), s)
        isb, isf = self.C("is_bwd", 8), self.C("is_fwd", 8)
        b1 = q.dve(op(nc.vector.tensor_scalar, rows(1)[:, CTX], rows(1)[:, CTX], rows(3)[:, NC_TOK - 1:NC_TOK], isb, ALU.add, ALU.mult), b)
        b2 = q.dve(op(nc.vector.tensor_scalar, rows(1)[:, LAT], rows(1)[:, LAT], tot, isb, ALU.add, ALU.mult), b, t)
        f = q.dve(op(nc.vector.scalar_tensor_tensor, rows(1), rows(3), isf, rows(1), ALU.mult, ALU.add), b1, b2)
        g = q.dve(op(nc.vector.tensor_tensor, rows(0), rows(0), rows(1), ALU.subtract), f)
        bank = self.next_bank()
        free = bank.free(self.q.loop_now)
        for tt in range(TT):
            done = q.pe(op(nc.tensor.transpose, bank.ap[:, tt * 8:(tt + 1) * 8], rows(1)[:, tt * P:(tt + 1) * P], self.C("ident")[0:8, 0:8]), f, free)
        c = q.dve(op(nc.vector.tensor_copy, self.fcol[:, :], bank.ap[:, 0:TT * 8]), done)
        bank.free_after(c)
        return g, c

    def diff_lambda(self):
        q, nc = self.q, self.nc
        l = lambda j: self.S("lambda", j * HD, HD)
        col = self.next_cols()
        free = col.free(self.q.loop_now)
        tmp = self.next_temp()
        tfree = tmp.free(self.q.loop_now)
        for j in range(2):
            a = q.dve(op(nc.vector.tensor_tensor, tmp.ap[:, j * HD:(j + 1) * HD], l(2 * j), l(2 * j + 1), ALU.mult), tfree, self.ready)
            a = q.dve(op(nc.vector.tensor_reduce, col.ap[:, j:j + 1], tmp.ap[:, j * HD:(j + 1) * HD], AX.X, ALU.add), a, free)
        tmp.free_after(a)
        a = q.act(op(nc.scalar.activation, col.ap[:, 2:4], col.ap[:, 0:2], ACT.Exp), a)
        a = q.dve(op(nc.vector.tensor_tensor, col.ap[:, 4:5], col.ap[:, 3:4], col.ap[:, 2:3], ALU.subtract), a)
        b = q.dve(op(nc.vector.tensor_scalar, self.neg_lam[:, 0:1], col.ap[:, 4:5], -LAM_INIT, None, ALU.add), a)
        col.free_after(b)
        return q.dve(op(nc.vector.tensor_scalar, self.neg_lam[:, 1:2], self.S("diff_norm_g"), 1.0 - LAM_INIT, None, ALU.mult), b)

    def conv_silu(self, first, scratch, ready):
        q, nc = self.q, self.nc
        for j in range(4):
            x, y = self.big[:, first + j, :], self.big[:, scratch + j, :]
            w = lambda tap, j=j: self.S("conv_w", 4 * tap + j, 1)
            a = q.act(op(nc.scalar.activation, y, x, ACT.Identity, scale=w(1), bias=self.S("conv_b", j, 1)), ready, self.big_free)
            for s, c in STREAMS:
                lo, hi = c.start, c.stop
                a = q.dve(op(nc.vector.scalar_tensor_tensor, y[:, lo + 1:hi], x[:, lo:hi - 1], w(0), y[:, lo + 1:hi], ALU.mult, ALU.add), a)
                a = q.dve(op(nc.vector.scalar_tensor_tensor, y[:, lo:hi - 1], x[:, lo + 1:hi], w(2), y[:, lo:hi - 1], ALU.mult, ALU.add), a)
            a = q.act(op(nc.scalar.activation, x, y, ACT.Silu), a)
        return a

    def odd_mixer(self):
        q, nc = self.q, self.nc
        src = lambda k, lo=0: self.h[:, k, lo:T]
        Q0, K0, R0, V0, W0 = 0, 4, 8, 16, 24
        fm, _ = self.project_fm("odd_fm", 8, 0, src, self.h_ready)
        vals, tm, _ = self.project_tm("odd_tm", 4, V0, src, self.h_ready)
        buf, loaded = self.load_slab("odd_rank", lambda i: 0, 8 * 32)
        for d in range(2):
            bank = self.next_bank()
            done = self.matmuls(bank.ap[0:16, :], [
                (buf.ap[:, k * 32 + 16 * d:k * 32 + 16 * d + 16], src(k)) for k in range(DT)],
                loaded, self.h_ready, bank.free(self.q.loop_now))
            rank = q.act(op(nc.scalar.activation, self.rows[:, d, :], bank.ap[0:16, :], ACT.Identity), done)
            bank.free_after(rank)
        buf.free_after(done)
        h_free = done
        k = self.slab_at % W_SLOTS
        self.slab_at += 1
        gate_w = self.slab[k]
        gate_loaded = q.dma(op(nc.sync.dma_start, gate_w.ap[0:16, 0:D], self.w["odd_gate"][0, :, :]),
                            self.slab_sem[k], gate_w.free(self.q.loop_now))
        for j in range(8):
            swish = q.act(op(nc.scalar.activation, self.big[:, R0 + j, LAT], self.big[:, R0 + j, LAT], ACT.Silu), fm)

        n_chunks, L = NX_TOK // GLA_CHUNK, GLA_CHUNK
        self.ring = range(7)
        self.bank_at = 0
        scratch_free = [self.big_free, self.big_free]
        for hd in range(4):
            o_bank = self.bank[7]
            o_free = o_bank.free(self.q.loop_now)
            first = True
            for d in range(2):
                la, cum, incl, excl = (self.big[:, W0 + 4 * d + n, :] for n in range(4))
                bank = self.next_bank()
                z = self.matmuls(bank.ap[:, :], [(gate_w.ap[0:16, d * 512 + hd * P:d * 512 + (hd + 1) * P],
                                                  self.rows[:, d, :])], rank, gate_loaded, bank.free(self.q.loop_now))
                bias = self.S("gla_b", 4 * d + hd, 1)
                a = self._biased(la, bank, bias, z, scratch_free[d])
                bank.free_after(a)
                a = self._log_sigmoid(la, cum, a)
                s = self._scan(cum, la, a)
                e1 = self._rest(excl, cum, s, n_chunks, L)
                if d == 0:
                    inc_ap, exc_ap = cum, excl
                    inc_ready = exc_ready = e1
                else:
                    inc_ap, exc_ap = excl, incl
                    inc_ready, exc_ready = self._backward_sums(excl, incl, cum, la, e1)
                qk, kd = self.temp[d], self.temp[2 + d]
                k_t, smat, a_t, col = self.gla_kt[d], self.gla_s[d], self.gla_at[d], self.next_cols()
                qk_ready, kd_ready, dec = self._gla_factors(hd, qk, kd, col, inc_ap, exc_ap, cum, inc_ready, exc_ready, s, fm)
                scratch_free[d] = [kd_ready, dec, qk_ready]
                bank = self.next_bank()
                free = bank.free(self.q.loop_now)
                for tt in range(TT):
                    done = q.pe(op(nc.tensor.transpose, bank.ap[:, tt * P:(tt + 1) * P], kd.ap[:, tt * P:(tt + 1) * P], self.C("ident")),
                        kd_ready, free, signal=(tt == TT - 1))
                kd.free_after(done)
                kt_ready = q.act(op(nc.scalar.activation, k_t.ap[:, :], bank.ap[:, :], ACT.Identity),
                                 done, k_t.free(self.q.loop_now))
                bank.free_after(kt_ready)
                v = lambda tt, lo, n, p0=0, pn=P, hd=hd: vals[p0:p0 + pn, tt, hd * 256 + lo:hd * 256 + lo + n]
                bank = self.next_bank()
                st = self.matmuls(bank.ap[:, 0:256], [(k_t.ap[:, tt * P:(tt + 1) * P], v(tt, 0, 256)) for tt in range(2)],
                                  kt_ready, tm, bank.free(self.q.loop_now))
                s_ready = q.dve(op(nc.vector.tensor_copy, smat.ap[:, :], bank.ap[:, 0:256]),
                                st, smat.free(self.q.loop_now))
                bank.free_after(s_ready)
                at_free = a_t.free(self.q.loop_now)
                for tile in range(2):
                    bank = self.next_bank()
                    c = slice(tile * P, (tile + 1) * P)
                    sc = self.matmuls(bank.ap[:, 0:P], [(qk.ap[:, 256 + tile * P:256 + (tile + 1) * P], qk.ap[:, c])],
                                      qk_ready, bank.free(self.q.loop_now))
                    at_ready = q.dve(op(nc.vector.tensor_tensor, a_t.ap[:, c], bank.ap[:, 0:P], self.C(f"gla_mask{d}"), ALU.mult), sc, at_free)
                    bank.free_after(at_ready)
                    for et in range(2):
                        done = self._acc(o_bank.ap[:, et * 256 + tile * P:et * 256 + (tile + 1) * P],
                                         v(2 + tile, et * P, P), a_t.ap[:, c], first, at_ready, tm, o_free)
                        first = False
                a_t.free_after(done)
                order = range(n_chunks) if d == 0 else range(n_chunks - 1, -1, -1)
                for n, c in enumerate(order):
                    for et in range(2):
                        read = self._acc(o_bank.ap[:, et * 256 + c * L:et * 256 + (c + 1) * L],
                                         smat.ap[:, et * P:(et + 1) * P], qk.ap[:, c * L:(c + 1) * L], False, s_ready)
                    if n == n_chunks - 1:
                        break
                    tt, p0 = 2 + c // 2, (c % 2) * L
                    bank = self.next_bank()
                    up = self.matmuls(bank.ap[:, 0:256], [(k_t.ap[p0:p0 + L, tt * P:(tt + 1) * P], v(tt, 0, 256, p0, L))],
                                      kt_ready, bank.free(self.q.loop_now))
                    s_ready = q.dve(op(nc.vector.scalar_tensor_tensor, smat.ap[:, :], smat.ap[:, :], col.ap[:, c:c + 1], bank.ap[:, 0:256], ALU.mult, ALU.add), up, read, dec)
                    bank.free_after(s_ready)
                qk.free_after(read)
                smat.free_after(read)
                k_t.free_after(read)
                col.free_after(s_ready)
            for et in range(2):
                o = q.act(op(nc.scalar.activation, self.h[:, 2 * hd + et, LAT], o_bank.ap[:, et * 256:(et + 1) * 256], ACT.Identity), read, h_free)
            o_bank.free_after(o)
            r = self.inverse_rms([self.h[:, 2 * hd + et, LAT] for et in range(2)], 256, RMS_EPS, LAT, o)
            for et in range(2):
                y = q.dve(op(nc.vector.scalar_tensor_tensor, self.h[:, 2 * hd + et, LAT], self.h[:, 2 * hd + et, LAT], self.S("gla_norm_g", et, 1),
                    self.rstd[:, 0:NX_TOK], ALU.mult, ALU.mult), r)
                y = q.dve(op(nc.vector.tensor_tensor, self.h[:, 2 * hd + et, LAT], self.h[:, 2 * hd + et, LAT], self.big[:, R0 + 2 * hd + et, LAT], ALU.mult),
                    y, swish)
            self.rstd_free = [y]
        gate_w.free_after(z)
        self.ring = range(8)
        self.big_free = [done, read, y]
        self.h_ready = [y]

    def _acc(self, out, a, b, start, *waits):
        return self.q.pe(op(self.nc.tensor.matmul, out, a, b, start=start, stop=True, skip_group_check=True), *waits)

    def _biased(self, out, bank, bias, *waits):
        return self.q.act(op(self.nc.scalar.activation, out, bank.ap[:, :], ACT.Identity, bias=bias), *waits)

    def _log_sigmoid(self, z, tmp, ready):
        q, nc = self.q, self.nc
        a = q.act(op(nc.scalar.activation, tmp, z, ACT.Abs), ready)
        a = q.act(op(nc.scalar.activation, tmp, tmp, ACT.Exp, scale=-1.0), a)
        a = q.act(op(nc.scalar.activation, tmp, tmp, ACT.Ln, bias=1.0), a)
        return q.dve(op(nc.vector.scalar_tensor_tensor, z, z, 0.0, tmp, ALU.min, ALU.subtract), a)

    def _scan(self, out, la, ready):
        return self.q.dve(op(self.nc.vector.tensor_tensor_scan, out, self.C("gla_carry"), la, 0.0, ALU.mult, ALU.add), ready)

    def _rest(self, out, cum, ready, n_chunks, L):
        q, nc = self.q, self.nc
        a = q.dve(op(nc.vector.tensor_scalar, out[:, CTX], cum[:, CTX], -1.0, cum[:, NC_TOK - 1:NC_TOK], ALU.mult, ALU.add), ready)
        by = lambda ap: ap[:, LAT].rearrange("p (c l) -> p c l", l=L)
        return q.dve(op(nc.vector.tensor_tensor, by(out), by(cum)[:, :, L - 1:L].broadcast_to([P, n_chunks, L]), by(cum), ALU.subtract), ready)

    def _backward_sums(self, rest, excl, cum, la, ready):
        q, nc = self.q, self.nc
        a = q.pool(op(nc.gpsimd.tensor_tensor, rest, rest, la, ALU.add), ready)
        b = q.dve(op(nc.vector.tensor_tensor, excl, cum, la, ALU.subtract), ready)
        return a, b

    def _gla_factors(self, hd, qk, kd, col, incl, excl, cum, inc_ready, exc_ready, scan_ready, proj):
        q, nc = self.q, self.nc
        inv_tau = 1.0 / 16.0
        qh, kh = self.big[:, hd, LAT], self.big[:, 4 + hd, :]
        free = qk.free(self.q.loop_now)
        a = q.act(op(nc.scalar.activation, qk.ap[:, 0:256], incl[:, LAT], ACT.Exp, scale=inv_tau), inc_ready, free)
        b = q.act(op(nc.scalar.activation, qk.ap[:, 256:512], incl[:, LAT], ACT.Exp, scale=-inv_tau), inc_ready)
        c = q.act(op(nc.scalar.activation, kd.ap[:, :], excl, ACT.Exp, scale=inv_tau), exc_ready, kd.free(self.q.loop_now))
        ends = cum[:, LAT].rearrange("p (c l) -> p c l", l=GLA_CHUNK)[:, :, GLA_CHUNK - 1]
        dec = q.act(op(nc.scalar.activation, col.ap[:, 0:4], ends, ACT.Exp, scale=inv_tau), scan_ready, col.free(self.q.loop_now))
        a = q.dve(op(nc.vector.scalar_tensor_tensor, qk.ap[:, 0:256], qk.ap[:, 0:256], 128 ** -0.5, qh, ALU.mult, ALU.mult), a, proj)
        b = q.dve(op(nc.vector.tensor_tensor, qk.ap[:, 256:512], qk.ap[:, 256:512], kh[:, LAT], ALU.mult), b, proj)
        c = q.pool(op(nc.gpsimd.tensor_tensor, kd.ap[:, :], kd.ap[:, :], kh, ALU.mult), c, proj)
        return b, c, dec

    def final_norm(self):
        q, nc = self.q, self.nc
        r = self.inverse_rms([self.x[:, k, LAT] for k in range(DT)], D, RMS_EPS, LAT, self.x_ready)
        for k in range(DT):
            a = q.dve(op(nc.vector.scalar_tensor_tensor, self.x[:, k, LAT], self.x[:, k, LAT], self.S("final_g", k, 1), self.rstd[:, 0:NX_TOK], ALU.mult, ALU.mult), r)
        self.rstd_free = [a]
        c = q.dma(op(nc.sync.dma_start, self.x[:, :, CTX], self.w["ctx_2"]), self.side_sem, r)
        self.x_ready = [a, c]

    def modulate(self, streams):
        q, nc = self.q, self.nc
        shift = self.shift
        for k in range(DT):
            for s, c in streams:
                if (k + s) % 2:
                    a = q.act(op(nc.scalar.activation, self.h[:, k, c], self.x[:, k, c], ACT.Identity, scale=self.scales[:, k, s:s + 1], bias=shift(k, s)),
                        self.x_ready, self.scales_ready, self.h_free)
                else:
                    b = q.dve(op(nc.vector.tensor_scalar, self.h[:, k, c], self.x[:, k, c], self.scales[:, k, s:s + 1], shift(k, s), ALU.mult, ALU.add),
                        self.x_ready, self.scales_ready, self.h_free)
        self.h_ready = [a, b]
        self.scales_free = [a, b]
        self.mods_free = self.mods_free + [a, b]

    def layer_norm(self, streams, layer, which):
        q, nc = self.q, self.nc
        cols = slice(streams[0][1].start, T)
        n = cols.stop - cols.start
        bank = self.next_bank()
        total = self.matmuls(bank.ap[:, 0:n], [(self.C("ones"), self.x[:, k, cols]) for k in range(DT)],
                             self.x_ready, bank.free(self.q.loop_now))
        for k in range(DT):
            a = q.dve(op(nc.vector.scalar_tensor_tensor, self.x[:, k, cols], bank.ap[:, 0:n], -1.0 / D, self.x[:, k, cols], ALU.mult, ALU.add), total)
        bank.free_after(a)
        r = self.inverse_rms([self.x[:, k, cols] for k in range(DT)], D, LN_EPS, cols, a)
        g = lambda k: self.S("ln", (4 * layer + 2 * which) * DT + k, 1)
        b = lambda k: self.S("ln", (4 * layer + 2 * which + 1) * DT + k, 1)
        for k in range(DT):
            a = q.dve(op(nc.vector.scalar_tensor_tensor, self.x[:, k, cols], self.x[:, k, cols], g(k), self.rstd[:, 0:n], ALU.mult, ALU.mult), r)
            c = q.act(op(nc.scalar.activation, self.x[:, k, cols], self.x[:, k, cols], ACT.Identity, bias=b(k)), a)
        self.rstd_free = [a]
        self.x_ready = [c]

    def softmax_scores(self, pairs, n, temp, col, ready):
        q, nc = self.q, self.nc
        bank = self.next_bank()
        s = self.matmuls(bank.ap[:, 0:n], pairs, ready, bank.free(self.q.loop_now))
        m = q.dve(op(nc.vector.tensor_reduce, col.ap[:, 0:1], bank.ap[:, 0:n], AX.X, ALU.max, negate=True),
                  s, col.free(self.q.loop_now))
        e = q.act(op(nc.scalar.activation, temp.ap[:, 0:n], bank.ap[:, 0:n], ACT.Exp, bias=col.ap[:, 0:1],
                                                 accum_out=col.ap[:, 1:2]), m, temp.free(self.q.loop_now))
        bank.free_after(e)
        return self.normalise(n, temp, col, e)

    def normalise(self, n, temp, col, e):
        q, nc = self.q, self.nc
        r = q.dve(op(nc.vector.reciprocal, col.ap[:, 2:3], col.ap[:, 1:2]), e)
        w = q.pool(op(nc.gpsimd.tensor_scalar, temp.ap[:, 0:n], temp.ap[:, 0:n], col.ap[:, 2:3], None, ALU.mult), r)
        col.free_after(w)
        return w

    def mla_mixer(self):
        q, nc = self.q, self.nc
        src = lambda k, lo=0: self.h[:, k, lo:T]
        QC, KC, KPE, QN, QPE, KN, WT = 0, 4, 6, 8, 16, 20, (0, 28)
        heads, scale = 8, (128 + 64) ** -0.5
        qc, _ = self.project_fm("mla_dq", 2, QC, src, self.h_ready)
        kc, _ = self.project_fm("mla_dkv", 1, KC, src, self.h_ready)
        buf, loaded = self.load_slab("mla_kpe", lambda i: 0, 8 * P)
        bank = self.next_bank()
        h_done = self.matmuls(bank.ap[:, :], [(buf.ap[:, k * P:(k + 1) * P], src(k)) for k in range(DT)],
                              loaded, self.h_ready, bank.free(self.q.loop_now))
        buf.free_after(h_done)
        t = q.act(op(nc.scalar.activation, self.big[:, KPE, :], bank.ap[:, :], ACT.Identity), h_done, self.big_free)
        bank.free_after(t)
        kpe = self.rope(KPE, [t])
        for first, n, dim, gain, ready in ((QC, 4, 512, "q_norm", qc), (KC, 2, 256, "kv_norm", kc)):
            r = self.inverse_rms([self.big[:, first + k, :] for k in range(n)], dim, RMS_EPS, slice(0, T), ready)
            for k in range(n):
                a = q.dve(op(nc.vector.scalar_tensor_tensor, self.big[:, first + k, :], self.big[:, first + k, :], self.S(gain, k, 1), self.rstd[:, :],
                    ALU.mult, ALU.mult), r)
            self.rstd_free = [a]
        normed = a
        q_parts = []
        for s in range(4):
            buf, loaded = self.load_slab("mla_uq", lambda i, s=s: s, 4 * 384)
            for t, tile in enumerate((QN + 2 * s, QN + 2 * s + 1, QPE + s)):
                bank = self.next_bank()
                done = self.matmuls(bank.ap[:, :], [
                    (buf.ap[:, k * 384 + t * P:k * 384 + (t + 1) * P], self.big[:, QC + k, :]) for k in range(4)],
                    loaded, normed, bank.free(self.q.loop_now))
                c = q.act(op(nc.scalar.activation, self.big[:, tile, :], bank.ap[:, :], ACT.Identity, scale=scale), done, self.big_free)
                bank.free_after(c)
            buf.free_after(done)
            q_parts += [self.rope(QPE + s, [c]), c]
        wt_free = [[done], self.big_free]
        buf, loaded = self.load_slab("mla_ukv", lambda i: 0, SLAB)
        for t in range(heads):
            bank = self.next_bank()
            done = self.matmuls(bank.ap[:, :], [
                (buf.ap[:, k * 1024 + t * P:k * 1024 + (t + 1) * P], self.big[:, KC + k, :]) for k in range(2)],
                loaded, normed, bank.free(self.q.loop_now))
            kn = q.dve(op(nc.vector.tensor_copy, self.big[:, KN + t, :], bank.ap[:, :]), done, self.big_free)
            bank.free_after(kn)
        buf.free_after(done)
        vals = self.h[:, :, :].rearrange("p a n -> p (a n)").rearrange("p (t n) -> p t n", t=TT)
        buf, loaded = self.load_slab("mla_ukv", lambda i: 1, SLAB)
        for tt in range(TT):
            for half in range(2):
                bank = self.next_bank()
                done = self.matmuls(bank.ap[:, :], [
                    (self.big[:, KC + k, tt * P:(tt + 1) * P], buf.ap[:, k * 1024 + half * 512:k * 1024 + (half + 1) * 512])
                    for k in range(2)], loaded, normed, bank.free(self.q.loop_now))
                v = q.act(op(nc.scalar.activation, vals[:, tt, half * 512:(half + 1) * 512], bank.ap[:, :], ACT.Identity), done, h_done)
                bank.free_after(v)
        buf.free_after(done)
        for hd in range(heads):
            w_t = self.big[:, WT[hd % 2]:WT[hd % 2] + TT, :]
            copies, base = [], HD * (hd % 2)
            n_keys = lambda qt: NC_TOK if qt < NC_TOK // P else T

            def scores(qt, hd=hd, base=base):
                n, c = n_keys(qt), slice(qt * P, (qt + 1) * P)
                temp, col = self.temp[qt % 4], self.next_cols()
                return temp, self.softmax_scores([
                    (self.big[:, QN + hd, c], self.big[:, KN + hd, 0:n]),
                    (self.big[base:base + HD, QPE + hd // 2, c], self.big[base:base + HD, KPE, 0:n])],
                    n, temp, col, [kpe, kn, *q_parts])

            def turn(qt, got, hd=hd):
                w, ready = got
                done, copy = self.transpose_weights(w.ap, qt, n_keys(qt), w_t, ready, wt_free[hd % 2])
                w.free_after(done)
                copies.append(copy)

            self.in_order(range(TT), scores, turn)
            bank, done = self.weigh_values(lambda kt, hd=hd: vals[:, kt, hd * P:(hd + 1) * P], w_t, copies + [v])
            wt_free[hd % 2] = [done]
            o = q.act(op(nc.scalar.activation, self.big[:, QN + hd, :], bank.ap[:, :], ACT.Identity), done)
            bank.free_after(o)
        self.h_free = [done]
        d = self.add_branch("mla_out", 4, "cols", lambda k, lo: self.big[:, QN + k, lo:T], o, STREAMS, alpha=ALPHA)
        self.big_free = [d]

    def na_mixer(self):
        q, nc = self.q, self.nc
        src = lambda k, lo=0: self.h[:, k, lo:T]
        Q0, K0, V0, WT = 0, 8, 16, (24, 28)
        heads, scale = 16, HD ** -0.5
        fq, _ = self.project_fm("na_fm", 4, Q0, src, self.h_ready, bias=self.S("na_b", 0, 8), lo=NC_TOK)
        fk, _ = self.project_fm("na_fm", 4, K0, src, self.h_ready, bias=self.S("na_b", 8, 8), slab0=4)
        vals, tm, h_free = self.project_tm("na_tm", 4, V0, src, self.h_ready, bias=self.S("na_bv"))
        wt_free = [self.big_free, self.big_free]
        rel = NX_TOK // GRID_W + 2
        rpb = self.w["na_rpb"]
        n_r, n_c = 15, 31
        out = None
        for hd in range(heads):
            base, tile = HD * (hd % 2), hd // 2
            w_t = self.big[:, WT[hd % 2]:WT[hd % 2] + TT, :]
            copies = []
            raw, b_buf, n_b = self.gla_kt[hd % 2], self.na_bias[hd % 2], rel * GRID_W
            free = raw.free(self.q.loop_now)
            for r2 in range(2):
                at = bass.AP(rpb.tensor, hd * n_r * n_c + (4 + r2) * n_c + 15 - (GRID_W - 1), [[1, GRID_W], [n_c, rel], [1, GRID_W]])
                got = q.dma(op(nc.sync.dma_start, raw.ap[r2 * GRID_W:(r2 + 1) * GRID_W, 0:n_b].rearrange("p (m n) -> p m n", n=GRID_W), at),
                    self.bias_sem[hd % 2], free)
            mask = self.C("na_mask")[:, 0:GRID_W].rearrange("p (o n) -> p o n", o=1).broadcast_to([P, rel, GRID_W])
            bias = b_buf.ap[:, :]
            biased = q.pool(op(nc.gpsimd.tensor_copy, bias, raw.ap[:, n_b - 1::-1]), got, b_buf.free(self.q.loop_now))
            raw.free_after(biased)
            biased = q.pool(op(nc.gpsimd.tensor_tensor, bias.rearrange("p (m n) -> p m n", n=GRID_W), bias.rearrange("p (m n) -> p m n", n=GRID_W), mask, ALU.add), biased)

            def scores(qt, base=base, tile=tile, bias=bias, biased=biased):
                temp, col, bank = self.temp[qt % 4], self.next_cols(), self.next_bank()
                s = self.matmuls(bank.ap[:, :], [(
                    self.big[base:base + HD, Q0 + tile, qt * P:(qt + 1) * P], self.big[base:base + HD, K0 + tile, :])],
                    fq, fk, bank.free(self.q.loop_now))
                a = q.act(op(nc.scalar.activation, temp.ap[:, CTX], bank.ap[:, CTX], ACT.Identity, scale=scale), s, temp.free(self.q.loop_now))
                at = (2 - 2 * (qt - 2)) * GRID_W
                b = q.dve(op(nc.vector.scalar_tensor_tensor, temp.ap[:, LAT], bank.ap[:, LAT], scale, bias[:, at:at + NX_TOK], ALU.mult, ALU.add), s, biased, a)
                bank.free_after(b)
                m = q.dve(op(nc.vector.tensor_reduce, col.ap[:, 0:1], temp.ap[:, :], AX.X, ALU.max, negate=True),
                          a, b, col.free(self.q.loop_now))
                e = q.act(op(nc.scalar.activation, temp.ap[:, :], temp.ap[:, :], ACT.Exp, bias=col.ap[:, 0:1],
                                                         accum_out=col.ap[:, 1:2]), m)
                used[0] = b
                return temp, self.normalise(T, temp, col, e)

            used = [None]

            def turn(qt, got, hd=hd, w_t=w_t):
                w, ready = got
                done, copy = self.transpose_weights(w.ap, qt, T, w_t, ready, wt_free[hd % 2])
                w.free_after(done)
                copies.append(copy)

            self.in_order(range(2, TT), scores, turn)
            b_buf.free_after(used[0])
            bank = self.next_bank()
            done = self.matmuls(bank.ap[base:base + HD, 0:NX_TOK], [
                (vals[:, kt, hd * HD:(hd + 1) * HD], w_t[:, kt, LAT]) for kt in range(TT)], copies, tm, bank.free(self.q.loop_now))
            wt_free[hd % 2] = [done]
            out = q.act(op(nc.scalar.activation, self.h[base:base + HD, tile, LAT], bank.ap[base:base + HD, 0:NX_TOK], ACT.Identity), done, h_free)
            bank.free_after(out)
        self.h_ready = [out]
        d = self.add_branch("na_out", 4, "cols", lambda k, lo: self.h[:, k, lo:T], out, STREAMS[1:], alpha=ALPHA)
        self.big_free = self.h_free = [d]


def run_stages(m):
    BOTH, LATENT = STREAMS, STREAMS[1:]
    g = lambda l, n: m.S("norm_g", (3 * l + n) * DT, DT)
    m.load_inputs()
    m.modulation("ada0", 0, 36, "ada_b", 0)
    m.scale_and_gate(0, 1, 2, g(0, 0), True)
    m.ada_norm(BOTH)
    m.swiglu(0, 0, BOTH)
    m.scale_and_gate(3, 4, 5, g(0, 1), False)
    m.ada_norm(BOTH)
    m.even_mixer()
    m.big_free = m.big_free + [m.add_branch("even_out", 4, "cols", lambda k, lo: m.h[:, k, lo:T], m.h_ready, BOTH)]
    m.h_free = m.big_free[-1:]
    m.scale_and_gate(6, 7, 8, g(0, 2), True)
    m.ada_norm(BOTH)
    m.swiglu(0, 1, BOTH)

    m.modulation("ada1", 0, 36, "ada_b", 72)
    m.scale_and_gate(0, 1, 2, g(1, 0), True)
    m.ada_norm(BOTH)
    m.swiglu(1, 0, BOTH)
    m.scale_and_gate(3, 4, 5, g(1, 1), False)
    m.ada_norm(BOTH)
    m.odd_mixer()
    m.big_free = m.big_free + [m.add_branch("odd_out", 4, "cols", lambda k, lo: m.h[:, k, lo:T], m.h_ready, LATENT)]
    m.h_free = m.big_free[-1:]
    m.scale_and_gate(6, 7, 8, g(1, 2), True)
    m.ada_norm(LATENT)
    m.swiglu(1, 1, LATENT)
    m.final_norm()

    for l, streams in ((0, BOTH), (1, LATENT)):
        m.modulation(f"ada2{l}", 1, 24, "ada_b_2", 48 * l)
        m.scale_and_gate(0, 1, 2, None, False)
        m.modulate(BOTH)
        (m.mla_mixer, m.na_mixer)[l]()
        m.layer_norm(streams, l, 0)
        m.scale_and_gate(3, 4, 5, None, False)
        m.modulate(streams)
        m.relu_mlp(l, streams)
        m.layer_norm(streams, l, 1)
    m.store_output(m.x[:, :, LAT], m.x_ready)


def build_program(nc, w, out):
    with ExitStack() as stack:
        m = Model(nc, stack, w, out)
        run_stages(m)
        m.q.emit()


def kernel(**inputs):
    import concourse.bacc as bacc
    from concourse.bass_utils import run_bass_kernel_spmd

    arrays = lay_out(inputs)
    nc = bacc.Bacc("TRN2", target_bir_lowering=False, num_devices=1)
    w = {n: nc.dram_tensor(n, a.shape, F32, kind="ExternalInput").ap() for n, a in arrays.items()}
    out = nc.dram_tensor("out", (P, DT, NX_TOK), F32, kind="ExternalOutput").ap()
    build_program(nc, w, out)
    r = run_bass_kernel_spmd(nc, [arrays], core_ids=[0])
    got = r.results[0]["out"]
    return np.ascontiguousarray(got.transpose(2, 1, 0).reshape(1, NX_TOK, D))
```

```python
import math
from contextlib import ExitStack, contextmanager

import numpy as np
import concourse.bass as bass
from concourse import mybir
from concourse.alu_op_type import AluOpType as ALU

F32 = mybir.dt.float32
F32R = mybir.dt.float32r
ACT = mybir.ActivationFunctionType
AX = mybir.AxisListType

P = 128
D = 1024
DT = D // P
NC_TOK = 256
NX_TOK = 256
T = NC_TOK + NX_TOK
TT = T // P
GRID_W = 64
FF = 2816
FT = FF // P
FF2 = 4096
FT2 = FF2 // P
N_MOD1, N_MOD2 = 9, 6
SLAB = 1024
RAW_SLOTS, SPLIT_SLOTS = 6, 3
ADA_SLOTS = 3
HD = 64
RMS_EPS, LN_EPS = 1e-6, 1e-5
LAM_INIT = 0.8 - 0.6 * math.exp(0.0)
ALPHA = (2.0 * 2) ** 0.25
NEG = -1.0e30
CTX, LAT = slice(0, NC_TOK), slice(NC_TOK, T)
STREAMS = ((0, CTX), (1, LAT))
GLA_CHUNK = 64


class Sem:
    def __init__(self, handle, start):
        self.handle, self.count = handle, start


class Loop:

    def __init__(self, n, at):
        self.n, self.at, self.step = n, at, {}


class Event:

    def __init__(self, sem, value, loop):
        self.sem, self.value, self.loop = sem, value, loop


class LastTurn:

    def __init__(self, mark, loop):
        self.mark, self.loop = mark, loop


class Mark:

    def __init__(self):
        self.events, self.in_loop = [], {}

    def set(self, *events):
        self.events = list(events)
        for t in events:
            if t.loop is not None:
                self.in_loop[t.loop] = list(events)

    def get(self, loop):
        waits = list(self.events)
        if loop is not None and not any(t.loop is loop for t in waits):
            waits.append(LastTurn(self, loop))
        return waits


class Slot:

    def __init__(self, ap, low=None):
        self.ap, self.low, self.loaded, self.unused = ap, low, Mark(), Mark()

    def free(self, loop):
        return self.unused.get(loop)

    def free_after(self, *events):
        self.unused.set(*events)


ENGINES = ("tensor", "scalar", "vector", "gpsimd", "sync")
PRIME = 512


def op(build, *args, **kwargs):
    return lambda i: build(*args, **kwargs)


class Queues:
    def __init__(self, nc, stack):
        self.nc, self.stack = nc, stack
        self.queue = {e: [] for e in ENGINES}
        self.sems = []
        self.done = {e: self.sem(f"done_{e}", PRIME) for e in ENGINES if e != "sync"}
        self.loop_now = None

    def sem(self, name, start=0):
        s = Sem(self.stack.enter_context(self.nc.semaphore(name)), start)
        self.sems.append(s)
        return s

    @contextmanager
    def loop(self, n):
        lp = Loop(n, {s: s.count for s in self.sems})
        outer, self.queue = self.queue, {e: [] for e in ENGINES}
        self.loop_now = lp
        yield
        self.loop_now = None
        inner, self.queue = self.queue, outer
        for s in self.sems:
            lp.step[s] = s.count - lp.at.get(s, s.count)
            s.count += (n - 1) * lp.step[s]
        for e in ENGINES:
            if inner[e]:
                self.queue[e].append((lp, inner[e]))

    def add(self, engine, fn, waits, sem, inc):
        flat = []
        for w in waits:
            flat += w if isinstance(w, (list, tuple)) else [w]
        self.queue[engine].append((fn, [w for w in flat if w is not None], sem, inc))
        if sem is None:
            return None
        sem.count += inc
        return Event(sem, sem.count, self.loop_now)

    def pe(self, fn, *waits, signal=True):
        return self.add("tensor", fn, waits, self.done["tensor"] if signal else None, 1)

    def act(self, fn, *waits):
        return self.add("scalar", fn, waits, self.done["scalar"], 1)

    def dve(self, fn, *waits):
        return self.add("vector", fn, waits, self.done["vector"], 1)

    def pool(self, fn, *waits):
        return self.add("gpsimd", fn, waits, self.done["gpsimd"], 1)

    def dma(self, fn, sem, *waits, engine="sync"):
        return self.add(engine, fn, waits, sem, 16)

    def emit(self):
        with self.nc.Block() as block:
            for name in ENGINES:
                self._register(block, name)

    def _register(self, block, name):
        def program(eng):
            if name in self.done:
                eng.sem_inc(self.done[name].handle, PRIME)
            self._run(eng, self.queue[name], None, 0, {})

        {"tensor": block.tensor, "scalar": block.scalar, "vector": block.vector,
         "gpsimd": block.gpsimd, "sync": block.sync}[name](program)

    def _run(self, eng, items, loop, i, seen):
        for item in items:
            if isinstance(item[0], Loop):
                with eng.Fori(0, item[0].n) as j:
                    self._run(eng, item[1], item[0], j, dict(seen))
                continue
            fn, waits, sem, inc = item
            for w in waits:
                for handle, key, base, slope in self._values(w, loop):
                    if seen.get((key, slope), -1) >= base:
                        continue
                    seen[(key, slope)] = base
                    eng.wait_ge(handle, base if slope == 0 else i * slope + base)
            ins = fn(i)
            if sem is not None:
                ins.then_inc(sem.handle, inc)

    def _values(self, w, loop):
        if isinstance(w, LastTurn):
            out = []
            for t in w.mark.in_loop.get(w.loop, []):
                d = w.loop.step[t.sem]
                if t.value - d < 1:
                    raise ValueError("a loop's wait below one: raise PRIME")
                out.append((t.sem.handle, t.sem, t.value - d, d))
            return out
        if w.loop is None:
            return [(w.sem.handle, w.sem, w.value, 0)]
        d = w.loop.step[w.sem]
        if w.loop is loop:
            return [(w.sem.handle, w.sem, w.value, d)]
        return [(w.sem.handle, w.sem, w.value + (w.loop.n - 1) * d, 0)]


def constant_table():
    parts, at, n = [], {}, 0

    def put(name, a):
        nonlocal n
        full = np.zeros((P, a.shape[1]), np.float32)
        full[: a.shape[0]] = a
        parts.append(full)
        at[name] = (n, n + a.shape[1])
        n += a.shape[1]

    p = np.arange(P)
    put("ident", np.eye(P))
    put("ones", np.ones((P, P)))
    partner = np.where(p % 32 < 16, p + 16, p - 16)
    put("swap", (p[:, None] == partner[None, :]).astype(np.float32))
    pos = np.arange(NX_TOK)
    inv = (10000.0 ** (-np.arange(16, dtype=np.float32) * 2.0 / 32)).astype(np.float32)
    place = np.where((p % HD < 32)[:, None], pos[None, :] // GRID_W, pos[None, :] % GRID_W).astype(np.float32)
    ang = (place * inv[p % 16][:, None]).astype(np.float32)
    put("cos", np.cos(ang))
    put("sin", np.sin(ang) * np.where(p % 32 < 16, -1.0, 1.0)[:, None])
    s = np.arange(NX_TOK)[None, :]
    masks = []
    for d in range(2):
        for tile in range(2):
            t = tile * P + p[:, None]
            masks += [np.zeros((P, NC_TOK)), np.where(s <= t if d == 0 else s >= t, 0.0, NEG)]
    put("is_fwd", (np.arange(8) < 4)[:, None].astype(np.float32))
    put("is_bwd", (np.arange(8) >= 4)[:, None].astype(np.float32))
    carry = np.ones(T)
    carry[0] = 0.0
    carry[NC_TOK::GLA_CHUNK] = 0.0
    put("gla_carry", np.tile(carry, (P, 1)))
    blk = p[:, None] // GLA_CHUNK == p[None, :] // GLA_CHUNK
    put("gla_mask0", (blk & (p[:, None] <= p[None, :])).astype(np.float32))
    put("gla_mask1", (blk & (p[:, None] >= p[None, :])).astype(np.float32))
    c = np.arange(GRID_W)
    start = np.clip(c - 8, 0, GRID_W - 16)
    ok = (c[None, :] >= start[:, None]) & (c[None, :] < start[:, None] + 16)
    put("na_mask", np.where(ok, 0.0, NEG)[p % GRID_W])
    return np.ascontiguousarray(np.concatenate(parts, 1).astype(np.float32)), at, np.concatenate(masks, 1).astype(np.float32)


def columns(v):
    return np.asarray(v).reshape(-1, P).T


SMALL = [("ada_b", 240), ("norm_g", 48), ("final_g", 8), ("diff_norm_g", 1),
         ("ml_norm_g", 4), ("conv_w", 12), ("conv_b", 4), ("gla_b", 8), ("gla_norm_g", 2),
         ("ln", 64), ("q_norm", 4), ("kv_norm", 2), ("na_b", 16), ("lambda", 4 * HD), ("gate_b", 2)]


def small_at():
    at, n = {}, 0
    for name, w in SMALL:
        at[name] = (n, n + w)
        n += w
    return at, n


def small_table(a):
    def flat(x):
        return columns(np.asarray(x).reshape(-1))

    gate = np.zeros((P, 2), np.float32)
    gate[:8] = np.asarray(a["mlstm_gate_b"]).reshape(2, 8).T
    qb = np.asarray(a["na_b_qkv_2"]).reshape(3, D)
    ln = np.stack([np.asarray(a[k]) for k in ("ln1_g_2", "ln1_b_2", "ln2_g_2", "ln2_b_2")], 1)
    parts = dict(
        ada_b=np.concatenate([flat(a["ada_b"]), flat(a["ada_b_2"])], 1), norm_g=flat(a["norm_g"]),
        final_g=flat(a["final_g"]), diff_norm_g=flat(a["diff_norm_g"]), ml_norm_g=flat(a["mlstm_norm_g"]),
        conv_w=flat(a["mlstm_conv_w"]), conv_b=flat(a["mlstm_conv_b"]), gla_b=flat(a["gla_b_gate"]),
        gla_norm_g=flat(a["gla_norm_g"]), ln=flat(ln), q_norm=flat(a["mla_q_norm_2"]), kv_norm=flat(a["mla_kv_norm_2"]),
        na_b=flat(qb[:2]), gate_b=gate,
    )
    parts["lambda"] = np.broadcast_to(np.asarray(a["diff_lambda"]).reshape(-1), (P, 4 * HD))
    return np.ascontiguousarray(np.concatenate([parts[n] for n, _ in SMALL], 1))


def slabs(w, k_tiles):
    K, N = w.shape
    cols = SLAB // k_tiles
    r = w.reshape(K // (P * k_tiles), k_tiles, P, N // cols, cols)
    return r.transpose(3, 0, 2, 1, 4).reshape(-1, P, SLAB)


def padded(w, cols=P):
    out = np.zeros((w.shape[0], cols), w.dtype)
    out[:, : w.shape[1]] = w
    return out


def chunks(first, second, n_first):
    n = len(second) // 2
    return np.concatenate([first.reshape(n, n_first, P, SLAB), second.reshape(n, 2, P, SLAB)], 1).reshape(-1, P, SLAB)


STREAM = [("ffn00", 66), ("even_fm", 18), ("even_tm", 8), ("even_out", 8), ("ffn01", 66),
          ("ffn10", 66), ("odd_fm", 18), ("odd_tm", 8), ("odd_out", 8), ("ffn11", 66),
          ("mla_down", 7), ("mla_uq", 6), ("mla_ukv", 4), ("mla_out", 8), ("mlp0", 64),
          ("na_fm", 16), ("na_tm", 8), ("na_out", 8), ("mlp1", 64)]
N_SLABS = sum(n for _, n in STREAM)


def weight_stream(a):
    f = lambda name: np.asarray(a[name])
    out = {}
    for l in range(2):
        for h in range(2):
            ab = f("ffn_w_in")[l, h].reshape(D, 2, FT, P).transpose(0, 2, 1, 3).reshape(D, 2 * FF)
            out[f"ffn{l}{h}"] = chunks(slabs(ab, 8), f("ffn_w_out")[l, h].reshape(FT, P, D), 4)
        out[f"mlp{l}"] = chunks(slabs(f("mlp_w1_2")[l], 8), f("mlp_w2_2")[l].reshape(FT2, P, D), 2)
    q, k, v, mqk, mv, mo, g = np.split(f("even_w_in")[0], np.cumsum([512] * 6), axis=1)
    out["even_fm"] = slabs(np.concatenate([q, k, mqk, mo, padded(g[:, :8]), padded(g[:, 8:])], 1), 8)
    out["even_tm"] = slabs(np.concatenate([v, mv], 1), 2)
    out["even_out"] = slabs(f("even_w_out")[0], 8)
    q, k, v, r, lr = np.split(f("odd_w_in")[0], np.cumsum([512, 512, 1024, 1024]), axis=1)
    out["odd_fm"] = slabs(np.concatenate([q, k, r, padded(lr[:, :16]), padded(lr[:, 16:])], 1), 8)
    out["odd_tm"] = slabs(v, 2)
    out["odd_out"] = slabs(f("odd_w_out")[0], 8)
    dkv = f("mla_w_dkv_2")[0]
    out["mla_down"] = slabs(np.concatenate([f("mla_w_dq_2")[0], dkv, dkv[:, 256:]], 1), 8)
    uq = f("mla_w_uq_2")[0].reshape(512, 8, 192)
    out["mla_uq"] = slabs(np.concatenate([uq[..., :P].reshape(512, -1), uq[..., P:].reshape(512, -1)], 1), 4)
    ukv = f("mla_w_ukv_2")[0].reshape(256, 8, 2, P).transpose(0, 2, 1, 3).reshape(256, -1)
    out["mla_ukv"] = slabs(ukv, 2)
    out["mla_out"] = slabs(f("mla_w_o_2")[0], 8)
    qkv = f("na_w_qkv_2")[0]
    out["na_fm"] = slabs(qkv[:, : 2 * D], 8)
    out["na_tm"] = slabs(qkv[:, 2 * D:], 2)
    out["na_out"] = slabs(f("na_w_o_2")[0], 8)
    return np.concatenate([out[name] for name, _ in STREAM])


def modulation_stream(a):
    w = [np.asarray(a[n])[l].T.reshape(-1, P, D) for n in ("ada_w", "ada_w_2") for l in range(2)]
    return np.concatenate(w)


def feature_major(x):
    return np.asarray(x).reshape(-1, DT, P).transpose(2, 1, 0)


def lay_out(a):
    x = np.concatenate([feature_major(np.asarray(a["ctx"])[0]), feature_major(np.asarray(a["x"])[0])], 2)
    out = {"weights": weight_stream(a), "ada": modulation_stream(a)}
    out["cond"] = np.stack([np.broadcast_to(np.asarray(a[n]).reshape(D), (P, D)) for n in ("c_ctx", "c", "c_ctx_2", "c_2")], 1)
    out["gla_gate"] = np.ascontiguousarray(np.asarray(a["gla_w_gate"])[0].transpose(1, 0, 2).reshape(16, D))
    out["na_rpb"] = np.ascontiguousarray(np.asarray(a["na_rpb_2"])[0][:, ::-1, ::-1])
    out["na_bv"] = np.ascontiguousarray(np.broadcast_to(np.asarray(a["na_b_qkv_2"])[0, 2 * D:], (P, D)))
    out["tokens"] = np.ascontiguousarray(x)
    out["ctx_2"] = np.ascontiguousarray(feature_major(np.asarray(a["ctx_2"])[0]))
    out["small"] = small_table(a)
    out["constants"], _, masks = constant_table()
    out["ml_masks"] = masks
    return out


class Model:

    def __init__(self, nc, stack, w, out):
        self.nc, self.w, self.out = nc, w, out
        self.stack, self.stage_stack = stack, None
        self.q = Queues(nc, stack)
        self.c_at = constant_table()[1]
        self.s_at, n_small = small_at()
        sb = self.sb
        self.const = sb("const", (P, max(b for _, b in self.c_at.values())))
        self.small = sb("small", (P, n_small))
        self.x = sb("x_res", (P, DT, T))
        self.hh = sb("h_high", (P, DT, T), F32R)
        self.hl = sb("h_low", (P, DT, T), F32R)
        self.mods = sb("mods", (P, 240, 2))
        self.scales = sb("scales", (P, DT, 2))
        self.gates = sb("gates", (P, DT, 2))
        self.rstd = sb("rstd", (P, T))
        self.stat = sb("stat", (P, T))
        self.fcol = sb("fcol", (P, TT * 8))
        self.neg_lam = sb("neg_lam", (P, 4))
        self.cols = [Slot(sb(f"cols{i}", (P, 8))) for i in range(6)]
        self.cols_at = 0
        self.raw = [Slot(sb(f"raw{i}", (P, SLAB))) for i in range(RAW_SLOTS)]
        self.raw_sem = [self.q.sem(f"raw{i}_loaded") for i in range(RAW_SLOTS)]
        self.split = [Slot(sb(f"split_high{i}", (P, SLAB), F32R), sb(f"split_low{i}", (P, SLAB), F32R))
                      for i in range(SPLIT_SLOTS)]
        self.slab_no, self.per_turn = 0, 0
        self.temp = [Slot(sb(f"temp{i}", (P, T))) for i in range(4)]
        self.temp_at = 0
        self.bank = [Slot(stack.enter_context(nc.psum_tensor(f"bank{i}", [P, 512], F32))) for i in range(8)]
        self.bank_at = 0
        self.ring = range(8)
        self.load_sem = self.q.sem("inputs_loaded")
        self.store_sem = self.q.sem("output_stored")
        self.side_sem = self.q.sem("side_loaded")
        self.ada_sem = [self.q.sem(f"ada{i}_loaded") for i in range(ADA_SLOTS)]
        self.bias_sem = [self.q.sem(f"bias{i}_loaded") for i in range(2)]
        self.ada_col = Slot(sb("ada_col", (P, 16, 2)))
        self.ada_no = 0
        self.scales_free, self.gates_free, self.rstd_free, self.h_free, self.x_free = [], [], [], [], []
        self.region_free = []

    def sb(self, name, shape, dtype=F32):
        return (self.stage_stack or self.stack).enter_context(self.nc.sbuf_tensor(f"sb_{name}", list(shape), dtype))

    @contextmanager
    def stage(self):
        with ExitStack() as own:
            self.stage_stack = own
            yield
            self.stage_stack = None

    def C(self, name, rows=P):
        a, b = self.c_at[name]
        return self.const[0:rows, a:b]

    def S(self, name, j=0, n=None):
        a, b = self.s_at[name]
        return self.small[:, a + j:(a + j + n if n else b)]

    def free(self, slot):
        return slot.free(self.q.loop_now)

    def next_bank(self):
        b = self.bank[self.ring[self.bank_at % len(self.ring)]]
        self.bank_at += 1
        return b

    def next_temp(self):
        b = self.temp[self.temp_at % 4]
        self.temp_at += 1
        return b

    def next_cols(self):
        b = self.cols[self.cols_at % len(self.cols)]
        self.cols_at += 1
        return b

    @contextmanager
    def turns(self, n, slabs):
        assert slabs % RAW_SLOTS == 0 and slabs % SPLIT_SLOTS == 0
        start, self.per_turn = self.slab_no, slabs
        with self.q.loop(n):
            yield
            assert self.slab_no == start + slabs
        self.slab_no, self.per_turn = start + n * slabs, 0

    def prefetch(self, s):
        if s >= N_SLABS:
            return
        q, nc, step = self.q, self.nc, self.per_turn
        raw, sem, part = self.raw[s % RAW_SLOTS], self.raw_sem[s % RAW_SLOTS], self.split[s % SPLIT_SLOTS]

        def load(i):
            src = self.w["weights"]
            src = src[s, :, :] if step == 0 else src[bass.ds(i * step + s, 1), :, :].rearrange("a p n -> p (a n)")
            return nc.sync.dma_start(raw.ap[:, :], src)

        loaded = q.dma(load, sem, self.free(raw))
        high = q.act(op(nc.scalar.activation, part.ap[:, :], raw.ap[:, :], ACT.Identity), loaded, self.free(part))
        low = q.dve(op(nc.vector.tensor_tensor, part.low[:, :], raw.ap[:, :], part.ap[:, :].bitcast(F32), ALU.subtract), high)
        raw.free_after(low)
        part.loaded.set(low)

    def next_slab(self, held=0):
        s = self.slab_no
        self.slab_no += 1
        if not held:
            self.prefetch(s + 2)
        part = self.split[s % SPLIT_SLOTS]
        return part.ap, part.low, part.loaded.get(self.q.loop_now), part

    def matmuls(self, out, pairs, *waits):
        nc, n = self.nc, len(pairs)
        for j, (a, b) in enumerate(pairs):
            t = self.q.pe(op(nc.tensor.matmul, out, a, b, start=(j == 0), stop=(j == n - 1)),
                          *(waits if j == 0 else ()), signal=(j == n - 1))
        return t

    def products(self, out, terms, *waits, start=True, stop=True, signal=True):
        nc = self.nc
        passes = [p for ah, al, bh, bl in terms for p in ((ah, bh), (ah, bl), (al, bh))]
        for j, (a, b) in enumerate(passes):
            last = j == len(passes) - 1
            t = self.q.pe(op(nc.tensor.matmul, out, a, b, start=(start and j == 0), stop=(stop and last)),
                          *(waits if j == 0 else ()), signal=(signal and last))
        return t

    def put_h(self, k, cols, src, *ready):
        q, nc = self.q, self.nc
        high = q.act(op(nc.scalar.activation, self.hh[:, k, cols], src, ACT.Identity), *ready, self.h_free)
        return q.dve(op(nc.vector.tensor_tensor, self.hl[:, k, cols], src, self.hh[:, k, cols].bitcast(F32), ALU.subtract), high)

    def load_inputs(self):
        q, nc = self.q, self.nc
        q.dma(op(nc.sync.dma_start, self.small[:, :], self.w["small"]), self.load_sem)
        q.dma(op(nc.sync.dma_start, self.const[:, :], self.w["constants"]), self.load_sem)
        t = q.dma(op(nc.sync.dma_start, self.x[:, :, :], self.w["tokens"]), self.load_sem)
        self.ready = [t]
        self.x_ready = [t]

    def open_modulation(self, block):
        q, nc = self.q, self.nc
        self.ada = [Slot(self.sb(f"ada{i}_{self.ada_no}", (P, D))) for i in range(ADA_SLOTS)]
        self.ada_junk = [Slot(self.sb(f"ada_junk{s}_{self.ada_no}", (P, D), mybir.dt.bfloat16)) for s in range(2)]
        self.cond = self.sb(f"cond_{self.ada_no}", (P, 2, D))
        for s in [*self.ada, *self.ada_junk]:
            s.free_after(*self.region_free)
        load = q.dma(op(nc.sync.dma_start, self.cond[:, :, :], self.w["cond"][:, 2 * block:2 * block + 2, :]),
                     self.side_sem, self.region_free)
        self.cond_ready = q.act(op(nc.scalar.activation, self.cond[:, :, :], self.cond[:, :, :], ACT.Silu), load)

    def modulation_tile(self, j, slot_no, step):
        q, nc, n = self.q, self.nc, self.ada_no
        slot, sem = self.ada[slot_no % ADA_SLOTS], self.ada_sem[slot_no % ADA_SLOTS]
        self.ada_no += 1

        def load(i):
            src = self.w["ada"]
            src = src[n, :, :] if step == 0 else src[bass.ds(i * step + n, 1), :, :].rearrange("a p n -> p (a n)")
            return nc.gpsimd.dma_start(slot.ap[:, :], src)

        loaded = q.dma(load, sem, self.free(slot), engine="gpsimd")
        for s, junk in enumerate(self.ada_junk):
            t = q.dve(op(nc.vector.tensor_tensor_reduce, out=junk.ap[:, :], in0=slot.ap[:, :], in1=self.cond[:, s, :],
                         scale=1.0, scalar=0.0, op0=ALU.mult, op1=ALU.add, accum_out=self.ada_col.ap[:, j, s:s + 1]),
                      loaded, self.cond_ready, self.free(junk), self.free(self.ada_col) if j == 0 else [])
            junk.free_after(t)
        slot.free_after(t)
        return t

    def modulation_finish(self, n, step, done):
        q, nc, first = self.q, self.nc, self.ada_no - n
        cols = self.S("ada_b")

        def add(i):
            at = first if step == 0 else i * step + first
            b = cols[:, at:at + n] if step == 0 else cols[:, bass.ds(at, n)]
            m = self.mods[:, at:at + n, :] if step == 0 else self.mods[:, bass.ds(at, n), :]
            return nc.vector.tensor_tensor(m, self.ada_col.ap[:, 0:n, :],
                                           b.rearrange("p (t o) -> p t o", o=1).broadcast_to([P, n, 2]), ALU.add)

        self.mods_ready = q.dve(add, done, self.ready)
        self.ada_col.free_after(self.mods_ready)

    def modulation(self, n):
        for j in range(n):
            t = self.modulation_tile(j % 16, j, 0)
            if j % 16 == 15 or j == n - 1:
                self.modulation_finish(j % 16 + 1, 0, t)

    def scale_and_gate(self, first, shift, scale, gate, g, half):
        q, nc = self.q, self.nc
        sc = self.mods[:, first + scale * DT:first + (scale + 1) * DT, :]
        if g is None:
            t = q.dve(op(nc.vector.tensor_scalar, self.scales[:, :, :], sc, 1.0, None, ALU.add),
                      self.mods_ready, self.scales_free)
        else:
            gb = g.rearrange("p (t o) -> p t o", o=1).broadcast_to([P, DT, 2])
            t = q.dve(op(nc.vector.scalar_tensor_tensor, self.scales[:, :, :], sc, 1.0, gb, ALU.add, ALU.mult),
                      self.mods_ready, self.scales_free)
        self.gates_ready = q.dve(op(nc.vector.tensor_scalar,
            self.gates[:, :, :], self.mods[:, first + gate * DT:first + (gate + 1) * DT, :], 0.5 if half else 1.0, None, ALU.mult),
            self.mods_ready, self.gates_free)
        self.scales_ready = t
        self.shift = lambda k, s: self.mods[:, first + shift * DT + k, s:s + 1]

    def inverse_rms(self, tiles, dim, eps, cols, *waits):
        q, nc = self.q, self.nc
        n = cols.stop - cols.start
        bank = self.next_bank()
        free = self.free(bank)
        for k, src in enumerate(tiles):
            tmp = self.next_temp()
            sq = q.act(op(nc.scalar.activation, tmp.ap[:, 0:n], src, ACT.Square), self.free(tmp), *waits)
            done = q.pe(op(nc.tensor.matmul, bank.ap[:, 0:n], self.C("ones"), tmp.ap[:, 0:n],
                           start=(k == 0), stop=(k == len(tiles) - 1)), sq, free, self.ready)
            tmp.free_after(done)
        a = q.dve(op(nc.vector.tensor_scalar, self.stat[:, 0:n], bank.ap[:, 0:n], 1.0 / dim, eps, ALU.mult, ALU.add), done)
        bank.free_after(a)
        b = q.act(op(nc.scalar.activation, self.stat[:, 0:n], self.stat[:, 0:n], ACT.Sqrt), a)
        return q.dve(op(nc.vector.reciprocal, self.rstd[:, 0:n], self.stat[:, 0:n]), b, self.rstd_free)

    def ada_norm(self, streams):
        q, nc = self.q, self.nc
        lo = streams[0][1].start
        cols = slice(lo, T)
        r = self.inverse_rms([self.x[:, k, cols] for k in range(DT)], D, RMS_EPS, cols, self.x_ready)
        shift = self.shift
        for k in range(DT):
            tmp = self.next_temp()
            free = self.free(tmp)
            for s, c in streams:
                y = tmp.ap[:, c.start - lo:c.stop - lo]
                a = q.dve(op(nc.vector.scalar_tensor_tensor, y, self.x[:, k, c], self.scales[:, k, s:s + 1],
                             self.rstd[:, c.start - lo:c.stop - lo], ALU.mult, ALU.mult), r, self.scales_ready, free)
                b = q.act(op(nc.scalar.activation, self.hh[:, k, c], y, ACT.Identity, bias=shift(k, s)), a, self.h_free)
                h = q.dve(op(nc.vector.scalar_tensor_tensor, self.hl[:, k, c], y, shift(k, s),
                             self.hh[:, k, c].bitcast(F32), ALU.add, ALU.subtract), b)
            tmp.free_after(h)
        self.rstd_free = [a]
        self.scales_free = [a]
        self.h_ready = [h]

    def h_term(self, k, lo=0, hi=T):
        return self.hh[:, k, lo:hi], self.hl[:, k, lo:hi]

    def add_to_x(self, tile, bank, streams, done):
        q, nc = self.q, self.nc
        lo = streams[0][1].start
        for s, c in streams:
            def add(i, s=s, c=c):
                k = tile(i)
                if isinstance(k, int):
                    x, g = self.x[:, k, c], self.gates[:, k, s:s + 1]
                else:
                    x, g = self.x[:, bass.ds(k, 1), c].rearrange("p a n -> p (a n)"), self.gates[:, bass.ds(k, 1), s]
                return nc.vector.scalar_tensor_tensor(x, bank.ap[:, c.start - lo:c.stop - lo], g, x, ALU.mult, ALU.add)
            a = q.dve(add, done, self.gates_ready, self.x_free)
        bank.free_after(a)
        self.x_ready, self.gates_free = [a], [a]
        return a

    def project_out(self, streams):
        lo = streams[0][1].start

        def tile_out(j, tile):
            wh, wl, loaded, slot = self.next_slab()
            bank = self.bank[j % 3]
            done = self.products(bank.ap[:, 0:T - lo], [
                (wh[:, k * P:(k + 1) * P], wl[:, k * P:(k + 1) * P], *self.h_term(k, lo)) for k in range(DT)],
                loaded, self.h_ready, self.free(bank))
            slot.free_after(done)
            self.add_to_x(tile, bank, streams, done)
            return done

        for j in range(DT):
            done = tile_out(j, lambda i, j=j: j)
        self.h_free = [done]

    def feed_forward(self, kind, streams, loops, chunks_per_turn, ada):
        q, nc = self.q, self.nc
        lo = streams[0][1].start
        n = T - lo
        hidden = [Slot(self.sb(f"hidden_high{t}_{self.slab_no}", (P, T), F32R),
                       self.sb(f"hidden_low{t}_{self.slab_no}", (P, T), F32R)) for t in range(2)]
        for hid in hidden:
            hid.free_after(*self.region_free)
        ada_at = [0, 0, None]

        def some_ada(share, step):
            while ada_at[0] < ada_at[1] * share:
                ada_at[2] = self.modulation_tile(ada_at[0], ada_at[0], step)
                ada_at[0] += 1

        def up(bank):
            wh, wl, loaded, slot = self.next_slab()
            done = self.products(bank.ap[:, 0:n], [
                (wh[:, k * P:(k + 1) * P], wl[:, k * P:(k + 1) * P], *self.h_term(k, lo)) for k in range(DT)],
                loaded, self.h_ready, self.free(bank))
            slot.free_after(done)
            return done

        def chunk(c, of, step):
            ready = []
            for t in range(2):
                temp, hid = self.temp[t], hidden[t]
                if kind == "swiglu":
                    a_bank, b_bank = self.bank[2 * t], self.bank[2 * t + 1]
                    a_done = up(a_bank)
                    a = q.act(op(nc.scalar.activation, temp.ap[:, 0:n], a_bank.ap[:, 0:n], ACT.Silu), a_done, self.free(temp))
                    a_bank.free_after(a)
                    some_ada((6 * c + 2 * t + 1) / (6 * of), step)
                    b_done = up(b_bank)
                    b = q.dve(op(nc.vector.tensor_tensor, temp.ap[:, 0:n], temp.ap[:, 0:n], b_bank.ap[:, 0:n], ALU.mult), a, b_done)
                    b_bank.free_after(b)
                else:
                    bank = self.bank[2 * t]
                    b_done = up(bank)
                    a = q.act(op(nc.scalar.activation, temp.ap[:, 0:n], bank.ap[:, 0:n], ACT.Relu), b_done, self.free(temp))
                    bank.free_after(a)
                    b = q.pool(op(nc.gpsimd.tensor_tensor, temp.ap[:, 0:n], temp.ap[:, 0:n], temp.ap[:, 0:n], ALU.mult), a)
                high = q.act(op(nc.scalar.activation, hid.ap[:, 0:n], temp.ap[:, 0:n], ACT.Identity), b, self.free(hid))
                low = q.dve(op(nc.vector.tensor_tensor, hid.low[:, 0:n], temp.ap[:, 0:n], hid.ap[:, 0:n].bitcast(F32), ALU.subtract), high)
                temp.free_after(low)
                ready.append(low)
                some_ada((6 * c + 2 * t + 2) / (6 * of), step)
            slabs = [self.next_slab(), self.next_slab(held=1)]
            for group in range(2):
                for t, (wh, wl, loaded, slot) in enumerate(slabs):
                    for j in range(4):
                        k, bank = 4 * group + j, self.bank[4 + j]
                        done = self.products(bank.ap[:, 0:n], [
                            (wh[:, k * P:(k + 1) * P], wl[:, k * P:(k + 1) * P], hidden[t].ap[:, 0:n], hidden[t].low[:, 0:n])],
                            loaded, ready[t], self.free(bank) if t == 0 else [], start=(t == 0), stop=(t == 1),
                            signal=(t == 1 or (group == 1 and j == 3)))
                        if t == 1:
                            self.add_to_x(lambda i, k=k: k, bank, streams, done)
                    if group == 1:
                        slot.free_after(done)
                        hidden[t].free_after(done)
                        if t == 0:
                            self.prefetch(self.slab_no + 1)
                some_ada((6 * c + 5 + group) / (6 * of), step)
            self.h_free = [done]

        with self.turns(loops, chunks_per_turn * (6 if kind == "swiglu" else 4)):
            ada_at[:] = [0, ada, None]
            for c in range(chunks_per_turn):
                chunk(c, chunks_per_turn, ada)
            if ada:
                self.modulation_finish(ada, ada, ada_at[2])
        self.ada_no += (loops - 1) * ada
        ada_at[:] = [0, 0, None]
        chunk(0, 1, 0)
        self.region_free = [*self.x_ready, *self.h_free]

    def token_major(self, first):
        return self.big[:, first:first + 8, :].rearrange("p a n -> p (a n)").rearrange("p (t n) -> p t n", t=TT)

    def project_fm(self, n_tiles, first, term, ready, lo=0, bias=None, scale=None):
        q, nc = self.q, self.nc
        n = T - lo
        last, big = {}, self.big

        def tile_out(j, tile):
            wh, wl, loaded, slot = self.next_slab()
            bank = self.bank[j % 3]
            done = self.products(bank.ap[:, 0:n], [
                (wh[:, k * P:(k + 1) * P], wl[:, k * P:(k + 1) * P], *term(k, lo)) for k in range(DT)],
                loaded, ready, self.free(bank))
            slot.free_after(done)

            def copy(i):
                k = tile(i)
                dst = big[:, k + first, lo:T] if isinstance(k, int) else \
                    big[:, bass.ds(k + first, 1), lo:T].rearrange("p a n -> p (a n)")
                b = None if bias is None else bias[:, k:k + 1] if isinstance(k, int) else bias[:, bass.ds(k, 1)]
                if j % 2 == 0:
                    return nc.scalar.activation(dst, bank.ap[:, 0:n], ACT.Identity, **({} if b is None else {"bias": b}))
                if b is None:
                    return nc.vector.tensor_copy(dst, bank.ap[:, 0:n])
                return nc.vector.tensor_scalar(dst, bank.ap[:, 0:n], b, None, ALU.add)

            last[j % 2] = (q.act if j % 2 == 0 else q.dve)(copy, done, self.region_free)
            bank.free_after(last[j % 2])
            return done

        turns = n_tiles // RAW_SLOTS
        if turns > 1:
            with self.turns(turns, RAW_SLOTS):
                for j in range(RAW_SLOTS):
                    done = tile_out(j, lambda i, j=j: i * RAW_SLOTS + j)
        else:
            turns = 0
        for j in range(turns * RAW_SLOTS, n_tiles):
            done = tile_out(j, lambda i, j=j: j)
        return list(last.values()), done

    def project_tm(self, groups, term, dst, ready, dst_free, k_slabs=4, bias=None):
        q, nc = self.q, self.nc
        last = {}
        for g in range(groups):
            banks = [self.bank[4 * (g % 2) + tt] for tt in range(TT)]
            for s in range(k_slabs):
                wh, wl, loaded, slot = self.next_slab()
                for tt, bank in enumerate(banks):
                    terms = []
                    for k in range(2):
                        hh, hl = term(2 * s + k)
                        c = slice(tt * P, (tt + 1) * P)
                        terms.append((hh[:, c], hl[:, c], wh[:, k * 512:(k + 1) * 512], wl[:, k * 512:(k + 1) * 512]))
                    done = self.products(bank.ap[:, :], terms, loaded, ready, self.free(bank) if s == 0 else [],
                                         start=(s == 0), stop=(s == k_slabs - 1))
                    if s == k_slabs - 1:
                        if bias is not None:
                            e = q.dve(op(nc.vector.tensor_tensor, dst(tt, g), bank.ap[:, :], bias[:, g * 512:(g + 1) * 512], ALU.add), done, dst_free)
                            last[0] = e
                        elif tt % 2:
                            last[1] = e = q.act(op(nc.scalar.activation, dst(tt, g), bank.ap[:, :], ACT.Identity), done, dst_free)
                        else:
                            last[0] = e = q.dve(op(nc.vector.tensor_copy, dst(tt, g), bank.ap[:, :]), done, dst_free)
                        bank.free_after(e)
                slot.free_after(done)
        return list(last.values()), done

    def store_output(self, src, ready):
        q, nc = self.q, self.nc
        t = q.dma(op(nc.sync.dma_start, self.out, src), self.store_sem, ready)
        q.add("sync", op(nc.sync.nop), [t], None, 0)

    def transpose_weights(self, w, qt, n_keys, w_t, w_ready, wt_free):
        q, nc = self.q, self.nc
        bank = self.next_bank()
        free = self.free(bank)
        nk = n_keys // P
        for kt in range(nk):
            done = q.pe(op(nc.tensor.transpose, bank.ap[:, kt * P:(kt + 1) * P], w[:, kt * P:(kt + 1) * P], self.C("ident")),
                w_ready, free, signal=(kt == nk - 1))
        copy = q.act(op(nc.scalar.activation, w_t[:, 0:nk, qt * P:(qt + 1) * P], bank.ap[:, 0:nk * P].rearrange("p (k n) -> p k n", k=nk), ACT.Identity),
            done, wt_free)
        bank.free_after(copy)
        return done, copy

    def weigh_values(self, value, w_t, ready, lo=0):
        q, nc = self.q, self.nc
        bank = self.next_bank()
        free = self.free(bank)
        for kt in range(TT):
            c = slice(lo if kt < NC_TOK // P else NC_TOK, T)
            done = q.pe(op(nc.tensor.matmul, bank.ap[:, c], value(kt), w_t[:, kt, c], start=(kt == 0), stop=(kt == TT - 1)),
                ready, free, signal=(kt == TT - 1))
        return bank, done

    def in_order(self, units, start, finish):
        held = None
        for u in units:
            got = start(u)
            if held is not None:
                finish(*held)
            held = (u, got)
        finish(*held)

    def mix_pair(self, pair, n, coef, ready):
        q, nc = self.q, self.nc
        a = q.pool(op(nc.gpsimd.tensor_scalar, pair[0].ap[:, 0:n], pair[0].ap[:, 0:n], coef[:, 0:1], None, ALU.mult), ready)
        return q.dve(op(nc.vector.scalar_tensor_tensor, pair[0].ap[:, 0:n], pair[1].ap[:, 0:n], coef[:, 1:2], pair[0].ap[:, 0:n], ALU.mult, ALU.add), a)

    def rope(self, tile, ready):
        q, nc = self.q, self.nc
        x = self.big[:, tile, LAT]
        bank, tmp = self.next_bank(), self.next_temp()
        sw = self.matmuls(bank.ap[:, 0:NX_TOK], [(self.C("swap"), x)], ready, self.free(bank))
        a = q.dve(op(nc.vector.tensor_tensor, tmp.ap[:, 0:NX_TOK], bank.ap[:, 0:NX_TOK], self.C("sin"), ALU.mult),
                  sw, self.free(tmp))
        bank.free_after(a)
        b = q.pool(op(nc.gpsimd.tensor_tensor, x, x, self.C("cos"), ALU.mult), sw)
        c = q.pool(op(nc.gpsimd.tensor_tensor, x, x, tmp.ap[:, 0:NX_TOK], ALU.add), a, b)
        tmp.free_after(c)
        return c

    def even_mixer(self):
        q, nc = self.q, self.nc
        Q0, K0, MQK0, OP0, GATES, V0, WT, ROWS = 0, 4, 8, 12, 16, 18, (26, 30), 34
        self.big = self.sb("even_big", (P, 36, T))
        masks = self.sb("ml_masks", (P, 4 * T))
        masks_ready = q.dma(op(nc.sync.dma_start, masks[:, :], self.w["ml_masks"]), self.side_sem, self.region_free)
        fm, _ = self.project_fm(18, 0, self.h_term, self.h_ready)
        vals = self.token_major(V0)
        tm, done = self.project_tm(2, self.h_term, lambda tt, g: vals[:, tt, g * 512:(g + 1) * 512], self.h_ready, self.region_free)
        self.h_free = [done]
        row_tile = (GATES, GATES + 1, ROWS, ROWS + 1)
        rows = lambda r: self.big[0:8, row_tile[r], :]
        for r in range(2):
            t = q.act(op(nc.scalar.activation, rows(r), rows(r), ACT.Identity, bias=self.S("gate_b", r, 1)[0:8, :]), fm, self.region_free)
        g_ready, f_ready = self.forget_sums(rows, t)
        lam = self.diff_lambda()

        for j in range(4):
            t = q.pool(op(nc.gpsimd.tensor_scalar, self.big[:, Q0 + j, :], self.big[:, Q0 + j, :], HD ** -0.5, None, ALU.mult), fm)
        roped = [self.rope(Q0 + j, [t, *fm]) for j in range(8)]
        conv = self.conv_silu(MQK0, WT[0], fm)
        for j in range(4):
            og = q.act(op(nc.scalar.activation, self.big[:, OP0 + j, :], self.big[:, OP0 + j, :], ACT.Sigmoid), fm)

        wt_free = [conv, conv]
        n_keys = lambda qt: NC_TOK if qt < NC_TOK // P else T

        for hd in range(4):
            w_t = self.big[:, WT[hd % 2]:WT[hd % 2] + TT, :]
            copies = []

            def scores(qt, hd=hd):
                n = n_keys(qt)
                pair = self.temp[2 * (qt % 2):2 * (qt % 2) + 2]
                col = self.next_cols()
                free = self.free(col)
                for c in range(2):
                    bank = self.next_bank()
                    s = self.matmuls(bank.ap[:, 0:n], [(
                        self.big[HD * c:HD * c + HD, Q0 + hd, qt * P:(qt + 1) * P],
                        self.big[HD * c:HD * c + HD, K0 + hd, 0:n])], roped, self.free(bank))
                    m = q.dve(op(nc.vector.tensor_reduce, col.ap[:, c:c + 1], bank.ap[:, 0:n], AX.X, ALU.max, negate=True), s, free)
                    e = q.act(op(nc.scalar.activation, pair[c].ap[:, 0:n], bank.ap[:, 0:n], ACT.Exp, bias=col.ap[:, c:c + 1],
                        accum_out=col.ap[:, 2 + c:3 + c]), m, self.free(pair[c]))
                    bank.free_after(e)
                r = q.dve(op(nc.vector.reciprocal, col.ap[:, 4:6], col.ap[:, 2:4]), e)
                r2 = q.dve(op(nc.vector.tensor_tensor, col.ap[:, 5:6], col.ap[:, 5:6], self.neg_lam[:, 0:1], ALU.mult), r, lam)
                w = self.mix_pair(pair, n, col.ap[:, 4:6], [r, r2, e])
                col.free_after(w)
                pair[1].free_after(w)
                return pair[0], w

            def turn(qt, got, hd=hd):
                w, ready = got
                done, copy = self.transpose_weights(w.ap, qt, n_keys(qt), w_t, ready, wt_free[hd % 2])
                w.free_after(done)
                copies.append(copy)

            self.in_order(range(TT), scores, turn)
            bank, done = self.weigh_values(lambda kt, hd=hd: vals[:, kt, hd * P:(hd + 1) * P], w_t, copies + tm)
            wt_free[hd % 2] = done
            y_tile = self.big[:, Q0 + hd, :]
            o = q.act(op(nc.scalar.activation, y_tile, bank.ap[:, :], ACT.Identity), done)
            bank.free_after(o)
            r = self.inverse_rms([y_tile], P, RMS_EPS, slice(0, T), o)
            y = q.dve(op(nc.vector.scalar_tensor_tensor, y_tile, y_tile, self.neg_lam[:, 1:2], self.rstd[:, 0:T], ALU.mult, ALU.mult), r, lam)
            self.rstd_free = [y]
            self.put_h(hd, slice(0, T), y_tile, y)

        self.ring = range(6)
        self.bank_at = 0
        for hd in range(4):
            w_t = self.big[:, WT[hd % 2]:WT[hd % 2] + TT, :]
            copies = []
            for d in range(2):
                row = 4 * d + hd
                g_bank = self.bank[6 + d]
                g_all = self.matmuls(g_bank.ap[:, :], [(self.C("ident")[0:8, row:row + 1].broadcast_to([8, P]), rows(0))],
                                     g_ready, self.free(g_bank))
            base = HD * (hd % 2)

            def weights(qt, hd=hd, g_all=g_all, base=base):
                n = n_keys(qt)
                pair = self.temp[2 * (qt % 2):2 * (qt % 2) + 2]
                col = self.next_cols()
                free = self.free(col)
                bank = self.next_bank()
                s = self.matmuls(bank.ap[:, 0:n], [(
                    self.big[base:base + HD, MQK0 + hd // 2, qt * P:(qt + 1) * P],
                    self.big[base:base + HD, MQK0 + 2 + hd // 2, 0:n])], conv, self.free(bank))
                exps = []
                for d in range(2):
                    end = (2 * d + qt % 2 + 1) * T
                    a = q.dve(op(nc.vector.tensor_tensor, pair[d].ap[:, 0:n], self.bank[6 + d].ap[:, 0:n], masks[:, end - n:end], ALU.add),
                              g_all, masks_ready, self.free(pair[d]))
                    m = q.dve(op(nc.vector.tensor_reduce, col.ap[:, d:d + 1], pair[d].ap[:, 0:n], AX.X, ALU.max, negate=True), a, free)
                    exps.append(q.act(op(nc.scalar.activation, pair[d].ap[:, 0:n], pair[d].ap[:, 0:n], ACT.Exp, bias=col.ap[:, d:d + 1]), m))
                f = self.fcol[:, qt * 8:(qt + 1) * 8].rearrange("p (d h) -> p h d", d=2)[:, hd, :]
                b = q.dve(op(nc.vector.tensor_tensor, col.ap[:, 2:4], col.ap[:, 0:2], f, ALU.subtract), m, f_ready)
                b = q.dve(op(nc.vector.tensor_scalar, col.ap[:, 2:4], col.ap[:, 2:4], 80.0, None, ALU.min), b)
                b = q.act(op(nc.scalar.activation, col.ap[:, 2:4], col.ap[:, 2:4], ACT.Exp), b)
                for d in range(2):
                    w = q.dve(op(nc.vector.scalar_tensor_tensor, pair[d].ap[:, 0:n], bank.ap[:, 0:n], HD ** -0.5, pair[d].ap[:, 0:n], ALU.mult, ALU.mult,
                        accum_out=col.ap[:, 4 + d:5 + d]), s, exps[d])
                bank.free_after(w)
                c = q.dve(op(nc.vector.scalar_tensor_tensor, col.ap[:, 6:8], col.ap[:, 4:6], -1.0, col.ap[:, 4:6], ALU.mult, ALU.max), w)
                c = q.dve(op(nc.vector.tensor_tensor, col.ap[:, 6:8], col.ap[:, 6:8], col.ap[:, 2:4], ALU.max), c, b)
                c = q.dve(op(nc.vector.reciprocal, col.ap[:, 6:8], col.ap[:, 6:8]), c)
                out = self.mix_pair(pair, n, col.ap[:, 6:8], [c])
                col.free_after(out)
                pair[1].free_after(out)
                last_dve[0] = a
                return pair[0], out

            last_dve = [None]

            def turn(qt, got, hd=hd):
                w, ready = got
                done, copy = self.transpose_weights(w.ap, qt, n_keys(qt), w_t, ready, wt_free[hd % 2])
                w.free_after(done)
                copies.append(copy)

            self.in_order(range(TT), weights, turn)
            for d in range(2):
                self.bank[6 + d].free_after(last_dve[0])
            bank, done = self.weigh_values(lambda kt, hd=hd: vals[:, kt, 512 + hd * P:512 + (hd + 1) * P], w_t, copies + tm)
            wt_free[hd % 2] = done
            y_tile = self.big[:, K0 + hd, :]
            o = q.act(op(nc.scalar.activation, y_tile, bank.ap[:, :], ACT.Identity), done)
            bank.free_after(o)
            r = self.inverse_rms([y_tile], P, RMS_EPS, slice(0, T), o)
            y = q.dve(op(nc.vector.scalar_tensor_tensor, y_tile, y_tile, self.S("ml_norm_g", hd, 1), self.rstd[:, 0:T], ALU.mult, ALU.mult), r)
            self.rstd_free = [y]
            y = q.dve(op(nc.vector.tensor_tensor, y_tile, y_tile, self.big[:, OP0 + hd, :], ALU.mult), y, og)
            h_ready = self.put_h(4 + hd, slice(0, T), y_tile, y)
        self.ring = range(8)
        self.region_free = [h_ready]
        self.h_ready = [h_ready]

    def forget_sums(self, rows, ready):
        q, nc = self.q, self.nc
        a = q.act(op(nc.scalar.activation, rows(2), rows(1), ACT.Abs), ready)
        a = q.act(op(nc.scalar.activation, rows(2), rows(2), ACT.Exp, scale=-1.0), a)
        a = q.act(op(nc.scalar.activation, rows(2), rows(2), ACT.Ln, bias=1.0), a)
        lf = q.dve(op(nc.vector.scalar_tensor_tensor, rows(1), rows(1), 0.0, rows(2), ALU.min, ALU.subtract), a)
        one = self.C("ones")[0:8, 0:1].broadcast_to([8, T])
        s = q.dve(op(nc.vector.tensor_tensor_scan, rows(3), one, rows(1), 0.0, ALU.mult, ALU.add), lf)
        tot = self.neg_lam[0:8, 2:3]
        t = q.dve(op(nc.vector.tensor_tensor, tot, rows(3)[:, NC_TOK - 1:NC_TOK], rows(3)[:, T - 1:T], ALU.add), s)
        b = q.dve(op(nc.vector.tensor_tensor, rows(1), rows(1), rows(3), ALU.subtract), s)
        isb, isf = self.C("is_bwd", 8), self.C("is_fwd", 8)
        b1 = q.dve(op(nc.vector.tensor_scalar, rows(1)[:, CTX], rows(1)[:, CTX], rows(3)[:, NC_TOK - 1:NC_TOK], isb, ALU.add, ALU.mult), b)
        b2 = q.dve(op(nc.vector.tensor_scalar, rows(1)[:, LAT], rows(1)[:, LAT], tot, isb, ALU.add, ALU.mult), b, t)
        f = q.dve(op(nc.vector.scalar_tensor_tensor, rows(1), rows(3), isf, rows(1), ALU.mult, ALU.add), b1, b2)
        g = q.dve(op(nc.vector.tensor_tensor, rows(0), rows(0), rows(1), ALU.subtract), f)
        bank = self.next_bank()
        free = self.free(bank)
        for tt in range(TT):
            done = q.pe(op(nc.tensor.transpose, bank.ap[:, tt * 8:(tt + 1) * 8], rows(1)[:, tt * P:(tt + 1) * P], self.C("ident")[0:8, 0:8]), f, free)
        c = q.dve(op(nc.vector.tensor_copy, self.fcol[:, :], bank.ap[:, 0:TT * 8]), done)
        bank.free_after(c)
        return g, c

    def diff_lambda(self):
        q, nc = self.q, self.nc
        l = lambda j: self.S("lambda", j * HD, HD)
        col = self.next_cols()
        free = self.free(col)
        tmp = self.next_temp()
        tfree = self.free(tmp)
        for j in range(2):
            a = q.dve(op(nc.vector.tensor_tensor, tmp.ap[:, j * HD:(j + 1) * HD], l(2 * j), l(2 * j + 1), ALU.mult), tfree, self.ready)
            a = q.dve(op(nc.vector.tensor_reduce, col.ap[:, j:j + 1], tmp.ap[:, j * HD:(j + 1) * HD], AX.X, ALU.add), a, free)
        tmp.free_after(a)
        a = q.act(op(nc.scalar.activation, col.ap[:, 2:4], col.ap[:, 0:2], ACT.Exp), a)
        a = q.dve(op(nc.vector.tensor_tensor, col.ap[:, 4:5], col.ap[:, 3:4], col.ap[:, 2:3], ALU.subtract), a)
        b = q.dve(op(nc.vector.tensor_scalar, self.neg_lam[:, 0:1], col.ap[:, 4:5], -LAM_INIT, None, ALU.add), a)
        col.free_after(b)
        return q.dve(op(nc.vector.tensor_scalar, self.neg_lam[:, 1:2], self.S("diff_norm_g"), 1.0 - LAM_INIT, None, ALU.mult), b)

    def conv_silu(self, first, scratch, ready):
        q, nc = self.q, self.nc
        for j in range(4):
            x, y = self.big[:, first + j, :], self.big[:, scratch + j, :]
            w = lambda tap, j=j: self.S("conv_w", 4 * tap + j, 1)
            a = q.act(op(nc.scalar.activation, y, x, ACT.Identity, scale=w(1), bias=self.S("conv_b", j, 1)), ready, self.region_free)
            for s, c in STREAMS:
                lo, hi = c.start, c.stop
                a = q.dve(op(nc.vector.scalar_tensor_tensor, y[:, lo + 1:hi], x[:, lo:hi - 1], w(0), y[:, lo + 1:hi], ALU.mult, ALU.add), a)
                a = q.dve(op(nc.vector.scalar_tensor_tensor, y[:, lo:hi - 1], x[:, lo + 1:hi], w(2), y[:, lo:hi - 1], ALU.mult, ALU.add), a)
            a = q.act(op(nc.scalar.activation, x, y, ACT.Silu), a)
        return a

    def odd_mixer(self):
        q, nc = self.q, self.nc
        Q0, K0, R0, RANK, V0, W0 = 0, 4, 8, 16, 18, 26
        self.big = self.sb("odd_big", (P, 34, T))
        gla_kt = [Slot(self.sb(f"gla_kt{i}", (P, T))) for i in range(2)]
        gla_s = [Slot(self.sb(f"gla_s{i}", (P, 256))) for i in range(2)]
        gla_at = [Slot(self.sb(f"gla_at{i}", (P, 256))) for i in range(2)]
        gate_w = self.sb("gla_gate", (16, D))
        for slot in (*gla_kt, *gla_s, *gla_at):
            slot.free_after(*self.region_free)
        gate_loaded = q.dma(op(nc.sync.dma_start, gate_w[:, :], self.w["gla_gate"]), self.side_sem, self.region_free)
        fm, _ = self.project_fm(18, 0, self.h_term, self.h_ready)
        vals = self.token_major(V0)
        tm, done = self.project_tm(2, self.h_term, lambda tt, g: vals[:, tt, g * 512:(g + 1) * 512], self.h_ready, self.region_free)
        self.h_free = [done]
        for j in range(8):
            swish = q.act(op(nc.scalar.activation, self.big[:, R0 + j, LAT], self.big[:, R0 + j, LAT], ACT.Silu), fm)

        n_chunks, L = NX_TOK // GLA_CHUNK, GLA_CHUNK
        self.ring = range(7)
        self.bank_at = 0
        scratch_free = [self.region_free, self.region_free]
        for hd in range(4):
            o_bank = self.bank[7]
            o_free = self.free(o_bank)
            first = True
            for d in range(2):
                la, cum, incl, excl = (self.big[:, W0 + 4 * d + n, :] for n in range(4))
                bank = self.next_bank()
                z = self.matmuls(bank.ap[:, :], [(gate_w[:, d * 512 + hd * P:d * 512 + (hd + 1) * P],
                                                  self.big[0:16, RANK + d, :])], fm, gate_loaded, self.free(bank))
                bias = self.S("gla_b", 4 * d + hd, 1)
                a = self._biased(la, bank, bias, z, scratch_free[d])
                bank.free_after(a)
                a = self._log_sigmoid(la, cum, a)
                s = self._scan(cum, la, a)
                e1 = self._rest(excl, cum, s, n_chunks, L)
                if d == 0:
                    inc_ap, exc_ap = cum, excl
                    inc_ready = exc_ready = e1
                else:
                    inc_ap, exc_ap = excl, incl
                    inc_ready, exc_ready = self._backward_sums(excl, incl, cum, la, e1)
                qk, kd = self.temp[d], self.temp[2 + d]
                k_t, smat, a_t, col = gla_kt[d], gla_s[d], gla_at[d], self.next_cols()
                qk_ready, kd_ready, dec = self._gla_factors(hd, qk, kd, col, inc_ap, exc_ap, cum, inc_ready, exc_ready, s, fm)
                scratch_free[d] = [kd_ready, dec, qk_ready]
                bank = self.next_bank()
                free = self.free(bank)
                for tt in range(TT):
                    done = q.pe(op(nc.tensor.transpose, bank.ap[:, tt * P:(tt + 1) * P], kd.ap[:, tt * P:(tt + 1) * P], self.C("ident")),
                        kd_ready, free, signal=(tt == TT - 1))
                kd.free_after(done)
                kt_ready = q.act(op(nc.scalar.activation, k_t.ap[:, :], bank.ap[:, :], ACT.Identity),
                                 done, self.free(k_t))
                bank.free_after(kt_ready)
                v = lambda tt, lo, n, p0=0, pn=P, hd=hd: vals[p0:p0 + pn, tt, hd * 256 + lo:hd * 256 + lo + n]
                bank = self.next_bank()
                st = self.matmuls(bank.ap[:, 0:256], [(k_t.ap[:, tt * P:(tt + 1) * P], v(tt, 0, 256)) for tt in range(2)],
                                  kt_ready, tm, self.free(bank))
                s_ready = q.dve(op(nc.vector.tensor_copy, smat.ap[:, :], bank.ap[:, 0:256]),
                                st, self.free(smat))
                bank.free_after(s_ready)
                at_free = self.free(a_t)
                for tile in range(2):
                    bank = self.next_bank()
                    c = slice(tile * P, (tile + 1) * P)
                    sc = self.matmuls(bank.ap[:, 0:P], [(qk.ap[:, 256 + tile * P:256 + (tile + 1) * P], qk.ap[:, c])],
                                      qk_ready, self.free(bank))
                    at_ready = q.dve(op(nc.vector.tensor_tensor, a_t.ap[:, c], bank.ap[:, 0:P], self.C(f"gla_mask{d}"), ALU.mult), sc, at_free)
                    bank.free_after(at_ready)
                    for et in range(2):
                        done = self._acc(o_bank.ap[:, et * 256 + tile * P:et * 256 + (tile + 1) * P],
                                         v(2 + tile, et * P, P), a_t.ap[:, c], first, at_ready, tm, o_free)
                        first = False
                a_t.free_after(done)
                order = range(n_chunks) if d == 0 else range(n_chunks - 1, -1, -1)
                for n, c in enumerate(order):
                    for et in range(2):
                        read = self._acc(o_bank.ap[:, et * 256 + c * L:et * 256 + (c + 1) * L],
                                         smat.ap[:, et * P:(et + 1) * P], qk.ap[:, c * L:(c + 1) * L], False, s_ready)
                    if n == n_chunks - 1:
                        break
                    tt, p0 = 2 + c // 2, (c % 2) * L
                    bank = self.next_bank()
                    up = self.matmuls(bank.ap[:, 0:256], [(k_t.ap[p0:p0 + L, tt * P:(tt + 1) * P], v(tt, 0, 256, p0, L))],
                                      kt_ready, self.free(bank))
                    s_ready = q.dve(op(nc.vector.scalar_tensor_tensor, smat.ap[:, :], smat.ap[:, :], col.ap[:, c:c + 1], bank.ap[:, 0:256], ALU.mult, ALU.add), up, read, dec)
                    bank.free_after(s_ready)
                qk.free_after(read)
                smat.free_after(read)
                k_t.free_after(read)
                col.free_after(s_ready)
            y_tile = [self.big[:, tile, LAT] for tile in (Q0 + hd, K0 + hd)]
            for et in range(2):
                o = q.act(op(nc.scalar.activation, y_tile[et], o_bank.ap[:, et * 256:(et + 1) * 256], ACT.Identity), read, qk_ready, kd_ready)
            o_bank.free_after(o)
            r = self.inverse_rms(y_tile, 256, RMS_EPS, LAT, o)
            for et in range(2):
                y = q.dve(op(nc.vector.scalar_tensor_tensor, y_tile[et], y_tile[et], self.S("gla_norm_g", et, 1),
                    self.rstd[:, 0:NX_TOK], ALU.mult, ALU.mult), r)
                self.rstd_free = [y]
                y = q.dve(op(nc.vector.tensor_tensor, y_tile[et], y_tile[et], self.big[:, R0 + 2 * hd + et, LAT], ALU.mult),
                    y, swish)
                h_ready = self.put_h(2 * hd + et, LAT, y_tile[et], y)
        self.ring = range(8)
        self.region_free = [h_ready]
        self.h_ready = [h_ready]

    def _acc(self, out, a, b, start, *waits):
        return self.q.pe(op(self.nc.tensor.matmul, out, a, b, start=start, stop=True, skip_group_check=True), *waits)

    def _biased(self, out, bank, bias, *waits):
        return self.q.act(op(self.nc.scalar.activation, out, bank.ap[:, :], ACT.Identity, bias=bias), *waits)

    def _log_sigmoid(self, z, tmp, ready):
        q, nc = self.q, self.nc
        a = q.act(op(nc.scalar.activation, tmp, z, ACT.Abs), ready)
        a = q.act(op(nc.scalar.activation, tmp, tmp, ACT.Exp, scale=-1.0), a)
        a = q.act(op(nc.scalar.activation, tmp, tmp, ACT.Ln, bias=1.0), a)
        return q.dve(op(nc.vector.scalar_tensor_tensor, z, z, 0.0, tmp, ALU.min, ALU.subtract), a)

    def _scan(self, out, la, ready):
        return self.q.dve(op(self.nc.vector.tensor_tensor_scan, out, self.C("gla_carry"), la, 0.0, ALU.mult, ALU.add), ready)

    def _rest(self, out, cum, ready, n_chunks, L):
        q, nc = self.q, self.nc
        a = q.dve(op(nc.vector.tensor_scalar, out[:, CTX], cum[:, CTX], -1.0, cum[:, NC_TOK - 1:NC_TOK], ALU.mult, ALU.add), ready)
        by = lambda ap: ap[:, LAT].rearrange("p (c l) -> p c l", l=L)
        return q.dve(op(nc.vector.tensor_tensor, by(out), by(cum)[:, :, L - 1:L].broadcast_to([P, n_chunks, L]), by(cum), ALU.subtract), ready)

    def _backward_sums(self, rest, excl, cum, la, ready):
        q, nc = self.q, self.nc
        a = q.pool(op(nc.gpsimd.tensor_tensor, rest, rest, la, ALU.add), ready)
        b = q.dve(op(nc.vector.tensor_tensor, excl, cum, la, ALU.subtract), ready)
        return a, b

    def _gla_factors(self, hd, qk, kd, col, incl, excl, cum, inc_ready, exc_ready, scan_ready, proj):
        q, nc = self.q, self.nc
        inv_tau = 1.0 / 16.0
        qh, kh = self.big[:, hd, LAT], self.big[:, 4 + hd, :]
        free = self.free(qk)
        a = q.act(op(nc.scalar.activation, qk.ap[:, 0:256], incl[:, LAT], ACT.Exp, scale=inv_tau), inc_ready, free)
        b = q.act(op(nc.scalar.activation, qk.ap[:, 256:512], incl[:, LAT], ACT.Exp, scale=-inv_tau), inc_ready)
        c = q.act(op(nc.scalar.activation, kd.ap[:, :], excl, ACT.Exp, scale=inv_tau), exc_ready, self.free(kd))
        ends = cum[:, LAT].rearrange("p (c l) -> p c l", l=GLA_CHUNK)[:, :, GLA_CHUNK - 1]
        dec = q.act(op(nc.scalar.activation, col.ap[:, 0:4], ends, ACT.Exp, scale=inv_tau), scan_ready, self.free(col))
        a = q.dve(op(nc.vector.scalar_tensor_tensor, qk.ap[:, 0:256], qk.ap[:, 0:256], 128 ** -0.5, qh, ALU.mult, ALU.mult), a, proj)
        b = q.dve(op(nc.vector.tensor_tensor, qk.ap[:, 256:512], qk.ap[:, 256:512], kh[:, LAT], ALU.mult), b, proj)
        c = q.pool(op(nc.gpsimd.tensor_tensor, kd.ap[:, :], kd.ap[:, :], kh, ALU.mult), c, proj)
        return b, c, dec

    def final_norm(self):
        q, nc = self.q, self.nc
        r = self.inverse_rms([self.x[:, k, LAT] for k in range(DT)], D, RMS_EPS, LAT, self.x_ready)
        for k in range(DT):
            a = q.dve(op(nc.vector.scalar_tensor_tensor, self.x[:, k, LAT], self.x[:, k, LAT], self.S("final_g", k, 1), self.rstd[:, 0:NX_TOK], ALU.mult, ALU.mult), r)
        self.rstd_free = [a]
        c = q.dma(op(nc.sync.dma_start, self.x[:, :, CTX], self.w["ctx_2"]), self.side_sem, r)
        self.x_ready = [a, c]

    def modulate(self, streams, branch):
        q, nc = self.q, self.nc
        shift = self.shift
        for k in range(DT):
            tmp = self.next_temp()
            free = self.free(tmp)
            for s, c in streams:
                a = q.act(op(nc.scalar.activation, tmp.ap[:, c], self.x[:, k, c], ACT.Identity, scale=self.scales[:, k, s:s + 1],
                             bias=shift(k, s)), self.x_ready, self.scales_ready, free)
            cols = slice(streams[0][1].start, T)
            h = self.put_h(k, cols, tmp.ap[:, cols], a)
            tmp.free_after(h)
            cols = slice(branch[0][1].start, T)
            x = q.pool(op(nc.gpsimd.tensor_scalar, self.x[:, k, cols], self.x[:, k, cols], ALPHA, None, ALU.mult), a)
        self.h_ready = [h]
        self.scales_free = [a]
        self.x_free = [x]

    def layer_norm(self, streams, layer, which):
        q, nc = self.q, self.nc
        cols = slice(streams[0][1].start, T)
        n = cols.stop - cols.start
        bank = self.next_bank()
        total = self.matmuls(bank.ap[:, 0:n], [(self.C("ones"), self.x[:, k, cols]) for k in range(DT)],
                             self.x_ready, self.free(bank))
        for k in range(DT):
            a = q.dve(op(nc.vector.scalar_tensor_tensor, self.x[:, k, cols], bank.ap[:, 0:n], -1.0 / D, self.x[:, k, cols], ALU.mult, ALU.add), total)
        bank.free_after(a)
        r = self.inverse_rms([self.x[:, k, cols] for k in range(DT)], D, LN_EPS, cols, a)
        g = lambda k: self.S("ln", (4 * layer + 2 * which) * DT + k, 1)
        b = lambda k: self.S("ln", (4 * layer + 2 * which + 1) * DT + k, 1)
        for k in range(DT):
            a = q.dve(op(nc.vector.scalar_tensor_tensor, self.x[:, k, cols], self.x[:, k, cols], g(k), self.rstd[:, 0:n], ALU.mult, ALU.mult), r)
            c = q.act(op(nc.scalar.activation, self.x[:, k, cols], self.x[:, k, cols], ACT.Identity, bias=b(k)), a)
        self.rstd_free = [a]
        self.x_ready = [c]

    def softmax_scores(self, pairs, n, temp, col, ready):
        q, nc = self.q, self.nc
        bank = self.next_bank()
        s = self.matmuls(bank.ap[:, 0:n], pairs, ready, self.free(bank))
        m = q.dve(op(nc.vector.tensor_reduce, col.ap[:, 0:1], bank.ap[:, 0:n], AX.X, ALU.max, negate=True),
                  s, self.free(col))
        e = q.act(op(nc.scalar.activation, temp.ap[:, 0:n], bank.ap[:, 0:n], ACT.Exp, bias=col.ap[:, 0:1],
                                                 accum_out=col.ap[:, 1:2]), m, self.free(temp))
        bank.free_after(e)
        return self.normalise(n, temp, col, e)

    def normalise(self, n, temp, col, e):
        q, nc = self.q, self.nc
        r = q.dve(op(nc.vector.reciprocal, col.ap[:, 2:3], col.ap[:, 1:2]), e)
        w = q.pool(op(nc.gpsimd.tensor_scalar, temp.ap[:, 0:n], temp.ap[:, 0:n], col.ap[:, 2:3], None, ALU.mult), r)
        col.free_after(w)
        return w

    def mla_mixer(self):
        q, nc = self.q, self.nc
        QC, KC, KPE, QN, QPE, KN, V0, WT = 0, 4, 6, 8, 16, 20, 28, (0, 36)
        heads, scale = 8, (128 + 64) ** -0.5
        self.big = self.sb("mla_big", (P, 40, T))
        fm, done = self.project_fm(7, 0, self.h_term, self.h_ready)
        kpe = self.rope(KPE, fm)
        self.h_free = [done]
        for first, n, dim, gain in ((QC, 4, 512, "q_norm"), (KC, 2, 256, "kv_norm")):
            r = self.inverse_rms([self.big[:, first + k, :] for k in range(n)], dim, RMS_EPS, slice(0, T), fm)
            for k in range(n):
                tile = self.big[:, first + k, :]
                a = q.dve(op(nc.vector.scalar_tensor_tensor, tile, tile, self.S(gain, k, 1), self.rstd[:, :], ALU.mult, ALU.mult), r)
                normed = self.put_h(first + k, slice(0, T), tile, a)
            self.rstd_free = [a]
        for s in range(6):
            wh, wl, loaded, slot = self.next_slab()
            for t in range(2):
                bank = self.next_bank()
                cols = [slice(k * 256 + t * P, k * 256 + (t + 1) * P) for k in range(4)]
                done = self.products(bank.ap[:, :], [(wh[:, cols[k]], wl[:, cols[k]], *self.h_term(QC + k)) for k in range(4)],
                                     loaded, normed, self.free(bank))
                q_n = q.act(op(nc.scalar.activation, self.big[:, QN + 2 * s + t, :], bank.ap[:, :], ACT.Identity, scale=scale),
                            done, self.region_free)
                bank.free_after(q_n)
            slot.free_after(done)
        q_parts = [q_n, *[self.rope(QPE + j, [q_n]) for j in range(4)]]
        for s in range(2):
            wh, wl, loaded, slot = self.next_slab()
            for t in range(4):
                bank = self.next_bank()
                cols = [slice(k * 512 + t * P, k * 512 + (t + 1) * P) for k in range(2)]
                done = self.products(bank.ap[:, :], [(wh[:, cols[k]], wl[:, cols[k]], *self.h_term(KC + k)) for k in range(2)],
                                     loaded, normed, self.free(bank))
                kn = q.dve(op(nc.vector.tensor_copy, self.big[:, KN + 4 * s + t, :], bank.ap[:, :]), done, self.region_free)
                bank.free_after(kn)
            slot.free_after(done)
        vals = self.token_major(V0)
        tm, done = self.project_tm(2, lambda k: self.h_term(KC + k), lambda tt, g: vals[:, tt, g * 512:(g + 1) * 512],
                                   normed, self.region_free, k_slabs=1)
        self.h_free = [done]
        wt_free = [[normed], self.region_free]
        for hd in range(heads):
            w_t = self.big[:, WT[hd % 2]:WT[hd % 2] + TT, :]
            copies, base = [], HD * (hd % 2)
            n_keys = lambda qt: NC_TOK if qt < NC_TOK // P else T

            def scores(qt, hd=hd, base=base):
                n, c = n_keys(qt), slice(qt * P, (qt + 1) * P)
                temp, col = self.temp[qt % 4], self.next_cols()
                return temp, self.softmax_scores([
                    (self.big[:, QN + hd, c], self.big[:, KN + hd, 0:n]),
                    (self.big[base:base + HD, QPE + hd // 2, c], self.big[base:base + HD, KPE, 0:n])],
                    n, temp, col, [kpe, kn, *q_parts])

            def turn(qt, got, hd=hd):
                w, ready = got
                done, copy = self.transpose_weights(w.ap, qt, n_keys(qt), w_t, ready, wt_free[hd % 2])
                w.free_after(done)
                copies.append(copy)

            self.in_order(range(TT), scores, turn)
            bank, done = self.weigh_values(lambda kt, hd=hd: vals[:, kt, hd * P:(hd + 1) * P], w_t, copies + tm)
            wt_free[hd % 2] = [done]
            o = q.act(op(nc.scalar.activation, self.big[:, QN + hd, :], bank.ap[:, :], ACT.Identity), done)
            bank.free_after(o)
            h_ready = self.put_h(hd, slice(0, T), self.big[:, QN + hd, :], o)
        self.h_ready = self.region_free = [h_ready]

    def na_mixer(self):
        q, nc = self.q, self.nc
        Q0, K0, V0, WT = 0, 8, 16, (24, 28)
        heads, scale = 16, HD ** -0.5
        self.big = self.sb("na_big", (P, 32, T))
        na_raw = [Slot(self.sb(f"na_raw{i}", (P, 6 * GRID_W))) for i in range(2)]
        na_bias = [Slot(self.sb(f"na_bias{i}", (P, 6 * GRID_W))) for i in range(2)]
        bv = self.sb("na_bv", (P, D))
        for slot in (*na_raw, *na_bias):
            slot.free_after(*self.region_free)
        bv_loaded = q.dma(op(nc.sync.dma_start, bv[:, :], self.w["na_bv"]), self.side_sem, self.region_free)
        fq, _ = self.project_fm(8, Q0, self.h_term, self.h_ready, bias=self.S("na_b", 0, 8), lo=NC_TOK)
        fk, _ = self.project_fm(8, K0, self.h_term, self.h_ready, bias=self.S("na_b", 8, 8))
        vals = self.token_major(V0)
        tm, done = self.project_tm(2, self.h_term, lambda tt, g: vals[:, tt, g * 512:(g + 1) * 512], self.h_ready,
                                   [bv_loaded, *self.region_free], bias=bv)
        self.h_free = [done]
        wt_free = [self.region_free, self.region_free]
        rel = NX_TOK // GRID_W + 2
        rpb = self.w["na_rpb"]
        n_r, n_c = 15, 31
        for hd in range(heads):
            base, tile = HD * (hd % 2), hd // 2
            w_t = self.big[:, WT[hd % 2]:WT[hd % 2] + TT, :]
            copies = []
            raw, b_buf, n_b = na_raw[hd % 2], na_bias[hd % 2], rel * GRID_W
            free = self.free(raw)
            for r2 in range(2):
                at = bass.AP(rpb.tensor, hd * n_r * n_c + (4 + r2) * n_c + 15 - (GRID_W - 1), [[1, GRID_W], [n_c, rel], [1, GRID_W]])
                got = q.dma(op(nc.sync.dma_start, raw.ap[r2 * GRID_W:(r2 + 1) * GRID_W, 0:n_b].rearrange("p (m n) -> p m n", n=GRID_W), at),
                    self.bias_sem[hd % 2], free)
            mask = self.C("na_mask").rearrange("p (o n) -> p o n", o=1).broadcast_to([P, rel, GRID_W])
            bias = b_buf.ap[:, :]
            biased = q.pool(op(nc.gpsimd.tensor_copy, bias, raw.ap[:, n_b - 1::-1]), got, self.free(b_buf))
            raw.free_after(biased)
            biased = q.pool(op(nc.gpsimd.tensor_tensor, bias.rearrange("p (m n) -> p m n", n=GRID_W), bias.rearrange("p (m n) -> p m n", n=GRID_W), mask, ALU.add), biased)

            def scores(qt, base=base, tile=tile, bias=bias, biased=biased):
                temp, col, bank = self.temp[qt % 4], self.next_cols(), self.next_bank()
                s = self.matmuls(bank.ap[:, :], [(
                    self.big[base:base + HD, Q0 + tile, qt * P:(qt + 1) * P], self.big[base:base + HD, K0 + tile, :])],
                    fq, fk, self.free(bank))
                a = q.act(op(nc.scalar.activation, temp.ap[:, CTX], bank.ap[:, CTX], ACT.Identity, scale=scale), s, self.free(temp))
                at = (2 - 2 * (qt - 2)) * GRID_W
                b = q.dve(op(nc.vector.scalar_tensor_tensor, temp.ap[:, LAT], bank.ap[:, LAT], scale, bias[:, at:at + NX_TOK], ALU.mult, ALU.add), s, biased, a)
                bank.free_after(b)
                m = q.dve(op(nc.vector.tensor_reduce, col.ap[:, 0:1], temp.ap[:, :], AX.X, ALU.max, negate=True),
                          a, b, self.free(col))
                e = q.act(op(nc.scalar.activation, temp.ap[:, :], temp.ap[:, :], ACT.Exp, bias=col.ap[:, 0:1],
                                                         accum_out=col.ap[:, 1:2]), m)
                used[0] = b
                return temp, self.normalise(T, temp, col, e)

            used = [None]

            def turn(qt, got, hd=hd, w_t=w_t):
                w, ready = got
                done, copy = self.transpose_weights(w.ap, qt, T, w_t, ready, wt_free[hd % 2])
                w.free_after(done)
                copies.append(copy)

            self.in_order(range(2, TT), scores, turn)
            b_buf.free_after(used[0])
            bank = self.next_bank()
            done = self.matmuls(bank.ap[base:base + HD, 0:NX_TOK], [
                (vals[:, kt, hd * HD:(hd + 1) * HD], w_t[:, kt, LAT]) for kt in range(TT)], copies, tm, self.free(bank))
            wt_free[hd % 2] = [done]
            y = self.big[base:base + HD, Q0 + tile, LAT]
            out = q.act(op(nc.scalar.activation, y, bank.ap[base:base + HD, 0:NX_TOK], ACT.Identity), done)
            bank.free_after(out)
            if base:
                h_ready = self.put_h(tile, LAT, self.big[:, Q0 + tile, LAT], out)
        self.h_ready = self.region_free = [h_ready]


def run_stages(m):
    BOTH, LATENT = STREAMS, STREAMS[1:]
    g = lambda l, n: m.S("norm_g", (3 * l + n) * DT, DT)
    m.load_inputs()
    m.prefetch(0)
    m.prefetch(1)
    with m.stage():
        m.open_modulation(0)
        m.modulation(24)
        m.scale_and_gate(0, 0, 1, 2, g(0, 0), True)
        m.ada_norm(BOTH)
        m.feed_forward("swiglu", BOTH, 10, 1, 6)
    m.scale_and_gate(0, 3, 4, 5, g(0, 1), False)
    m.ada_norm(BOTH)
    with m.stage():
        m.even_mixer()
        m.project_out(BOTH)
    with m.stage():
        m.open_modulation(0)
        m.scale_and_gate(0, 6, 7, 8, g(0, 2), True)
        m.ada_norm(BOTH)
        m.feed_forward("swiglu", BOTH, 10, 1, 6)
    with m.stage():
        m.open_modulation(1)
        m.scale_and_gate(72, 0, 1, 2, g(1, 0), True)
        m.ada_norm(BOTH)
        m.feed_forward("swiglu", BOTH, 10, 1, 6)
    m.scale_and_gate(72, 3, 4, 5, g(1, 1), False)
    m.ada_norm(BOTH)
    with m.stage():
        m.odd_mixer()
        m.project_out(LATENT)
    with m.stage():
        m.scale_and_gate(72, 6, 7, 8, g(1, 2), True)
        m.ada_norm(LATENT)
        m.feed_forward("swiglu", LATENT, 10, 1, 0)
    m.final_norm()

    for l, (first, streams, mixer) in enumerate(((144, BOTH, m.mla_mixer), (192, LATENT, m.na_mixer))):
        m.scale_and_gate(first, 0, 1, 2, None, False)
        m.modulate(BOTH, streams)
        with m.stage():
            mixer()
            m.project_out(streams)
        m.layer_norm(streams, l, 0)
        with m.stage():
            if l == 0:
                m.open_modulation(1)
            m.scale_and_gate(first, 3, 4, 5, None, False)
            m.modulate(streams, streams)
            m.feed_forward("relu2", streams, 5, 3, 7 if l == 0 else 0)
            if l == 0:
                m.modulation(1)
        m.layer_norm(streams, l, 1)
    m.store_output(m.x[:, :, LAT], m.x_ready)


def build_program(nc, w, out):
    with ExitStack() as stack:
        m = Model(nc, stack, w, out)
        run_stages(m)
        m.q.emit()


def kernel(**inputs):
    import concourse.bacc as bacc
    from concourse.bass_utils import run_bass_kernel_spmd

    arrays = lay_out(inputs)
    nc = bacc.Bacc("TRN2", target_bir_lowering=False, num_devices=1)
    w = {n: nc.dram_tensor(n, a.shape, F32, kind="ExternalInput").ap() for n, a in arrays.items()}
    out = nc.dram_tensor("out", (P, DT, NX_TOK), F32, kind="ExternalOutput").ap()
    build_program(nc, w, out)
    r = run_bass_kernel_spmd(nc, [arrays], core_ids=[0])
    got = r.results[0]["out"]
    return np.ascontiguousarray(got.transpose(2, 1, 0).reshape(1, NX_TOK, D))
```

```python
import math
from contextlib import ExitStack, contextmanager

import numpy as np
import concourse.bass as bass
from concourse import mybir
from concourse.alu_op_type import AluOpType as ALU

F32 = mybir.dt.float32
F32R = mybir.dt.float32r
ACT = mybir.ActivationFunctionType
AX = mybir.AxisListType

P = 128
D = 1024
DT = D // P
NC_TOK = 256
NX_TOK = 256
T = NC_TOK + NX_TOK
TT = T // P
GRID_W = 64
FF = 2816
FT = FF // P
FF2 = 4096
FT2 = FF2 // P
N_MOD1, N_MOD2 = 9, 6
SLAB = 1024
RAW_SLOTS, SPLIT_SLOTS = 4, 4
AHEAD = SPLIT_SLOTS - 1
ADA_SLOTS = 6
HD = 64
RMS_EPS, LN_EPS = 1e-6, 1e-5
LAM_INIT = 0.8 - 0.6 * math.exp(0.0)
ALPHA = (2.0 * 2) ** 0.25
NEG = -1.0e30
CTX, LAT = slice(0, NC_TOK), slice(NC_TOK, T)
STREAMS = ((0, CTX), (1, LAT))
GLA_CHUNK = 64


class Sem:
    def __init__(self, handle, start):
        self.handle, self.count = handle, start


class Loop:

    def __init__(self, n, at):
        self.n, self.at, self.step = n, at, {}


class Event:

    def __init__(self, sem, value, loop):
        self.sem, self.value, self.loop = sem, value, loop


class LastTurn:

    def __init__(self, mark, loop):
        self.mark, self.loop = mark, loop


class Mark:

    def __init__(self):
        self.events, self.in_loop = [], {}

    def set(self, *events):
        self.events = flat(events)
        for t in self.events:
            if t.loop is not None:
                self.in_loop[t.loop] = self.events

    def get(self, loop):
        waits = list(self.events)
        if loop is not None and not any(t.loop is loop for t in waits):
            waits.append(LastTurn(self, loop))
        return waits


class Slot:

    def __init__(self, ap, low=None):
        self.ap, self.low, self.loaded, self.unused = ap, low, Mark(), Mark()

    def free(self, loop):
        return self.unused.get(loop)

    def free_after(self, *events):
        self.unused.set(*events)


ENGINES = ("tensor", "scalar", "vector", "gpsimd", "sync")
PRIME = 512


def flat(events):
    if isinstance(events, (list, tuple)):
        return [e for part in events for e in flat(part)]
    return [events]


def op(build, *args, **kwargs):
    return lambda i: build(*args, **kwargs)


class Queues:
    def __init__(self, nc, stack):
        self.nc, self.stack = nc, stack
        self.queue = {e: [] for e in ENGINES}
        self.sems = []
        self.done = {e: self.sem(f"done_{e}", PRIME) for e in ENGINES if e != "sync"}
        self.loop_now = None

    def sem(self, name, start=0):
        s = Sem(self.stack.enter_context(self.nc.semaphore(name)), start)
        self.sems.append(s)
        return s

    @contextmanager
    def loop(self, n):
        lp = Loop(n, {s: s.count for s in self.sems})
        outer, self.queue = self.queue, {e: [] for e in ENGINES}
        self.loop_now = lp
        yield
        self.loop_now = None
        inner, self.queue = self.queue, outer
        for s in self.sems:
            lp.step[s] = s.count - lp.at.get(s, s.count)
            s.count += (n - 1) * lp.step[s]
        for e in ENGINES:
            if inner[e]:
                self.queue[e].append((lp, inner[e]))

    def add(self, engine, fn, waits, sem, inc):
        self.queue[engine].append((fn, flat(waits), sem, inc))
        if sem is None:
            return None
        sem.count += inc
        return Event(sem, sem.count, self.loop_now)

    def pe(self, fn, *waits, signal=True):
        return self.add("tensor", fn, waits, self.done["tensor"] if signal else None, 1)

    def act(self, fn, *waits):
        return self.add("scalar", fn, waits, self.done["scalar"], 1)

    def dve(self, fn, *waits):
        return self.add("vector", fn, waits, self.done["vector"], 1)

    def pool(self, fn, *waits):
        return self.add("gpsimd", fn, waits, self.done["gpsimd"], 1)

    def dma(self, fn, sem, *waits, engine="sync"):
        return self.add(engine, fn, waits, sem, 16)

    def emit(self):
        with self.nc.Block() as block:
            for name in ENGINES:
                self._register(block, name)

    def _register(self, block, name):
        def program(eng):
            if name in self.done:
                eng.sem_inc(self.done[name].handle, PRIME)
            self._run(eng, self.queue[name], None, 0, {})

        {"tensor": block.tensor, "scalar": block.scalar, "vector": block.vector,
         "gpsimd": block.gpsimd, "sync": block.sync}[name](program)

    def _run(self, eng, items, loop, i, seen):
        for item in items:
            if isinstance(item[0], Loop):
                with eng.Fori(0, item[0].n) as j:
                    self._run(eng, item[1], item[0], j, dict(seen))
                continue
            fn, waits, sem, inc = item
            for w in waits:
                for handle, key, base, slope in self._values(w, loop):
                    if seen.get((key, slope), -1) >= base:
                        continue
                    seen[(key, slope)] = base
                    eng.wait_ge(handle, base if slope == 0 else i * slope + base)
            ins = fn(i)
            if sem is not None:
                ins.then_inc(sem.handle, inc)

    def _values(self, w, loop):
        if isinstance(w, LastTurn):
            out = []
            for t in w.mark.in_loop.get(w.loop, []):
                d = w.loop.step[t.sem]
                if t.value - d < 1:
                    raise ValueError("a loop's wait below one: raise PRIME")
                out.append((t.sem.handle, t.sem, t.value - d, d))
            return out
        if w.loop is None:
            return [(w.sem.handle, w.sem, w.value, 0)]
        d = w.loop.step[w.sem]
        if w.loop is loop:
            return [(w.sem.handle, w.sem, w.value, d)]
        return [(w.sem.handle, w.sem, w.value + (w.loop.n - 1) * d, 0)]


def constant_table():
    parts, at, n = [], {}, 0

    def put(name, a):
        nonlocal n
        full = np.zeros((P, a.shape[1]), np.float32)
        full[: a.shape[0]] = a
        parts.append(full)
        at[name] = (n, n + a.shape[1])
        n += a.shape[1]

    p = np.arange(P)
    put("ident", np.eye(P))
    put("ones", np.ones((P, P)))
    put("row_of", np.tile(np.eye(DT).reshape(1, -1), (P, 1)))
    partner = np.where(p % 32 < 16, p + 16, p - 16)
    put("swap", (p[:, None] == partner[None, :]).astype(np.float32))
    pos = np.arange(NX_TOK)
    inv = (10000.0 ** (-np.arange(16, dtype=np.float32) * 2.0 / 32)).astype(np.float32)
    place = np.where((p % HD < 32)[:, None], pos[None, :] // GRID_W, pos[None, :] % GRID_W).astype(np.float32)
    ang = (place * inv[p % 16][:, None]).astype(np.float32)
    put("cos", np.cos(ang))
    put("sin", np.sin(ang) * np.where(p % 32 < 16, -1.0, 1.0)[:, None])
    s = np.arange(NX_TOK)[None, :]
    masks = []
    for d in range(2):
        for tile in range(2):
            t = tile * P + p[:, None]
            masks += [np.zeros((P, NC_TOK)), np.where(s <= t if d == 0 else s >= t, 0.0, NEG)]
    put("is_fwd", (np.arange(8) < 4)[:, None].astype(np.float32))
    put("is_bwd", (np.arange(8) >= 4)[:, None].astype(np.float32))
    carry = np.ones(T)
    carry[0] = 0.0
    carry[NC_TOK::GLA_CHUNK] = 0.0
    put("gla_carry", np.tile(carry, (P, 1)))
    blk = p[:, None] // GLA_CHUNK == p[None, :] // GLA_CHUNK
    put("gla_mask0", (blk & (p[:, None] <= p[None, :])).astype(np.float32))
    put("gla_mask1", (blk & (p[:, None] >= p[None, :])).astype(np.float32))
    c = np.arange(GRID_W)
    start = np.clip(c - 8, 0, GRID_W - 16)
    ok = (c[None, :] >= start[:, None]) & (c[None, :] < start[:, None] + 16)
    put("na_mask", np.where(ok, 0.0, NEG)[p % GRID_W])
    return np.ascontiguousarray(np.concatenate(parts, 1).astype(np.float32)), at, np.concatenate(masks, 1).astype(np.float32)


def columns(v):
    return np.asarray(v).reshape(-1, P).T


SMALL = [("ada_b", 240), ("norm_g", 48), ("final_g", 8), ("diff_norm_g", 1),
         ("ml_norm_g", 4), ("conv_w", 12), ("conv_b", 4), ("gla_b", 8), ("gla_norm_g", 2),
         ("ln", 64), ("q_norm", 4), ("kv_norm", 2), ("na_b", 16), ("lambda", 4 * HD), ("gate_b", 2)]


def small_at():
    at, n = {}, 0
    for name, w in SMALL:
        at[name] = (n, n + w)
        n += w
    return at, n


def small_table(a):
    def flat(x):
        return columns(np.asarray(x).reshape(-1))

    gate = np.zeros((P, 2), np.float32)
    gate[:8] = np.asarray(a["mlstm_gate_b"]).reshape(2, 8).T
    qb = np.asarray(a["na_b_qkv_2"]).reshape(3, D)
    ln = np.stack([np.asarray(a[k]) for k in ("ln1_g_2", "ln1_b_2", "ln2_g_2", "ln2_b_2")], 1)
    parts = dict(
        ada_b=np.concatenate([flat(a["ada_b"]), flat(a["ada_b_2"])], 1), norm_g=flat(a["norm_g"]),
        final_g=flat(a["final_g"]), diff_norm_g=flat(a["diff_norm_g"]), ml_norm_g=flat(a["mlstm_norm_g"]),
        conv_w=flat(a["mlstm_conv_w"]), conv_b=flat(a["mlstm_conv_b"]), gla_b=flat(a["gla_b_gate"]),
        gla_norm_g=flat(a["gla_norm_g"]), ln=flat(ln), q_norm=flat(a["mla_q_norm_2"]), kv_norm=flat(a["mla_kv_norm_2"]),
        na_b=flat(qb[:2]), gate_b=gate,
    )
    parts["lambda"] = np.broadcast_to(np.asarray(a["diff_lambda"]).reshape(-1), (P, 4 * HD))
    return np.ascontiguousarray(np.concatenate([parts[n] for n, _ in SMALL], 1))


def slabs(w, k_tiles):
    K, N = w.shape
    cols = SLAB // k_tiles
    r = w.reshape(K // (P * k_tiles), k_tiles, P, N // cols, cols)
    return r.transpose(3, 0, 2, 1, 4).reshape(-1, P, SLAB)


def padded(w, cols=P):
    out = np.zeros((w.shape[0], cols), w.dtype)
    out[:, : w.shape[1]] = w
    return out


def chunks(up, down, n_up):
    n = len(down) // 2
    up, down = up.reshape(n, n_up, P, SLAB), down.reshape(n, 2, P, SLAB)
    between = np.concatenate([up[1:], down[:-1]], 1).reshape(-1, P, SLAB)
    return np.concatenate([up[0], between, down[-1]])


STREAM = [("ffn00", 66), ("even_fm", 18), ("even_tm", 8), ("even_out", 8), ("ffn01", 66),
          ("ffn10", 66), ("odd_fm", 18), ("odd_tm", 8), ("odd_out", 8), ("ffn11", 66),
          ("mla_down", 7), ("mla_uq", 6), ("mla_ukv", 4), ("mla_out", 8), ("mlp0", 64),
          ("na_fm", 16), ("na_tm", 8), ("na_out", 8), ("mlp1", 64)]
N_SLABS = sum(n for _, n in STREAM)


def weight_stream(a):
    f = lambda name: np.asarray(a[name])
    out = {}
    for l in range(2):
        for h in range(2):
            ab = f("ffn_w_in")[l, h].reshape(D, 2, FT, P).transpose(0, 2, 1, 3).reshape(D, 2 * FF)
            out[f"ffn{l}{h}"] = chunks(slabs(ab, 8), f("ffn_w_out")[l, h].reshape(FT, P, D), 4)
        out[f"mlp{l}"] = chunks(slabs(f("mlp_w1_2")[l], 8), f("mlp_w2_2")[l].reshape(FT2, P, D), 2)
    q, k, v, mqk, mv, mo, g = np.split(f("even_w_in")[0], np.cumsum([512] * 6), axis=1)
    out["even_fm"] = slabs(np.concatenate([q, k, mqk, mo, padded(g[:, :8]), padded(g[:, 8:])], 1), 8)
    out["even_tm"] = slabs(np.concatenate([v, mv], 1), 2)
    out["even_out"] = slabs(f("even_w_out")[0], 8)
    q, k, v, r, lr = np.split(f("odd_w_in")[0], np.cumsum([512, 512, 1024, 1024]), axis=1)
    out["odd_fm"] = slabs(np.concatenate([q, k, r, padded(lr[:, :16]), padded(lr[:, 16:])], 1), 8)
    out["odd_tm"] = slabs(v, 2)
    out["odd_out"] = slabs(f("odd_w_out")[0], 8)
    dkv = f("mla_w_dkv_2")[0]
    out["mla_down"] = slabs(np.concatenate([dkv[:, 256:], dkv[:, 256:], f("mla_w_dq_2")[0], dkv[:, :256]], 1), 8)
    uq = f("mla_w_uq_2")[0].reshape(512, 8, 192)
    out["mla_uq"] = slabs(np.concatenate([uq[..., :P].reshape(512, -1), uq[..., P:].reshape(512, -1)], 1), 4)
    ukv = f("mla_w_ukv_2")[0].reshape(256, 8, 2, P).transpose(0, 2, 1, 3).reshape(256, -1)
    out["mla_ukv"] = slabs(ukv, 2)
    out["mla_out"] = slabs(f("mla_w_o_2")[0], 8)
    qkv = f("na_w_qkv_2")[0]
    out["na_fm"] = slabs(qkv[:, : 2 * D], 8)
    out["na_tm"] = slabs(qkv[:, 2 * D:], 2)
    out["na_out"] = slabs(f("na_w_o_2")[0], 8)
    return np.concatenate([*[out[name] for name, _ in STREAM], np.zeros((1, P, SLAB), np.float32)])


def modulation_stream(a):
    w = [np.asarray(a[n])[l].T.reshape(-1, P, D) for n in ("ada_w", "ada_w_2") for l in range(2)]
    return np.concatenate(w)


def feature_major(x):
    return np.asarray(x).reshape(-1, DT, P).transpose(2, 1, 0)


def lay_out(a):
    x = np.concatenate([feature_major(np.asarray(a["ctx"])[0]), feature_major(np.asarray(a["x"])[0])], 2)
    out = {"weights": weight_stream(a), "ada": modulation_stream(a)}
    out["cond"] = np.stack([np.broadcast_to(np.asarray(a[n]).reshape(D), (P, D)) for n in ("c_ctx", "c", "c_ctx_2", "c_2")], 1)
    out["gla_gate"] = np.ascontiguousarray(np.asarray(a["gla_w_gate"])[0].transpose(1, 0, 2).reshape(16, D))
    out["na_rpb"] = np.ascontiguousarray(np.asarray(a["na_rpb_2"])[0][:, ::-1, ::-1])
    out["na_bv"] = np.ascontiguousarray(np.broadcast_to(np.asarray(a["na_b_qkv_2"])[0, 2 * D:], (P, D)))
    out["tokens"] = np.ascontiguousarray(x)
    out["ctx_2"] = np.ascontiguousarray(feature_major(np.asarray(a["ctx_2"])[0]))
    out["small"] = small_table(a)
    out["constants"], _, masks = constant_table()
    out["ml_masks"] = masks
    return out


class Model:

    def __init__(self, nc, stack, w, out):
        self.nc, self.w, self.out = nc, w, out
        self.stack, self.stage_stack = stack, None
        self.q = Queues(nc, stack)
        self.c_at = constant_table()[1]
        self.s_at, n_small = small_at()
        sb = self.sb
        self.const = sb("const", (P, max(b for _, b in self.c_at.values())))
        self.small = sb("small", (P, n_small))
        self.x = sb("x_res", (P, DT, T))
        self.hh = sb("h_high", (P, DT, T), F32R)
        self.hl = sb("h_low", (P, DT, T), F32R)
        self.mods = sb("mods", (P, 240, 2))
        self.scales = sb("scales", (P, DT, 2))
        self.gates = sb("gates", (P, DT, 2))
        self.rstd = sb("rstd", (P, T))
        self.stat = sb("stat", (P, T))
        self.fcol = sb("fcol", (P, TT * 8))
        self.neg_lam = sb("neg_lam", (P, 4))
        self.cols = [Slot(sb(f"cols{i}", (P, 8))) for i in range(6)]
        self.cols_at = 0
        self.raw = [Slot(sb(f"raw{i}", (P, SLAB))) for i in range(RAW_SLOTS)]
        self.raw_sem = [self.q.sem(f"raw{i}_loaded") for i in range(RAW_SLOTS)]
        self.split = [Slot(sb(f"split_high{i}", (P, SLAB), F32R), sb(f"split_low{i}", (P, SLAB), F32R))
                      for i in range(SPLIT_SLOTS)]
        self.slab_no, self.per_turn, self.fetched = 0, 0, 0
        self.temp = [Slot(sb(f"temp{i}", (P, T))) for i in range(6)]
        self.square = [Slot(sb(f"square{i}", (P, T))) for i in range(2)]
        self.temp_at = 0
        self.bank = [Slot(stack.enter_context(nc.psum_tensor(f"bank{i}", [P, 512], F32))) for i in range(8)]
        self.bank_at = 0
        self.ring = range(8)
        self.load_sem = self.q.sem("inputs_loaded")
        self.store_sem = self.q.sem("output_stored")
        self.side_sem = self.q.sem("side_loaded")
        self.ada_sem = [self.q.sem(f"ada{i}_loaded") for i in range(ADA_SLOTS)]
        self.bias_sem = [self.q.sem(f"bias{i}_loaded") for i in range(2)]
        self.ada_col = Slot(sb("ada_col", (P, 16, 2)))
        self.ada_no = 0
        self.scales_free, self.gates_free, self.rstd_free, self.h_free, self.x_free = [], [], [], [], []
        self.region_free = []

    def sb(self, name, shape, dtype=F32):
        return (self.stage_stack or self.stack).enter_context(self.nc.sbuf_tensor(f"sb_{name}", list(shape), dtype))

    @contextmanager
    def stage(self):
        with ExitStack() as own:
            self.stage_stack = own
            yield
            self.stage_stack = None

    def C(self, name, rows=P):
        a, b = self.c_at[name]
        return self.const[0:rows, a:b]

    def S(self, name, j=0, n=None):
        a, b = self.s_at[name]
        return self.small[:, a + j:(a + j + n if n else b)]

    def free(self, slot):
        return slot.free(self.q.loop_now)

    def next_bank(self):
        b = self.bank[self.ring[self.bank_at % len(self.ring)]]
        self.bank_at += 1
        return b

    def next_temp(self):
        b = self.temp[self.temp_at % len(self.temp)]
        self.temp_at += 1
        return b

    def next_cols(self):
        b = self.cols[self.cols_at % len(self.cols)]
        self.cols_at += 1
        return b

    @contextmanager
    def turns(self, n, slabs):
        assert slabs % RAW_SLOTS == 0 and slabs % SPLIT_SLOTS == 0 and self.fetched == self.slab_no + AHEAD
        start, self.per_turn = self.slab_no, slabs
        with self.q.loop(n):
            yield
            assert self.slab_no == start + slabs
        self.slab_no, self.per_turn = start + n * slabs, 0
        self.fetched = self.slab_no + AHEAD

    def prefetch(self, s):
        if s >= N_SLABS or s < self.fetched:
            return
        self.fetched = s + 1
        q, nc, step = self.q, self.nc, self.per_turn
        raw, sem, part = self.raw[s % RAW_SLOTS], self.raw_sem[s % RAW_SLOTS], self.split[s % SPLIT_SLOTS]

        def load(i):
            src = self.w["weights"]
            src = src[s, :, :] if step == 0 else src[bass.ds(i * step + s, 1), :, :].rearrange("a p n -> p (a n)")
            return nc.sync.dma_start(raw.ap[:, :], src)

        loaded = q.dma(load, sem, self.free(raw))
        high = q.act(op(nc.scalar.activation, part.ap[:, :], raw.ap[:, :], ACT.Identity), loaded, self.free(part))
        low = q.dve(op(nc.vector.tensor_tensor, part.low[:, :], raw.ap[:, :], part.ap[:, :].bitcast(F32), ALU.subtract), high)
        raw.free_after(low)
        part.loaded.set(low)

    def next_slab(self, fetch=True):
        s = self.slab_no
        self.slab_no += 1
        if fetch:
            self.prefetch(s + AHEAD)
        part = self.split[s % SPLIT_SLOTS]
        return part.ap, part.low, part.loaded.get(self.q.loop_now), part

    def matmuls(self, out, pairs, *waits, ready=None):
        nc, n = self.nc, len(pairs)
        for j, (a, b) in enumerate(pairs):
            t = self.q.pe(op(nc.tensor.matmul, out, a, b, start=(j == 0), stop=(j == n - 1)),
                          *(waits if j == 0 else ()), ready[j] if ready else [], signal=(j == n - 1))
        return t

    def products(self, out, terms, *waits, start=True, stop=True, signal=True, ready=None):
        nc = self.nc
        passes = [p for ah, al, bh, bl in terms for p in ((ah, bh), (ah, bl), (al, bh))]
        for j, (a, b) in enumerate(passes):
            last = j == len(passes) - 1
            t = self.q.pe(op(nc.tensor.matmul, out, a, b, start=(start and j == 0), stop=(stop and last)),
                          *(waits if j == 0 else ()), ready[j // 3] if ready and j % 3 == 0 else [],
                          signal=(signal and last))
        return t

    def put_h(self, k, cols, src, *ready):
        q, nc = self.q, self.nc
        high = q.act(op(nc.scalar.activation, self.hh[:, k, cols], src, ACT.Identity), *ready, self.h_free)
        low = q.dve(op(nc.vector.tensor_tensor, self.hl[:, k, cols], src, self.hh[:, k, cols].bitcast(F32), ALU.subtract), high)
        self.h_ready[k] = [low]
        return low

    def load_inputs(self):
        q, nc = self.q, self.nc
        q.dma(op(nc.sync.dma_start, self.small[:, :], self.w["small"]), self.load_sem)
        q.dma(op(nc.sync.dma_start, self.const[:, :], self.w["constants"]), self.load_sem)
        t = q.dma(op(nc.sync.dma_start, self.x[:, :, :], self.w["tokens"]), self.load_sem)
        self.ready = [t]
        self.x_ready = [[t] for _ in range(DT)]
        self.h_ready = [[] for _ in range(DT)]

    def open_modulation(self, block):
        q, nc = self.q, self.nc
        self.ada = [Slot(self.sb(f"ada{i}_{self.ada_no}", (P, D))) for i in range(ADA_SLOTS)]
        self.ada_junk = [Slot(self.sb(f"ada_junk{s}_{self.ada_no}", (P, D), mybir.dt.bfloat16)) for s in range(2)]
        self.cond = self.sb(f"cond_{self.ada_no}", (P, 2, D))
        for s in [*self.ada, *self.ada_junk]:
            s.free_after(*self.region_free)
        load = q.dma(op(nc.sync.dma_start, self.cond[:, :, :], self.w["cond"][:, 2 * block:2 * block + 2, :]),
                     self.side_sem, self.region_free)
        self.cond_ready = q.act(op(nc.scalar.activation, self.cond[:, :, :], self.cond[:, :, :], ACT.Silu), load)

    def modulation_tile(self, j, step):
        q, nc, n = self.q, self.nc, self.ada_no
        slot, sem = self.ada[j % ADA_SLOTS], self.ada_sem[j % ADA_SLOTS]
        queue = ("gpsimd", "sync")[j % ADA_SLOTS % 2]
        self.ada_no += 1

        def load(i):
            src = self.w["ada"]
            src = src[n, :, :] if step == 0 else src[bass.ds(i * step + n, 1), :, :].rearrange("a p n -> p (a n)")
            return (nc.gpsimd if queue == "gpsimd" else nc.sync).dma_start(slot.ap[:, :], src)

        loaded = q.dma(load, sem, self.free(slot), engine=queue)
        for s, junk in enumerate(self.ada_junk):
            t = q.dve(op(nc.vector.tensor_tensor_reduce, out=junk.ap[:, :], in0=slot.ap[:, :], in1=self.cond[:, s, :],
                         scale=1.0, scalar=0.0, op0=ALU.mult, op1=ALU.add, accum_out=self.ada_col.ap[:, j, s:s + 1]),
                      loaded, self.cond_ready, self.free(junk), self.free(self.ada_col) if j == 0 else [])
            junk.free_after(t)
        slot.free_after(t)
        return t

    def modulation_finish(self, n, step, done):
        q, nc, first = self.q, self.nc, self.ada_no - n
        cols = self.S("ada_b")

        def add(i):
            at = first if step == 0 else i * step + first
            b = cols[:, at:at + n] if step == 0 else cols[:, bass.ds(at, n)]
            m = self.mods[:, at:at + n, :] if step == 0 else self.mods[:, bass.ds(at, n), :]
            return nc.vector.tensor_tensor(m, self.ada_col.ap[:, 0:n, :],
                                           b.rearrange("p (t o) -> p t o", o=1).broadcast_to([P, n, 2]), ALU.add)

        self.mods_ready = q.dve(add, done, self.ready)
        self.ada_col.free_after(self.mods_ready)

    def modulation(self, n):
        for j in range(n):
            t = self.modulation_tile(j % 16, 0)
            if j % 16 == 15 or j == n - 1:
                self.modulation_finish(j % 16 + 1, 0, t)

    def scale_and_shift(self, first, shift, scale, g):
        q, nc = self.q, self.nc
        sc = self.mods[:, first + scale * DT:first + (scale + 1) * DT, :]
        if g is None:
            t = q.dve(op(nc.vector.tensor_scalar, self.scales[:, :, :], sc, 1.0, None, ALU.add),
                      self.mods_ready, self.scales_free)
        else:
            gb = g.rearrange("p (t o) -> p t o", o=1).broadcast_to([P, DT, 2])
            t = q.dve(op(nc.vector.scalar_tensor_tensor, self.scales[:, :, :], sc, 1.0, gb, ALU.add, ALU.mult),
                      self.mods_ready, self.scales_free)
        self.scales_ready = t
        self.shift = lambda k, s: self.mods[:, first + shift * DT + k, s:s + 1]

    def gate(self, first, gate, factor=1.0):
        q, nc = self.q, self.nc
        src = self.mods[:, first + gate * DT:first + (gate + 1) * DT, :]
        self.gates_ready = q.dve(op(nc.vector.tensor_scalar, self.gates[:, :, :], src, factor, None, ALU.mult),
                                 self.mods_ready, self.gates_free)

    def inverse_rms(self, tiles, dim, eps, cols, ready):
        q, nc = self.q, self.nc
        n = cols.stop - cols.start
        bank = self.next_bank()
        free = self.free(bank)
        for k, src in enumerate(tiles):
            tmp = self.square[k % 2]
            sq = q.act(op(nc.scalar.activation, tmp.ap[:, 0:n], src, ACT.Square), self.free(tmp), ready[k])
            done = q.pe(op(nc.tensor.matmul, bank.ap[:, 0:n], self.C("ones"), tmp.ap[:, 0:n],
                           start=(k == 0), stop=(k == len(tiles) - 1)), sq, free, self.ready)
            tmp.free_after(done)
        a = q.dve(op(nc.vector.tensor_scalar, self.stat[:, 0:n], bank.ap[:, 0:n], 1.0 / dim, eps, ALU.mult, ALU.add), done)
        bank.free_after(a)
        b = q.act(op(nc.scalar.activation, self.stat[:, 0:n], self.stat[:, 0:n], ACT.Sqrt), a)
        return q.dve(op(nc.vector.reciprocal, self.rstd[:, 0:n], self.stat[:, 0:n]), b, self.rstd_free)

    def ada_norm(self, streams):
        q, nc = self.q, self.nc
        lo = streams[0][1].start
        cols = slice(lo, T)
        r = self.inverse_rms([self.x[:, k, cols] for k in range(DT)], D, RMS_EPS, cols, self.x_ready)
        shift = self.shift

        def scaled(k):
            tmp = self.next_temp()
            free = self.free(tmp)
            for s, c in streams:
                y = tmp.ap[:, c.start - lo:c.stop - lo]
                a = q.dve(op(nc.vector.scalar_tensor_tensor, y, self.x[:, k, c], self.scales[:, k, s:s + 1],
                             self.rstd[:, c.start - lo:c.stop - lo], ALU.mult, ALU.mult), r, self.x_ready[k], self.scales_ready, free)
                b = q.act(op(nc.scalar.activation, self.hh[:, k, c], y, ACT.Identity, bias=shift(k, s)), a, self.h_free)
            self.rstd_free = self.scales_free = [a]
            return tmp, b

        def rest(k, got):
            tmp, high = got
            for s, c in streams:
                h = q.dve(op(nc.vector.scalar_tensor_tensor, self.hl[:, k, c], tmp.ap[:, c.start - lo:c.stop - lo], shift(k, s),
                             self.hh[:, k, c].bitcast(F32), ALU.add, ALU.subtract), high)
            tmp.free_after(h)
            self.h_ready[k] = [h]

        self.in_order(range(DT), scaled, None, rest)

    def h_term(self, k, lo=0, hi=T):
        return self.hh[:, k, lo:hi], self.hl[:, k, lo:hi]

    def add_to_x(self, k, bank, streams, done):
        q, nc = self.q, self.nc
        lo = streams[0][1].start
        for s, c in streams:
            x = self.x[:, k, c]
            a = q.dve(op(nc.vector.scalar_tensor_tensor, x, bank.ap[:, c.start - lo:c.stop - lo], self.gates[:, k, s:s + 1], x,
                         ALU.mult, ALU.add), done, self.gates_ready, self.x_free)
        bank.free_after(a)
        self.x_ready[k], self.gates_free = [a], [a]

    def project_out(self, streams):
        lo = streams[0][1].start
        for j in range(DT):
            wh, wl, loaded, slot = self.next_slab()
            bank = self.bank[j % 3]
            done = self.products(bank.ap[:, 0:T - lo], [
                (wh[:, k * P:(k + 1) * P], wl[:, k * P:(k + 1) * P], *self.h_term(k, lo)) for k in range(DT)],
                loaded, self.free(bank), ready=self.h_ready)
            slot.free_after(done)
            self.add_to_x(j, bank, streams, done)
        self.h_free = [done]

    def feed_forward(self, kind, streams, ada):
        q, nc = self.q, self.nc
        lo = streams[0][1].start
        n = T - lo
        turns, per_turn, slabs = (5, 2, 12) if kind == "swiglu" else (5, 3, 12)
        hidden = [[Slot(self.sb(f"hidden_high{c}{t}_{self.slab_no}", (P, T), F32R),
                        self.sb(f"hidden_low{c}{t}_{self.slab_no}", (P, T), F32R)) for t in range(2)] for c in range(per_turn)]
        for pair in hidden:
            for hid in pair:
                hid.free_after(*self.region_free)
        ada_at = [0, 0, None]
        share = [0, 1]

        def some_ada():
            share[0] += 1
            while ada_at[0] * share[1] < ada_at[1] * share[0]:
                ada_at[2] = self.modulation_tile(ada_at[0], ada_at[1])
                ada_at[0] += 1

        def product_up(bank):
            wh, wl, loaded, slot = self.next_slab()
            done = self.products(bank.ap[:, 0:n], [
                (wh[:, k * P:(k + 1) * P], wl[:, k * P:(k + 1) * P], *self.h_term(k, lo)) for k in range(DT)],
                loaded, self.free(bank), ready=self.h_ready)
            slot.free_after(done)
            self.h_free = [done]
            return done

        def up(pair):
            for t, hid in enumerate(pair):
                temp, bank = self.temp[t], self.bank[0 if kind == "swiglu" else t]
                done = product_up(bank)
                if kind == "swiglu":
                    b_bank = self.bank[1]
                    a = q.act(op(nc.scalar.activation, temp.ap[:, 0:n], bank.ap[:, 0:n], ACT.Silu), done, self.free(temp))
                    bank.free_after(a)
                    some_ada()
                    b_done = product_up(b_bank)
                    b = q.dve(op(nc.vector.tensor_tensor, temp.ap[:, 0:n], temp.ap[:, 0:n], b_bank.ap[:, 0:n], ALU.mult), a, b_done)
                    b_bank.free_after(b)
                else:
                    a = q.act(op(nc.scalar.activation, temp.ap[:, 0:n], bank.ap[:, 0:n], ACT.Relu), done, self.free(temp))
                    bank.free_after(a)
                    b = q.pool(op(nc.gpsimd.tensor_tensor, temp.ap[:, 0:n], temp.ap[:, 0:n], temp.ap[:, 0:n], ALU.mult), a)
                high = q.act(op(nc.scalar.activation, hid.ap[:, 0:n], temp.ap[:, 0:n], ACT.Identity), b, self.free(hid))
                low = q.dve(op(nc.vector.tensor_tensor, hid.low[:, 0:n], temp.ap[:, 0:n], hid.ap[:, 0:n].bitcast(F32), ALU.subtract), high)
                temp.free_after(low)
                hid.loaded.set(low)
                some_ada()

        def down(pair):
            slabs = [self.next_slab(fetch=False), self.next_slab(fetch=False)]
            for group in range(2):
                for t, (wh, wl, loaded, slot) in enumerate(slabs):
                    for j in range(4):
                        k, bank = 4 * group + j, self.bank[2 + (4 * group + j) % 6]
                        done = self.products(bank.ap[:, 0:n], [
                            (wh[:, k * P:(k + 1) * P], wl[:, k * P:(k + 1) * P], pair[t].ap[:, 0:n], pair[t].low[:, 0:n])],
                            loaded, pair[t].loaded.get(q.loop_now), self.free(bank) if t == 0 else [], start=(t == 0),
                            stop=(t == 1), signal=(t == 1 or (group == 1 and j == 3)))
                        if t == 1:
                            self.add_to_x(k, bank, streams, done)
                    if group == 1:
                        slot.free_after(done)
                        pair[t].free_after(done)
                        if t == 0:
                            self.prefetch(self.slab_no + AHEAD - 1)
                if group == 0:
                    self.prefetch(self.slab_no + AHEAD - 2)
                some_ada()

        up(hidden[0])
        with self.turns(turns, slabs):
            ada_at[:], share[:] = [0, ada, None], [0, per_turn * (6 if kind == "swiglu" else 4)]
            for c in range(per_turn):
                up(hidden[(c + 1) % per_turn])
                down(hidden[c])
            if ada:
                self.modulation_finish(ada, ada, ada_at[2])
        self.ada_no += (turns - 1) * ada
        ada_at[:] = [0, 0, None]
        down(hidden[0])
        self.region_free = [*self.x_ready, *self.h_free]

    def token_major(self, first):
        return self.big[:, first:first + 8, :].rearrange("p a n -> p (a n)").rearrange("p (t n) -> p t n", t=TT)

    def project_fm(self, n_tiles, first, lo=0, bias=None):
        q, nc = self.q, self.nc
        n = T - lo
        last, big = {}, self.big

        def tile_out(j, tile):
            wh, wl, loaded, slot = self.next_slab()
            bank = self.bank[j % 3]
            done = self.products(bank.ap[:, 0:n], [
                (wh[:, k * P:(k + 1) * P], wl[:, k * P:(k + 1) * P], *self.h_term(k, lo)) for k in range(DT)],
                loaded, self.free(bank), ready=self.h_ready)
            slot.free_after(done)

            def copy(i):
                k = tile(i)
                dst = big[:, k + first, lo:T] if isinstance(k, int) else \
                    big[:, bass.ds(k + first, 1), lo:T].rearrange("p a n -> p (a n)")
                b = None if bias is None else bias[:, k:k + 1] if isinstance(k, int) else bias[:, bass.ds(k, 1)]
                if j % 2 == 0:
                    return nc.scalar.activation(dst, bank.ap[:, 0:n], ACT.Identity, **({} if b is None else {"bias": b}))
                if b is None:
                    return nc.vector.tensor_copy(dst, bank.ap[:, 0:n])
                return nc.vector.tensor_scalar(dst, bank.ap[:, 0:n], b, None, ALU.add)

            last[j % 2] = (q.act if j % 2 == 0 else q.dve)(copy, done, self.region_free)
            bank.free_after(last[j % 2])
            return done

        first_slabs = n_tiles if n_tiles < 3 * RAW_SLOTS else n_tiles % RAW_SLOTS + RAW_SLOTS
        for j in range(first_slabs):
            done = tile_out(j, lambda i, j=j: j)
        if first_slabs < n_tiles:
            with self.turns((n_tiles - first_slabs) // RAW_SLOTS, RAW_SLOTS):
                for j in range(first_slabs, first_slabs + RAW_SLOTS):
                    done = tile_out(j, lambda i, j=j: i * RAW_SLOTS + j)
        return list(last.values()), done

    def project_tm(self, groups, dst, dst_free, first=0, k_slabs=4, bias=None):
        q, nc = self.q, self.nc
        last = {}
        for g in range(groups):
            banks = [self.bank[4 * (g % 2) + tt] for tt in range(TT)]
            for s in range(k_slabs):
                wh, wl, loaded, slot = self.next_slab()
                for tt, bank in enumerate(banks):
                    terms = []
                    for k in range(2):
                        hh, hl = self.h_term(first + 2 * s + k)
                        c = slice(tt * P, (tt + 1) * P)
                        terms.append((hh[:, c], hl[:, c], wh[:, k * 512:(k + 1) * 512], wl[:, k * 512:(k + 1) * 512]))
                    k0 = first + 2 * s
                    done = self.products(bank.ap[:, :], terms, loaded, self.free(bank) if s == 0 else [],
                                         ready=self.h_ready[k0:k0 + 2], start=(s == 0), stop=(s == k_slabs - 1))
                    if s == k_slabs - 1:
                        if bias is not None:
                            e = q.dve(op(nc.vector.tensor_tensor, dst(tt, g), bank.ap[:, :], bias[:, g * 512:(g + 1) * 512], ALU.add), done, dst_free)
                            last[0] = e
                        elif tt % 2:
                            last[1] = e = q.act(op(nc.scalar.activation, dst(tt, g), bank.ap[:, :], ACT.Identity), done, dst_free)
                        else:
                            last[0] = e = q.dve(op(nc.vector.tensor_copy, dst(tt, g), bank.ap[:, :]), done, dst_free)
                        bank.free_after(e)
                slot.free_after(done)
        return list(last.values()), done

    def store_output(self, src, ready):
        q, nc = self.q, self.nc
        t = q.dma(op(nc.sync.dma_start, self.out, src), self.store_sem, ready)
        q.add("sync", op(nc.sync.nop), [t], None, 0)

    def transpose_weights(self, w, qt, n_keys, w_t, w_ready, wt_free):
        q, nc = self.q, self.nc
        bank = self.next_bank()
        free = self.free(bank)
        nk = n_keys // P
        for kt in range(nk):
            done = q.pe(op(nc.tensor.transpose, bank.ap[:, kt * P:(kt + 1) * P], w[:, kt * P:(kt + 1) * P], self.C("ident")),
                w_ready, free, signal=(kt == nk - 1))
        copy = q.act(op(nc.scalar.activation, w_t[:, 0:nk, qt * P:(qt + 1) * P], bank.ap[:, 0:nk * P].rearrange("p (k n) -> p k n", k=nk), ACT.Identity),
            done, wt_free)
        bank.free_after(copy)
        return done, copy

    def weigh_values(self, value, w_t, ready, lo=0):
        q, nc = self.q, self.nc
        bank = self.next_bank()
        free = self.free(bank)
        for kt in range(TT):
            c = slice(lo if kt < NC_TOK // P else NC_TOK, T)
            done = q.pe(op(nc.tensor.matmul, bank.ap[:, c], value(kt), w_t[:, kt, c], start=(kt == 0), stop=(kt == TT - 1)),
                ready, free, signal=(kt == TT - 1))
        return bank, done

    def in_order(self, units, *stages):
        n, held, steps = len(units), {}, []
        for i in range(n + len(stages) - 1):
            due = [rest.pop(0) for rest in steps if rest]
            for k in range(len(stages) - 1, -1, -1):
                if not 0 <= i - k < n:
                    continue
                u = i - k
                if k == 0:
                    held[u] = stages[0](units[u])
                elif k == len(stages) - 1:
                    more = stages[k](units[u], held.pop(u))
                    for step in due:
                        step()
                    due = []
                    steps.append(list(more or []))
                elif stages[k]:
                    held[u] = stages[k](units[u], held[u])
        while any(steps):
            for rest in steps:
                if rest:
                    rest.pop(0)()

    def scale_first(self, pair, n, coef, ready):
        nc = self.nc
        return self.q.pool(op(nc.gpsimd.tensor_scalar, pair[0].ap[:, 0:n], pair[0].ap[:, 0:n], coef[:, 0:1], None, ALU.mult), ready)

    def add_second(self, pair, n, col, coef, ready):
        nc = self.nc
        a = self.q.dve(op(nc.vector.scalar_tensor_tensor, pair[0].ap[:, 0:n], pair[1].ap[:, 0:n], coef[:, 1:2], pair[0].ap[:, 0:n],
                          ALU.mult, ALU.add), ready)
        col.free_after(a)
        pair[1].free_after(a)
        return a

    def rope(self, tile, ready):
        q, nc = self.q, self.nc
        x = self.big[:, tile, LAT]
        bank, tmp = self.next_bank(), self.next_temp()
        sw = self.matmuls(bank.ap[:, 0:NX_TOK], [(self.C("swap"), x)], ready, self.free(bank))
        a = q.dve(op(nc.vector.tensor_tensor, tmp.ap[:, 0:NX_TOK], bank.ap[:, 0:NX_TOK], self.C("sin"), ALU.mult),
                  sw, self.free(tmp))
        bank.free_after(a)
        b = q.pool(op(nc.gpsimd.tensor_tensor, x, x, self.C("cos"), ALU.mult), sw)
        c = q.pool(op(nc.gpsimd.tensor_tensor, x, x, tmp.ap[:, 0:NX_TOK], ALU.add), a, b)
        tmp.free_after(c)
        return c

    def even_mixer(self):
        q, nc = self.q, self.nc
        Q0, K0, MQK0, OP0, GATES, V0, WT = 0, 4, 8, 12, 16, 18, (26, 30)
        self.big = self.sb("even_big", (P, 34, T))
        masks = self.sb("ml_masks", (P, 4 * T))
        masks_ready = q.dma(op(nc.sync.dma_start, masks[:, :], self.w["ml_masks"]), self.side_sem, self.region_free)
        fm, _ = self.project_fm(18, 0)
        vals = self.token_major(V0)
        tm, done = self.project_tm(2, lambda tt, g: vals[:, tt, g * 512:(g + 1) * 512], self.region_free)
        self.h_free = [done]
        row_tile = (GATES, GATES + 1, WT[1], WT[1] + 1)
        rows = lambda r: self.big[0:8, row_tile[r], :]
        for r in range(2):
            t = q.act(op(nc.scalar.activation, rows(r), rows(r), ACT.Identity, bias=self.S("gate_b", r, 1)[0:8, :]), fm, self.region_free)
        g_ready, f_ready = self.forget_sums(rows, t)
        lam = self.diff_lambda()

        for j in range(4):
            t = q.pool(op(nc.gpsimd.tensor_scalar, self.big[:, Q0 + j, :], self.big[:, Q0 + j, :], HD ** -0.5, None, ALU.mult), fm)
        roped = [self.rope(Q0 + j, [t, *fm]) for j in range(8)]
        conv = self.conv_silu(MQK0, WT[0], fm)
        for j in range(4):
            og = q.act(op(nc.scalar.activation, self.big[:, OP0 + j, :], self.big[:, OP0 + j, :], ACT.Sigmoid), fm)

        wt_free = [conv, [g_ready, f_ready]]
        n_keys = lambda qt: NC_TOK if qt < NC_TOK // P else T

        w_t = [self.big[:, at:at + TT, :] for at in WT]
        copies = [[] for _ in range(4)]
        def scores(unit):
            hd, qt = unit
            n, turn_no = n_keys(qt), hd * TT + qt
            pair = self.temp[2 * (turn_no % 3):2 * (turn_no % 3) + 2]
            col = self.next_cols()
            free = self.free(col)
            for c in range(2):
                bank = self.next_bank()
                s = self.matmuls(bank.ap[:, 0:n], [(
                    self.big[HD * c:HD * c + HD, Q0 + hd, qt * P:(qt + 1) * P],
                    self.big[HD * c:HD * c + HD, K0 + hd, 0:n])], roped, self.free(bank))
                m = q.dve(op(nc.vector.tensor_reduce, col.ap[:, c:c + 1], bank.ap[:, 0:n], AX.X, ALU.max, negate=True), s, free)
                e = q.act(op(nc.scalar.activation, pair[c].ap[:, 0:n], bank.ap[:, 0:n], ACT.Exp, bias=col.ap[:, c:c + 1],
                    accum_out=col.ap[:, 2 + c:3 + c]), m, self.free(pair[c]))
                bank.free_after(e)
            return pair, col, e

        def normalise(unit, got):
            (hd, qt), (pair, col, e) = unit, got
            r = q.dve(op(nc.vector.reciprocal, col.ap[:, 4:6], col.ap[:, 2:4]), e)
            r2 = q.dve(op(nc.vector.tensor_tensor, col.ap[:, 5:6], col.ap[:, 5:6], self.neg_lam[:, 0:1], ALU.mult), r, lam)
            return pair, col, [r2, self.scale_first(pair, n_keys(qt), col.ap[:, 4:6], [r2, e])]

        def combine(unit, got):
            pair, col, ready = got
            return pair[0], self.add_second(pair, n_keys(unit[1]), col, col.ap[:, 4:6], ready)

        def turn(unit, got):
            (hd, qt), (w, ready) = unit, got
            done, copy = self.transpose_weights(w.ap, qt, n_keys(qt), w_t[hd % 2], ready, wt_free[hd % 2])
            w.free_after(done)
            copies[hd].append(copy)
            if qt == TT - 1:
                return [lambda: weigh(hd), lambda: add_squares(hd)]

        def weigh(hd):
            bank, done = self.weigh_values(lambda kt: vals[:, kt, hd * P:(hd + 1) * P], w_t[hd % 2], copies[hd] + tm)
            wt_free[hd % 2] = done
            outs[hd] = q.act(op(nc.scalar.activation, self.big[:, Q0 + hd, :], bank.ap[:, :], ACT.Identity), done)
            bank.free_after(outs[hd])

        def add_squares(j):
            sq = self.square[j % 2]
            a = q.act(op(nc.scalar.activation, sq.ap[:, :], self.big[:, y_tiles[j], :], ACT.Square), outs[j], self.free(sq))
            squares[0] = q.pe(op(nc.tensor.matmul, sum_bank.ap[0:8, :], self.C("row_of")[:, 8 * j:8 * j + 8], sq.ap[:, :],
                                 start=(j == 0), stop=(j == 7)), a, sum_free)
            sq.free_after(squares[0])

        y_tiles = [*range(Q0, Q0 + 4), *range(K0, K0 + 4)]
        squares, sum_bank, sum_free = [None], self.bank[5], self.free(self.bank[5])
        self.ring = range(5)
        self.bank_at = 0
        outs = {}
        self.in_order([(hd, qt) for hd in range(4) for qt in range(TT)], scores, normalise, combine, turn)

        copies = [[] for _ in range(4)]
        g_all = {}
        def weights(unit):
            hd, qt = unit
            n, turn_no, base = n_keys(qt), hd * TT + qt, HD * (hd % 2)
            if qt == 0:
                for d in range(2):
                    row, g_bank = 4 * d + hd, self.bank[6 + d]
                    g_all[hd] = self.matmuls(g_bank.ap[:, :], [(self.C("ident")[0:8, row:row + 1].broadcast_to([8, P]), rows(0))],
                                             g_ready, self.free(g_bank))
            pair = self.temp[2 * (turn_no % 3):2 * (turn_no % 3) + 2]
            col = self.next_cols()
            free = self.free(col)
            bank = self.next_bank()
            s = self.matmuls(bank.ap[:, 0:n], [(
                self.big[base:base + HD, MQK0 + hd // 2, qt * P:(qt + 1) * P],
                self.big[base:base + HD, MQK0 + 2 + hd // 2, 0:n])], conv, self.free(bank))
            exps = []
            for d in range(2):
                end = (2 * d + qt % 2 + 1) * T
                a = q.dve(op(nc.vector.tensor_tensor, pair[d].ap[:, 0:n], self.bank[6 + d].ap[:, 0:n], masks[:, end - n:end], ALU.add),
                          g_all[hd], masks_ready, self.free(pair[d]))
                m = q.dve(op(nc.vector.tensor_reduce, col.ap[:, d:d + 1], pair[d].ap[:, 0:n], AX.X, ALU.max, negate=True), a, free)
                exps.append(q.act(op(nc.scalar.activation, pair[d].ap[:, 0:n], pair[d].ap[:, 0:n], ACT.Exp, bias=col.ap[:, d:d + 1]), m))
            if qt == TT - 1:
                for d in range(2):
                    self.bank[6 + d].free_after(a)
            return pair, col, bank, s, m, exps

        def normalise(unit, got):
            (hd, qt), (pair, col, bank, s, m, exps) = unit, got
            n = n_keys(qt)
            f = self.fcol[:, qt * 8:(qt + 1) * 8].rearrange("p (d h) -> p h d", d=2)[:, hd, :]
            b = q.dve(op(nc.vector.tensor_tensor, col.ap[:, 2:4], col.ap[:, 0:2], f, ALU.subtract), m, f_ready)
            b = q.dve(op(nc.vector.tensor_scalar, col.ap[:, 2:4], col.ap[:, 2:4], 80.0, None, ALU.min), b)
            b = q.act(op(nc.scalar.activation, col.ap[:, 2:4], col.ap[:, 2:4], ACT.Exp), b)
            for d in range(2):
                w = q.dve(op(nc.vector.scalar_tensor_tensor, pair[d].ap[:, 0:n], bank.ap[:, 0:n], HD ** -0.5, pair[d].ap[:, 0:n], ALU.mult, ALU.mult,
                    accum_out=col.ap[:, 4 + d:5 + d]), s, exps[d])
            bank.free_after(w)
            c = q.dve(op(nc.vector.scalar_tensor_tensor, col.ap[:, 6:8], col.ap[:, 4:6], -1.0, col.ap[:, 4:6], ALU.mult, ALU.max), w)
            c = q.dve(op(nc.vector.tensor_tensor, col.ap[:, 6:8], col.ap[:, 6:8], col.ap[:, 2:4], ALU.max), c, b)
            c = q.dve(op(nc.vector.reciprocal, col.ap[:, 6:8], col.ap[:, 6:8]), c)
            return pair, col, [c, self.scale_first(pair, n, col.ap[:, 6:8], [c])]

        def combine(unit, got):
            pair, col, ready = got
            return pair[0], self.add_second(pair, n_keys(unit[1]), col, col.ap[:, 6:8], ready)

        def turn(unit, got):
            (hd, qt), (w, ready) = unit, got
            done, copy = self.transpose_weights(w.ap, qt, n_keys(qt), w_t[hd % 2], ready, wt_free[hd % 2])
            w.free_after(done)
            copies[hd].append(copy)
            if qt == TT - 1:
                return [lambda: weigh(hd), lambda: add_squares(4 + hd)]

        def weigh(hd):
            bank, done = self.weigh_values(lambda kt: vals[:, kt, 512 + hd * P:512 + (hd + 1) * P], w_t[hd % 2], copies[hd] + tm)
            wt_free[hd % 2] = done
            outs[4 + hd] = q.act(op(nc.scalar.activation, self.big[:, K0 + hd, :], bank.ap[:, :], ACT.Identity), done)
            bank.free_after(outs[4 + hd])

        self.in_order([(hd, qt) for hd in range(4) for qt in range(TT)], weights, normalise, combine, turn)
        stat = rows(1)
        a = q.dve(op(nc.vector.tensor_scalar, stat, sum_bank.ap[0:8, :], 1.0 / P, RMS_EPS, ALU.mult, ALU.add), squares[0], g_ready, f_ready)
        sum_bank.free_after(a)
        a = q.act(op(nc.scalar.activation, stat, stat, ACT.Sqrt), a)
        inverse = q.dve(op(nc.vector.reciprocal, stat, stat), a)

        def spread(j):
            bank = self.next_bank()
            return bank, self.matmuls(bank.ap[:, :], [(self.C("ident")[0:8, j:j + 1].broadcast_to([8, P]), stat)], inverse, self.free(bank))

        def norm(j, got):
            bank, spread_ready = got
            y_tile = self.big[:, y_tiles[j], :]
            gain = self.neg_lam[:, 1:2] if j < 4 else self.S("ml_norm_g", j - 4, 1)
            y = q.dve(op(nc.vector.scalar_tensor_tensor, y_tile, y_tile, gain, bank.ap[:, :], ALU.mult, ALU.mult), spread_ready, lam)
            bank.free_after(y)
            if j >= 4:
                y = q.pool(op(nc.gpsimd.tensor_tensor, y_tile, y_tile, self.big[:, OP0 + j - 4, :], ALU.mult), y, og)
            self.region_free = [self.put_h(j, slice(0, T), y_tile, y)]

        self.in_order(range(8), spread, None, norm)
        self.ring = range(8)

    def forget_sums(self, rows, ready):
        q, nc = self.q, self.nc
        a = q.act(op(nc.scalar.activation, rows(2), rows(1), ACT.Abs), ready)
        a = q.act(op(nc.scalar.activation, rows(2), rows(2), ACT.Exp, scale=-1.0), a)
        a = q.act(op(nc.scalar.activation, rows(2), rows(2), ACT.Ln, bias=1.0), a)
        lf = q.dve(op(nc.vector.scalar_tensor_tensor, rows(1), rows(1), 0.0, rows(2), ALU.min, ALU.subtract), a)
        one = self.C("ones")[0:8, 0:1].broadcast_to([8, T])
        s = q.dve(op(nc.vector.tensor_tensor_scan, rows(3), one, rows(1), 0.0, ALU.mult, ALU.add), lf)
        tot = self.neg_lam[0:8, 2:3]
        t = q.dve(op(nc.vector.tensor_tensor, tot, rows(3)[:, NC_TOK - 1:NC_TOK], rows(3)[:, T - 1:T], ALU.add), s)
        b = q.dve(op(nc.vector.tensor_tensor, rows(1), rows(1), rows(3), ALU.subtract), s)
        isb, isf = self.C("is_bwd", 8), self.C("is_fwd", 8)
        b1 = q.dve(op(nc.vector.tensor_scalar, rows(1)[:, CTX], rows(1)[:, CTX], rows(3)[:, NC_TOK - 1:NC_TOK], isb, ALU.add, ALU.mult), b)
        b2 = q.dve(op(nc.vector.tensor_scalar, rows(1)[:, LAT], rows(1)[:, LAT], tot, isb, ALU.add, ALU.mult), b, t)
        f = q.dve(op(nc.vector.scalar_tensor_tensor, rows(1), rows(3), isf, rows(1), ALU.mult, ALU.add), b1, b2)
        g = q.dve(op(nc.vector.tensor_tensor, rows(0), rows(0), rows(1), ALU.subtract), f)
        bank = self.next_bank()
        free = self.free(bank)
        for tt in range(TT):
            done = q.pe(op(nc.tensor.transpose, bank.ap[:, tt * 8:(tt + 1) * 8], rows(1)[:, tt * P:(tt + 1) * P], self.C("ident")[0:8, 0:8]), f, free)
        c = q.dve(op(nc.vector.tensor_copy, self.fcol[:, :], bank.ap[:, 0:TT * 8]), done)
        bank.free_after(c)
        return g, c

    def diff_lambda(self):
        q, nc = self.q, self.nc
        l = lambda j: self.S("lambda", j * HD, HD)
        col = self.next_cols()
        free = self.free(col)
        tmp = self.next_temp()
        tfree = self.free(tmp)
        for j in range(2):
            a = q.dve(op(nc.vector.tensor_tensor, tmp.ap[:, j * HD:(j + 1) * HD], l(2 * j), l(2 * j + 1), ALU.mult), tfree, self.ready)
            a = q.dve(op(nc.vector.tensor_reduce, col.ap[:, j:j + 1], tmp.ap[:, j * HD:(j + 1) * HD], AX.X, ALU.add), a, free)
        tmp.free_after(a)
        a = q.act(op(nc.scalar.activation, col.ap[:, 2:4], col.ap[:, 0:2], ACT.Exp), a)
        a = q.dve(op(nc.vector.tensor_tensor, col.ap[:, 4:5], col.ap[:, 3:4], col.ap[:, 2:3], ALU.subtract), a)
        b = q.dve(op(nc.vector.tensor_scalar, self.neg_lam[:, 0:1], col.ap[:, 4:5], -LAM_INIT, None, ALU.add), a)
        col.free_after(b)
        return q.dve(op(nc.vector.tensor_scalar, self.neg_lam[:, 1:2], self.S("diff_norm_g"), 1.0 - LAM_INIT, None, ALU.mult), b)

    def conv_silu(self, first, scratch, ready):
        q, nc = self.q, self.nc
        for j in range(4):
            x, y = self.big[:, first + j, :], self.big[:, scratch + j, :]
            w = lambda tap, j=j: self.S("conv_w", 4 * tap + j, 1)
            a = q.act(op(nc.scalar.activation, y, x, ACT.Identity, scale=w(1), bias=self.S("conv_b", j, 1)), ready, self.region_free)
            for s, c in STREAMS:
                lo, hi = c.start, c.stop
                a = q.dve(op(nc.vector.scalar_tensor_tensor, y[:, lo + 1:hi], x[:, lo:hi - 1], w(0), y[:, lo + 1:hi], ALU.mult, ALU.add), a)
                a = q.dve(op(nc.vector.scalar_tensor_tensor, y[:, lo:hi - 1], x[:, lo + 1:hi], w(2), y[:, lo:hi - 1], ALU.mult, ALU.add), a)
            a = q.act(op(nc.scalar.activation, x, y, ACT.Silu), a)
        return a

    def odd_mixer(self):
        q, nc = self.q, self.nc
        Q0, K0, R0, RANK, V0, W0 = 0, 4, 8, 16, 18, 26
        self.big = self.sb("odd_big", (P, 34, T))
        gla_kt = [Slot(self.sb(f"gla_kt{i}", (P, T))) for i in range(2)]
        shared = self.temp[4:6]
        gla_s = [Slot(t.ap[:, 0:256]) for t in shared]
        gla_at = [Slot(t.ap[:, 256:512]) for t in shared]
        gate_w = self.sb("gla_gate", (16, D))
        for i, t in enumerate(shared):
            gla_kt[i].free_after(self.region_free)
            gla_s[i].free_after(self.free(t))
            gla_at[i].free_after(self.free(t))
        gate_loaded = q.dma(op(nc.sync.dma_start, gate_w[:, :], self.w["gla_gate"]), self.side_sem, self.region_free)
        fm, _ = self.project_fm(18, 0)
        vals = self.token_major(V0)
        tm, done = self.project_tm(2, lambda tt, g: vals[:, tt, g * 512:(g + 1) * 512], self.region_free)
        self.h_free = [done]
        for j in range(8):
            swish = q.act(op(nc.scalar.activation, self.big[:, R0 + j, LAT], self.big[:, R0 + j, LAT], ACT.Silu), fm)

        n_chunks, L = NX_TOK // GLA_CHUNK, GLA_CHUNK
        self.ring = range(6)
        self.bank_at = 0
        scratch_free = [self.region_free, self.region_free]
        sums, factors, read = {}, {}, {}

        def decay_sums(hd, d):
            la, cum, incl, excl = (self.big[:, W0 + 4 * d + n, :] for n in range(4))
            bank = self.next_bank()
            z = self.matmuls(bank.ap[:, :], [(gate_w[:, d * 512 + hd * P:d * 512 + (hd + 1) * P],
                                              self.big[0:16, RANK + d, :])], fm, gate_loaded, self.free(bank))
            a = self._biased(la, bank, self.S("gla_b", 4 * d + hd, 1), z, scratch_free[d])
            bank.free_after(a)
            yield
            a = self._log_sigmoid(la, cum, a)
            yield
            s = self._scan(cum, la, a)
            e1 = self._rest(excl, cum, s, n_chunks, L)
            yield
            if d == 0:
                sums[hd, d] = cum, excl, cum, e1, e1, s
            else:
                sums[hd, d] = excl, incl, cum, *self._backward_sums(excl, incl, cum, la, e1), s

        def make_factors(hd, d):
            inc_ap, exc_ap, cum, inc_ready, exc_ready, s = sums[hd, d]
            col = self.next_cols()
            ready = self._gla_factors(hd, self.temp[d], self.temp[2 + d], col, inc_ap, exc_ap, cum, inc_ready, exc_ready, s, fm)
            scratch_free[d] = list(ready)
            factors[hd, d] = col, *ready

        def attend(hd, d, first):
            o_bank, o_free = self.bank[6 + hd % 2], self.free(self.bank[6 + hd % 2])
            qk, kd, k_t, smat, a_t = self.temp[d], self.temp[2 + d], gla_kt[d], gla_s[d], gla_at[d]
            col, qk_ready, kd_ready, dec = factors[hd, d]
            bank = self.next_bank()
            free = self.free(bank)
            for tt in range(TT):
                done = q.pe(op(nc.tensor.transpose, bank.ap[:, tt * P:(tt + 1) * P], kd.ap[:, tt * P:(tt + 1) * P], self.C("ident")),
                    kd_ready, free, signal=(tt == TT - 1))
            kd.free_after(done)
            kt_ready = q.act(op(nc.scalar.activation, k_t.ap[:, :], bank.ap[:, :], ACT.Identity), done, self.free(k_t))
            bank.free_after(kt_ready)
            yield
            v = lambda tt, lo, n, p0=0, pn=P: vals[p0:p0 + pn, tt, hd * 256 + lo:hd * 256 + lo + n]
            at_free = self.free(a_t)
            for tile in range(2):
                bank = self.next_bank()
                c = slice(tile * P, (tile + 1) * P)
                sc = self.matmuls(bank.ap[:, 0:P], [(qk.ap[:, 256 + tile * P:256 + (tile + 1) * P], qk.ap[:, c])],
                                  qk_ready, self.free(bank))
                at_ready = q.dve(op(nc.vector.tensor_tensor, a_t.ap[:, c], bank.ap[:, 0:P], self.C(f"gla_mask{d}"), ALU.mult), sc, at_free)
                bank.free_after(at_ready)
            yield
            bank = self.next_bank()
            st = self.matmuls(bank.ap[:, 0:256], [(k_t.ap[:, tt * P:(tt + 1) * P], v(tt, 0, 256)) for tt in range(2)],
                              kt_ready, tm, self.free(bank))
            s_ready = q.dve(op(nc.vector.tensor_copy, smat.ap[:, :], bank.ap[:, 0:256]), st, self.free(smat))
            bank.free_after(s_ready)
            yield
            for tile in range(2):
                for et in range(2):
                    done = self._acc(o_bank.ap[:, et * 256 + tile * P:et * 256 + (tile + 1) * P],
                                     v(2 + tile, et * P, P), a_t.ap[:, tile * P:(tile + 1) * P], first, at_ready, tm, o_free)
                    first = False
            a_t.free_after(done)
            order = range(n_chunks) if d == 0 else range(n_chunks - 1, -1, -1)
            for n, c in enumerate(order):
                last = n == n_chunks - 1
                if not last:
                    tt, p0 = 2 + c // 2, (c % 2) * L
                    bank = self.next_bank()
                    up = self.matmuls(bank.ap[:, 0:256], [(k_t.ap[p0:p0 + L, tt * P:(tt + 1) * P], v(tt, 0, 256, p0, L))],
                                      kt_ready, self.free(bank))
                for et in range(2):
                    done = self._acc(o_bank.ap[:, et * 256 + c * L:et * 256 + (c + 1) * L],
                                     smat.ap[:, et * P:(et + 1) * P], qk.ap[:, c * L:(c + 1) * L], False, s_ready)
                if not last:
                    s_ready = q.dve(op(nc.vector.scalar_tensor_tensor, smat.ap[:, :], smat.ap[:, :], col.ap[:, c:c + 1], bank.ap[:, 0:256],
                                       ALU.mult, ALU.add), up, done, dec)
                    bank.free_after(s_ready)
                    yield
            qk.free_after(done)
            smat.free_after(done)
            k_t.free_after(done)
            col.free_after(s_ready)
            read[hd, d] = done

        def output(hd):
            y_tile = [self.big[:, tile, LAT] for tile in (Q0 + hd, K0 + hd)]
            o_bank = self.bank[6 + hd % 2]
            for et in range(2):
                o = q.act(op(nc.scalar.activation, y_tile[et], o_bank.ap[:, et * 256:(et + 1) * 256], ACT.Identity),
                          read[hd, 0], read[hd, 1], factors[hd, 0][1:3], factors[hd, 1][1:3])
            o_bank.free_after(o)
            yield
            r = self.inverse_rms(y_tile, 256, RMS_EPS, LAT, [o, o])
            yield
            for et in range(2):
                y = q.dve(op(nc.vector.scalar_tensor_tensor, y_tile[et], y_tile[et], self.S("gla_norm_g", et, 1),
                    self.rstd[:, 0:NX_TOK], ALU.mult, ALU.mult), r)
                self.rstd_free = [y]
                y = q.dve(op(nc.vector.tensor_tensor, y_tile[et], y_tile[et], self.big[:, R0 + 2 * hd + et, LAT], ALU.mult),
                    y, swish)
                self.region_free = [self.put_h(2 * hd + et, LAT, y_tile[et], y)]

        def interleave(*lanes):
            lanes = list(lanes)
            while lanes:
                lanes = [lane for lane in lanes if next(lane, self) is not self]

        interleave(decay_sums(0, 0), decay_sums(0, 1))
        for hd in range(4):
            for d in range(2):
                make_factors(hd, d)
            interleave(attend(hd, 0, True), attend(hd, 1, False), *([output(hd - 1)] if hd else []),
                       *([decay_sums(hd + 1, 0), decay_sums(hd + 1, 1)] if hd < 3 else []))
        interleave(output(3))
        self.ring = range(8)
        for i, t in enumerate(shared):
            t.free_after(self.free(gla_s[i]), self.free(gla_at[i]))

    def _acc(self, out, a, b, start, *waits):
        return self.q.pe(op(self.nc.tensor.matmul, out, a, b, start=start, stop=True, skip_group_check=True), *waits)

    def _biased(self, out, bank, bias, *waits):
        return self.q.act(op(self.nc.scalar.activation, out, bank.ap[:, :], ACT.Identity, bias=bias), *waits)

    def _log_sigmoid(self, z, tmp, ready):
        q, nc = self.q, self.nc
        a = q.act(op(nc.scalar.activation, tmp, z, ACT.Abs), ready)
        a = q.act(op(nc.scalar.activation, tmp, tmp, ACT.Exp, scale=-1.0), a)
        a = q.act(op(nc.scalar.activation, tmp, tmp, ACT.Ln, bias=1.0), a)
        return q.dve(op(nc.vector.scalar_tensor_tensor, z, z, 0.0, tmp, ALU.min, ALU.subtract), a)

    def _scan(self, out, la, ready):
        return self.q.dve(op(self.nc.vector.tensor_tensor_scan, out, self.C("gla_carry"), la, 0.0, ALU.mult, ALU.add), ready)

    def _rest(self, out, cum, ready, n_chunks, L):
        q, nc = self.q, self.nc
        a = q.dve(op(nc.vector.tensor_scalar, out[:, CTX], cum[:, CTX], -1.0, cum[:, NC_TOK - 1:NC_TOK], ALU.mult, ALU.add), ready)
        by = lambda ap: ap[:, LAT].rearrange("p (c l) -> p c l", l=L)
        return q.dve(op(nc.vector.tensor_tensor, by(out), by(cum)[:, :, L - 1:L].broadcast_to([P, n_chunks, L]), by(cum), ALU.subtract), ready)

    def _backward_sums(self, rest, excl, cum, la, ready):
        q, nc = self.q, self.nc
        a = q.pool(op(nc.gpsimd.tensor_tensor, rest, rest, la, ALU.add), ready)
        b = q.dve(op(nc.vector.tensor_tensor, excl, cum, la, ALU.subtract), ready)
        return a, b

    def _gla_factors(self, hd, qk, kd, col, incl, excl, cum, inc_ready, exc_ready, scan_ready, proj):
        q, nc = self.q, self.nc
        inv_tau = 1.0 / 16.0
        qh, kh = self.big[:, hd, LAT], self.big[:, 4 + hd, :]
        free = self.free(qk)
        a = q.act(op(nc.scalar.activation, qk.ap[:, 0:256], incl[:, LAT], ACT.Exp, scale=inv_tau), inc_ready, free)
        b = q.act(op(nc.scalar.activation, qk.ap[:, 256:512], incl[:, LAT], ACT.Exp, scale=-inv_tau), inc_ready)
        c = q.act(op(nc.scalar.activation, kd.ap[:, :], excl, ACT.Exp, scale=inv_tau), exc_ready, self.free(kd))
        ends = cum[:, LAT].rearrange("p (c l) -> p c l", l=GLA_CHUNK)[:, :, GLA_CHUNK - 1]
        dec = q.act(op(nc.scalar.activation, col.ap[:, 0:4], ends, ACT.Exp, scale=inv_tau), scan_ready, self.free(col))
        a = q.dve(op(nc.vector.scalar_tensor_tensor, qk.ap[:, 0:256], qk.ap[:, 0:256], 128 ** -0.5, qh, ALU.mult, ALU.mult), a, proj)
        b = q.dve(op(nc.vector.tensor_tensor, qk.ap[:, 256:512], qk.ap[:, 256:512], kh[:, LAT], ALU.mult), b, proj)
        c = q.pool(op(nc.gpsimd.tensor_tensor, kd.ap[:, :], kd.ap[:, :], kh, ALU.mult), c, proj)
        return b, c, dec

    def final_norm(self):
        q, nc = self.q, self.nc
        r = self.inverse_rms([self.x[:, k, LAT] for k in range(DT)], D, RMS_EPS, LAT, self.x_ready)
        for k in range(DT):
            a = q.dve(op(nc.vector.scalar_tensor_tensor, self.x[:, k, LAT], self.x[:, k, LAT], self.S("final_g", k, 1), self.rstd[:, 0:NX_TOK], ALU.mult, ALU.mult), r)
        self.rstd_free = [a]
        c = q.dma(op(nc.sync.dma_start, self.x[:, :, CTX], self.w["ctx_2"]), self.side_sem, r)
        self.x_ready = [[a, c] for _ in range(DT)]

    def modulate(self, streams, branch):
        q, nc = self.q, self.nc
        shift = self.shift

        def scaled(k):
            tmp = self.next_temp()
            free = self.free(tmp)
            for s, c in streams:
                a = q.act(op(nc.scalar.activation, tmp.ap[:, c], self.x[:, k, c], ACT.Identity, scale=self.scales[:, k, s:s + 1],
                             bias=shift(k, s)), self.x_ready[k], self.scales_ready, free)
            self.scales_free = [a]
            cols = slice(branch[0][1].start, T)
            x = q.pool(op(nc.gpsimd.tensor_scalar, self.x[:, k, cols], self.x[:, k, cols], ALPHA, None, ALU.mult), a)
            self.x_free = [x]
            return tmp, a

        def put(k, got):
            tmp, a = got
            cols = slice(streams[0][1].start, T)
            tmp.free_after(self.put_h(k, cols, tmp.ap[:, cols], a))

        self.in_order(range(DT), scaled, None, put)

    def layer_norm(self, streams, layer, which):
        q, nc = self.q, self.nc
        cols = slice(streams[0][1].start, T)
        n = cols.stop - cols.start
        bank = self.next_bank()
        total = self.matmuls(bank.ap[:, 0:n], [(self.C("ones"), self.x[:, k, cols]) for k in range(DT)],
                             self.free(bank), ready=self.x_ready)
        centred = [q.dve(op(nc.vector.scalar_tensor_tensor, self.x[:, k, cols], bank.ap[:, 0:n], -1.0 / D, self.x[:, k, cols],
                            ALU.mult, ALU.add), total) for k in range(DT)]
        bank.free_after(centred[-1])
        r = self.inverse_rms([self.x[:, k, cols] for k in range(DT)], D, LN_EPS, cols, centred)
        g = lambda k: self.S("ln", (4 * layer + 2 * which) * DT + k, 1)
        b = lambda k: self.S("ln", (4 * layer + 2 * which + 1) * DT + k, 1)
        for k in range(DT):
            a = q.dve(op(nc.vector.scalar_tensor_tensor, self.x[:, k, cols], self.x[:, k, cols], g(k), self.rstd[:, 0:n], ALU.mult, ALU.mult), r)
            c = q.act(op(nc.scalar.activation, self.x[:, k, cols], self.x[:, k, cols], ACT.Identity, bias=b(k)), a)
            self.x_ready[k] = [c]
        self.rstd_free = [a]

    def softmax_scores(self, pairs, n, temp, col, ready):
        q, nc = self.q, self.nc
        bank = self.next_bank()
        s = self.matmuls(bank.ap[:, 0:n], pairs, ready, self.free(bank))
        m = q.dve(op(nc.vector.tensor_reduce, col.ap[:, 0:1], bank.ap[:, 0:n], AX.X, ALU.max, negate=True),
                  s, self.free(col))
        e = q.act(op(nc.scalar.activation, temp.ap[:, 0:n], bank.ap[:, 0:n], ACT.Exp, bias=col.ap[:, 0:1],
                                                 accum_out=col.ap[:, 1:2]), m, self.free(temp))
        bank.free_after(e)
        return e

    def normalise(self, n, temp, col, e):
        q, nc = self.q, self.nc
        r = q.dve(op(nc.vector.reciprocal, col.ap[:, 2:3], col.ap[:, 1:2]), e)
        w = q.pool(op(nc.gpsimd.tensor_scalar, temp.ap[:, 0:n], temp.ap[:, 0:n], col.ap[:, 2:3], None, ALU.mult), r)
        col.free_after(w)
        return w

    def mla_mixer(self):
        q, nc = self.q, self.nc
        KPE, QC, KC, QN, QPE, KN, V0, WT = 0, 1, 5, 9, 17, 21, 29, (1, 5)
        HQ, HK = 0, 4
        heads, scale = 8, (128 + 64) ** -0.5
        self.big = self.sb("mla_big", (P, 37, T))
        fm, done = self.project_fm(7, 0)
        kpe = self.rope(KPE, fm)
        self.h_free = [done]
        for first, at, n, dim, gain in ((QC, HQ, 4, 512, "q_norm"), (KC, HK, 2, 256, "kv_norm")):
            r = self.inverse_rms([self.big[:, first + k, :] for k in range(n)], dim, RMS_EPS, slice(0, T), [fm] * n)
            for k in range(n):
                tile = self.big[:, first + k, :]
                a = q.dve(op(nc.vector.scalar_tensor_tensor, tile, tile, self.S(gain, k, 1), self.rstd[:, :], ALU.mult, ALU.mult), r)
                normed = self.put_h(at + k, slice(0, T), tile, a)
            self.rstd_free = [a]
        for s in range(6):
            wh, wl, loaded, slot = self.next_slab()
            for t in range(2):
                bank = self.next_bank()
                cols = [slice(k * 256 + t * P, k * 256 + (t + 1) * P) for k in range(4)]
                done = self.products(bank.ap[:, :], [(wh[:, cols[k]], wl[:, cols[k]], *self.h_term(HQ + k)) for k in range(4)],
                                     loaded, self.free(bank), ready=self.h_ready[HQ:HQ + 4])
                q_n = q.act(op(nc.scalar.activation, self.big[:, QN + 2 * s + t, :], bank.ap[:, :], ACT.Identity, scale=scale),
                            done, self.region_free)
                bank.free_after(q_n)
            slot.free_after(done)
        q_parts = [q_n, *[self.rope(QPE + j, [q_n]) for j in range(4)]]
        for s in range(2):
            wh, wl, loaded, slot = self.next_slab()
            for t in range(4):
                bank = self.next_bank()
                cols = [slice(k * 512 + t * P, k * 512 + (t + 1) * P) for k in range(2)]
                done = self.products(bank.ap[:, :], [(wh[:, cols[k]], wl[:, cols[k]], *self.h_term(HK + k)) for k in range(2)],
                                     loaded, self.free(bank), ready=self.h_ready[HK:HK + 2])
                kn = q.dve(op(nc.vector.tensor_copy, self.big[:, KN + 4 * s + t, :], bank.ap[:, :]), done, self.region_free)
                bank.free_after(kn)
            slot.free_after(done)
        vals = self.token_major(V0)
        tm, done = self.project_tm(2, lambda tt, g: vals[:, tt, g * 512:(g + 1) * 512], self.region_free, first=HK, k_slabs=1)
        self.h_free = [done]
        wt_free = [[normed], [normed, *self.region_free]]
        w_t = [self.big[:, at:at + TT, :] for at in WT]
        copies = [[] for _ in range(heads)]
        n_keys = lambda qt: NC_TOK if qt < NC_TOK // P else T

        def scores(unit):
            hd, qt = unit
            n, c, base = n_keys(qt), slice(qt * P, (qt + 1) * P), HD * (hd % 2)
            temp, col = self.temp[(TT * hd + qt) % 6], self.next_cols()
            return temp, col, self.softmax_scores([
                (self.big[:, QN + hd, c], self.big[:, KN + hd, 0:n]),
                (self.big[base:base + HD, QPE + hd // 2, c], self.big[base:base + HD, KPE, 0:n])],
                n, temp, col, [kpe, kn, *q_parts])

        def normalise(unit, got):
            temp, col, e = got
            return temp, self.normalise(n_keys(unit[1]), temp, col, e)

        def turn(unit, got):
            (hd, qt), (w, ready) = unit, got
            done, copy = self.transpose_weights(w.ap, qt, n_keys(qt), w_t[hd % 2], ready, wt_free[hd % 2])
            w.free_after(done)
            copies[hd].append(copy)
            if qt == TT - 1:
                return [lambda: weigh(hd)]

        def weigh(hd):
            bank, done = self.weigh_values(lambda kt: vals[:, kt, hd * P:(hd + 1) * P], w_t[hd % 2], copies[hd] + tm)
            wt_free[hd % 2] = [done]
            o = q.act(op(nc.scalar.activation, self.big[:, QN + hd, :], bank.ap[:, :], ACT.Identity), done)
            bank.free_after(o)
            self.region_free = [self.put_h(hd, slice(0, T), self.big[:, QN + hd, :], o)]

        self.in_order([(hd, qt) for hd in range(heads) for qt in range(TT)], scores, normalise, None, None, turn)

    def na_mixer(self):
        q, nc = self.q, self.nc
        Q0, K0, V0, WT = 0, 8, 16, (24, 28)
        heads, scale = 16, HD ** -0.5
        self.big = self.sb("na_big", (P, 32, T))
        na_raw = [Slot(self.sb(f"na_raw{i}", (P, 6 * GRID_W))) for i in range(2)]
        na_bias = [Slot(self.sb(f"na_bias{i}", (P, 6 * GRID_W))) for i in range(2)]
        bv = self.sb("na_bv", (P, D))
        for slot in (*na_raw, *na_bias):
            slot.free_after(*self.region_free)
        bv_loaded = q.dma(op(nc.sync.dma_start, bv[:, :], self.w["na_bv"]), self.side_sem, self.region_free)
        fq, _ = self.project_fm(8, Q0, bias=self.S("na_b", 0, 8), lo=NC_TOK)
        fk, _ = self.project_fm(8, K0, bias=self.S("na_b", 8, 8))
        vals = self.token_major(V0)
        tm, done = self.project_tm(2, lambda tt, g: vals[:, tt, g * 512:(g + 1) * 512],
                                   [bv_loaded, *self.region_free], bias=bv)
        self.h_free = [done]
        wt_free = [self.region_free, self.region_free]
        rel = NX_TOK // GRID_W + 2
        rpb = self.w["na_rpb"]
        n_r, n_c = 15, 31
        w_t = [self.big[:, at:at + TT, :] for at in WT]
        copies = [[] for _ in range(heads)]
        biases = {}

        def prepare_bias(hd):
            raw, b_buf, n_b = na_raw[hd % 2], na_bias[hd % 2], rel * GRID_W
            free = self.free(raw)
            for r2 in range(2):
                at = bass.AP(rpb.tensor, hd * n_r * n_c + (4 + r2) * n_c + 15 - (GRID_W - 1), [[1, GRID_W], [n_c, rel], [1, GRID_W]])
                got = q.dma(op(nc.sync.dma_start, raw.ap[r2 * GRID_W:(r2 + 1) * GRID_W, 0:n_b].rearrange("p (m n) -> p m n", n=GRID_W), at),
                    self.bias_sem[hd % 2], free)
            mask = self.C("na_mask").rearrange("p (o n) -> p o n", o=1).broadcast_to([P, rel, GRID_W])
            bias = b_buf.ap[:, :]
            biased = q.pool(op(nc.gpsimd.tensor_copy, bias, raw.ap[:, n_b - 1::-1]), got, self.free(b_buf))
            raw.free_after(biased)
            biased = q.pool(op(nc.gpsimd.tensor_tensor, bias.rearrange("p (m n) -> p m n", n=GRID_W), bias.rearrange("p (m n) -> p m n", n=GRID_W), mask, ALU.add), biased)

            biases[hd] = b_buf, biased

        def scores(unit):
            hd, qt = unit
            base, tile, turn_no = HD * (hd % 2), hd // 2, 2 * hd + qt
            if qt == 2 and hd + 1 < heads:
                prepare_bias(hd + 1)
            b_buf, biased = biases[hd]
            bias = b_buf.ap[:, :]
            temp, col, bank = self.temp[turn_no % 6], self.next_cols(), self.next_bank()
            s = self.matmuls(bank.ap[:, :], [(
                self.big[base:base + HD, Q0 + tile, qt * P:(qt + 1) * P], self.big[base:base + HD, K0 + tile, :])],
                fq, fk, self.free(bank))
            a = q.act(op(nc.scalar.activation, temp.ap[:, CTX], bank.ap[:, CTX], ACT.Identity, scale=scale), s, self.free(temp))
            at = (2 - 2 * (qt - 2)) * GRID_W
            b = q.dve(op(nc.vector.scalar_tensor_tensor, temp.ap[:, LAT], bank.ap[:, LAT], scale, bias[:, at:at + NX_TOK], ALU.mult, ALU.add), s, biased, a)
            bank.free_after(b)
            m = q.dve(op(nc.vector.tensor_reduce, col.ap[:, 0:1], temp.ap[:, :], AX.X, ALU.max, negate=True),
                      a, b, self.free(col))
            e = q.act(op(nc.scalar.activation, temp.ap[:, :], temp.ap[:, :], ACT.Exp, bias=col.ap[:, 0:1],
                                                     accum_out=col.ap[:, 1:2]), m)
            if qt == TT - 1:
                b_buf.free_after(b)
            return temp, col, e

        def normalise(unit, got):
            temp, col, e = got
            return temp, self.normalise(T, temp, col, e)

        def turn(unit, got):
            (hd, qt), (w, ready) = unit, got
            done, copy = self.transpose_weights(w.ap, qt, T, w_t[hd % 2], ready, wt_free[hd % 2])
            w.free_after(done)
            copies[hd].append(copy)
            if qt == TT - 1:
                return [lambda: weigh(hd)]

        def weigh(hd):
            base, tile = HD * (hd % 2), hd // 2
            bank = self.next_bank()
            done = self.matmuls(bank.ap[base:base + HD, 0:NX_TOK], [
                (vals[:, kt, hd * HD:(hd + 1) * HD], w_t[hd % 2][:, kt, LAT]) for kt in range(TT)], copies[hd], tm, self.free(bank))
            wt_free[hd % 2] = [done]
            out = q.act(op(nc.scalar.activation, self.big[base:base + HD, Q0 + tile, LAT], bank.ap[base:base + HD, 0:NX_TOK],
                           ACT.Identity), done)
            bank.free_after(out)
            if base:
                self.region_free = [self.put_h(tile, LAT, self.big[:, Q0 + tile, LAT], out)]

        prepare_bias(0)
        self.in_order([(hd, qt) for hd in range(heads) for qt in range(2, TT)], scores, normalise, None, None, turn)


def run_stages(m):
    BOTH, LATENT = STREAMS, STREAMS[1:]
    g = lambda l, n: m.S("norm_g", (3 * l + n) * DT, DT)
    m.load_inputs()
    for s in range(SPLIT_SLOTS):
        m.prefetch(s)

    for l in range(2):
        first = 72 * l
        streams = (BOTH, LATENT)[l]
        with m.stage():
            m.open_modulation(l)
            if l == 0:
                m.modulation(2 * DT)
            m.scale_and_shift(first, 0, 1, g(l, 0))
            m.ada_norm(BOTH)
            if l == 0:
                m.modulation(DT)
            m.gate(first, 2, 0.5)
            m.feed_forward("swiglu", BOTH, 12)
        m.scale_and_shift(first, 3, 4, g(l, 1))
        m.ada_norm(BOTH)
        m.gate(first, 5)
        with m.stage():
            (m.even_mixer, m.odd_mixer)[l]()
            m.project_out(streams)
        with m.stage():
            if l == 0:
                m.open_modulation(0)
            m.scale_and_shift(first, 6, 7, g(l, 2))
            m.ada_norm(streams)
            m.gate(first, 8, 0.5)
            m.feed_forward("swiglu", streams, (12, 0)[l])
    m.final_norm()

    for l in range(2):
        first, streams = 144 + 48 * l, (BOTH, LATENT)[l]
        m.scale_and_shift(first, 0, 1, None)
        m.modulate(BOTH, streams)
        m.gate(first, 2)
        with m.stage():
            (m.mla_mixer, m.na_mixer)[l]()
            m.project_out(streams)
        m.layer_norm(streams, l, 0)
        with m.stage():
            if l == 0:
                m.open_modulation(1)
            m.scale_and_shift(first, 3, 4, None)
            m.modulate(streams, streams)
            m.gate(first, 5)
            m.feed_forward("relu2", streams, (7, 0)[l])
            if l == 0:
                m.modulation(1)
        m.layer_norm(streams, l, 1)
    m.store_output(m.x[:, :, LAT], m.x_ready)


def build_program(nc, w, out):
    with ExitStack() as stack:
        m = Model(nc, stack, w, out)
        run_stages(m)
        m.q.emit()


def kernel(**inputs):
    import concourse.bacc as bacc
    from concourse.bass_utils import run_bass_kernel_spmd

    arrays = lay_out(inputs)
    nc = bacc.Bacc("TRN2", target_bir_lowering=False, num_devices=1)
    w = {n: nc.dram_tensor(n, a.shape, F32, kind="ExternalInput").ap() for n, a in arrays.items()}
    out = nc.dram_tensor("out", (P, DT, NX_TOK), F32, kind="ExternalOutput").ap()
    build_program(nc, w, out)
    r = run_bass_kernel_spmd(nc, [arrays], core_ids=[0])
    got = r.results[0]["out"]
    return np.ascontiguousarray(got.transpose(2, 1, 0).reshape(1, NX_TOK, D))
```
